# Optimizing a Trainium2 kernel written in Bass

```python
import math
import jax
import jax.numpy as jnp
from jax import lax
import numpy as np
import jax, jax.numpy as jnp

D_MODEL = 1024
BATCH = 1
SEQ = 512
DEPTH = 2

N_A_LAYERS = DEPTH // 2
N_B_LAYERS = DEPTH - N_A_LAYERS

SSM_EXPAND = 2
D_INNER = SSM_EXPAND * D_MODEL
SSM_HEAD_DIM = 64
SSM_HEADS = D_INNER // SSM_HEAD_DIM
SSM_GROUPS = 4
SSM_HEADS_PER_GROUP = SSM_HEADS // SSM_GROUPS
SSM_STATE = 128
SSM_CONV = 4
SSM_CHUNK = 128
SSM_CONV_DIM = D_INNER + 2 * SSM_GROUPS * SSM_STATE
SSM_IN_DIM = D_INNER + SSM_CONV_DIM + SSM_HEADS

ATT_HEAD_DIM = 64
ATT_HEADS = D_MODEL // (2 * ATT_HEAD_DIM)
ATT_V_DIM = 2 * ATT_HEAD_DIM
ATT_BLOCK = 128
K_DIM = ATT_HEADS * 2 * ATT_HEAD_DIM
V_TOTAL = ATT_HEADS * ATT_V_DIM

NUM_BUCKETS = 32
MAX_DISTANCE = 128

FFN_DIM = 256 * ((8 * D_MODEL // 3 + 255) // 256)
FFN_CONV = 3

EPS = 1e-6


def rms_norm(x, g):
    xf = x.astype(jnp.float32)
    y = xf * lax.rsqrt(jnp.mean(xf * xf, axis=-1, keepdims=True) + EPS)
    return y.astype(x.dtype) * g

def causal_dwconv(u, w, b):
    k_w = w.shape[0]
    s = u.shape[1]
    up = jnp.pad(u, ((0, 0), (k_w - 1, 0), (0, 0)))
    y = up[:, 0:s] * w[0]
    for k in range(1, k_w):
        y = y + up[:, k:k + s] * w[k]
    return y + b

def segsum(a):
    t = a.shape[-1]
    cs = jnp.cumsum(a, axis=-1)
    d = cs[..., :, None] - cs[..., None, :]
    mask = jnp.tril(jnp.ones((t, t), dtype=bool))
    return jnp.where(mask, d, -jnp.inf)

def ssd_chunked(xdt, a, bm, cm):
    b, s, h, p = xdt.shape
    g, r, l = SSM_GROUPS, SSM_HEADS_PER_GROUP, SSM_CHUNK
    c = s // l
    xc = xdt.reshape(b, c, l, g, r, p)
    ac = a.reshape(b, c, l, g, r).transpose(0, 3, 4, 1, 2)
    bc = bm.reshape(b, c, l, g, SSM_STATE)
    cc = cm.reshape(b, c, l, g, SSM_STATE)
    a_cs = jnp.cumsum(ac, axis=-1)
    decay_in = jnp.exp(segsum(ac))
    cb = jnp.einsum('bclgn,bcsgn->bcgls', cc, bc)
    y_diag = jnp.einsum('bcgls,bgrcls,bcsgrp->bclgrp', cb, decay_in, xc)
    decay_states = jnp.exp(a_cs[..., -1:] - a_cs)
    states = jnp.einsum('bclgn,bgrcl,bclgrp->bcgrpn', bc, decay_states, xc)
    states0 = jnp.concatenate([jnp.zeros_like(states[:, :1]), states], axis=1)
    chunk_tot = jnp.pad(a_cs[..., -1], ((0, 0), (0, 0), (0, 0), (1, 0)))
    decay_chunk = jnp.exp(segsum(chunk_tot))
    new_states = jnp.einsum('bgrzc,bcgrpn->bzgrpn', decay_chunk, states0)
    states_in = new_states[:, :-1]
    y_off = jnp.einsum('bclgn,bcgrpn,bgrcl->bclgrp', cc, states_in, jnp.exp(a_cs))
    return (y_diag + y_off).reshape(b, s, h, p)

def mamba2_mixer(x, ln_g, in_w, conv_w, conv_b, dt_bias, a_log, d_skip, norm_g, out_w):
    b, s, _ = x.shape
    zxbcdt = rms_norm(x, ln_g) @ in_w
    z = zxbcdt[..., :D_INNER]
    xbc = zxbcdt[..., D_INNER:D_INNER + SSM_CONV_DIM]
    dt = zxbcdt[..., D_INNER + SSM_CONV_DIM:]
    xbc = jax.nn.silu(causal_dwconv(xbc, conv_w, conv_b))
    gn = SSM_GROUPS * SSM_STATE
    xs = xbc[..., :D_INNER].reshape(b, s, SSM_HEADS, SSM_HEAD_DIM)
    bm = xbc[..., D_INNER:D_INNER + gn].reshape(b, s, SSM_GROUPS, SSM_STATE)
    cm = xbc[..., D_INNER + gn:].reshape(b, s, SSM_GROUPS, SSM_STATE)
    dt = jax.nn.softplus(dt.astype(jnp.float32) + dt_bias.astype(jnp.float32))
    a = dt * (-jnp.exp(a_log.astype(jnp.float32)))
    xs32 = xs.astype(jnp.float32)
    y = ssd_chunked(xs32 * dt[..., None], a, bm.astype(jnp.float32), cm.astype(jnp.float32))
    y = y + xs32 * d_skip.astype(jnp.float32)[:, None]
    y = y.reshape(b, s, D_INNER) * jax.nn.silu(z.astype(jnp.float32))
    y = rms_norm(y.reshape(b, s, SSM_GROUPS, D_INNER // SSM_GROUPS),
                 norm_g.reshape(SSM_GROUPS, D_INNER // SSM_GROUPS)).reshape(b, s, D_INNER)
    return y @ out_w

def conv_ffn(x, ln_g, up_w, conv_w, conv_b, down_w):
    u = causal_dwconv(rms_norm(x, ln_g) @ up_w, conv_w, conv_b)
    gate, up = u[..., :FFN_DIM], u[..., FFN_DIM:]
    return (jax.nn.silu(gate) * up) @ down_w

def shared_kv(x, kv_ln_g, kv_w, k_norm_g):
    b, s, _ = x.shape
    kv = rms_norm(x, kv_ln_g) @ kv_w
    k = kv[..., :K_DIM].reshape(b, s, ATT_HEADS, 2, ATT_HEAD_DIM)
    v = kv[..., K_DIM:].reshape(b, s, ATT_HEADS, ATT_V_DIM)
    return rms_norm(k, k_norm_g), v

def t5_bucket(dist):
    n = jnp.maximum(dist, 0)
    max_exact = NUM_BUCKETS // 2
    nf = jnp.maximum(n, 1).astype(jnp.float32)
    large = max_exact + (jnp.log(nf / max_exact) / math.log(MAX_DISTANCE / max_exact)
                         * (NUM_BUCKETS - max_exact)).astype(jnp.int32)
    large = jnp.minimum(large, NUM_BUCKETS - 1)
    return jnp.where(n < max_exact, n, large)

def diff_attention(x, k, v, rel_bias, ln_g, q_w, q_norm_g, lam_vecs, subln_g, out_w, lam_init):
    b, s, _ = x.shape
    q = (rms_norm(x, ln_g) @ q_w).reshape(b, s, ATT_HEADS, 2, ATT_HEAD_DIM)
    q = rms_norm(q, q_norm_g)
    lv = lam_vecs.astype(jnp.float32)
    lam = jnp.exp(jnp.sum(lv[0] * lv[1])) - jnp.exp(jnp.sum(lv[2] * lv[3])) + lam_init
    scale = ATT_HEAD_DIM ** -0.5
    nb = s // ATT_BLOCK
    qb = q.reshape(b, nb, ATT_BLOCK, ATT_HEADS, 2, ATT_HEAD_DIM).transpose(1, 0, 2, 3, 4, 5)
    kpos = jnp.arange(s)

    def block(args):
        qblk, i = args
        qpos = i * ATT_BLOCK + jnp.arange(ATT_BLOCK)
        dist = qpos[:, None] - kpos[None, :]
        bias = rel_bias[t5_bucket(dist)].astype(jnp.float32).transpose(2, 0, 1)
        logits = jnp.einsum('bqhcd,bkhcd->bhcqk', qblk, k).astype(jnp.float32) * scale
        logits = logits + bias[None, :, None]
        logits = jnp.where(dist >= 0, logits, -jnp.inf)
        p = jax.nn.softmax(logits, axis=-1)
        attn = p[:, :, 0] - lam * p[:, :, 1]
        return jnp.einsum('bhqk,bkhd->bqhd', attn.astype(v.dtype), v)

    o = lax.map(block, (qb, jnp.arange(nb)))
    o = o.transpose(1, 0, 2, 3, 4).reshape(b, s, ATT_HEADS, ATT_V_DIM)
    o = rms_norm(o, subln_g) * (1.0 - lam_init)
    return o.reshape(b, s, V_TOTAL) @ out_w

def first_inputs(seed: int = 0) -> dict:
    key = jax.random.key(seed)
    ks = jax.random.split(key, 32)
    f32 = jnp.float32

    def nrm(k, shape, scale):
        return jax.random.normal(k, shape, f32) * scale

    def gain(k, shape):
        return 1.0 + 0.02 * jax.random.normal(k, shape, f32)

    na, nb = N_A_LAYERS, N_B_LAYERS
    dt = jnp.exp(jax.random.uniform(ks[6], (na, SSM_HEADS), f32)
                 * (math.log(0.1) - math.log(0.001)) + math.log(0.001))
    return {
        'x': nrm(ks[0], (BATCH, SEQ, D_MODEL), 1.0),
        'ssm_ln_g': gain(ks[1], (na, D_MODEL)),
        'ssm_in_w': nrm(ks[2], (na, D_MODEL, SSM_IN_DIM), D_MODEL ** -0.5),
        'ssm_conv_w': nrm(ks[3], (na, SSM_CONV, SSM_CONV_DIM), SSM_CONV ** -0.5),
        'ssm_conv_b': nrm(ks[4], (na, SSM_CONV_DIM), 0.02),
        'ssm_dt_bias': dt + jnp.log(-jnp.expm1(-dt)),
        'ssm_a_log': jnp.log(jax.random.uniform(ks[7], (na, SSM_HEADS), f32, 1.0, 16.0)),
        'ssm_d': gain(ks[8], (na, SSM_HEADS)),
        'ssm_norm_g': gain(ks[9], (na, D_INNER)),
        'ssm_out_w': nrm(ks[10], (na, D_INNER, D_MODEL), D_INNER ** -0.5),
        'kv_ln_g': gain(ks[11], (D_MODEL,)),
        'kv_w': nrm(ks[12], (D_MODEL, K_DIM + V_TOTAL), D_MODEL ** -0.5),
        'k_norm_g': gain(ks[13], (ATT_HEAD_DIM,)),
        'rel_bias': nrm(ks[14], (NUM_BUCKETS, ATT_HEADS), 0.5),
        'attn_ln_g': gain(ks[15], (nb, D_MODEL)),
        'q_w': nrm(ks[16], (nb, D_MODEL, K_DIM), D_MODEL ** -0.5),
        'q_norm_g': gain(ks[17], (nb, ATT_HEAD_DIM)),
        'lam_vecs': nrm(ks[18], (nb, 4, ATT_HEAD_DIM), 0.1),
        'subln_g': gain(ks[19], (nb, ATT_V_DIM)),
        'attn_out_w': nrm(ks[20], (nb, V_TOTAL, D_MODEL), V_TOTAL ** -0.5),
        'ffn_ln_g': gain(ks[21], (DEPTH, D_MODEL)),
        'ffn_up_w': nrm(ks[22], (DEPTH, D_MODEL, 2 * FFN_DIM), D_MODEL ** -0.5),
        'ffn_conv_w': nrm(ks[23], (DEPTH, FFN_CONV, 2 * FFN_DIM), FFN_CONV ** -0.5),
        'ffn_conv_b': nrm(ks[24], (DEPTH, 2 * FFN_DIM), 0.02),
        'ffn_down_w': nrm(ks[25], (DEPTH, FFN_DIM, D_MODEL), FFN_DIM ** -0.5),
    }

def first_block(x, ssm_ln_g, ssm_in_w, ssm_conv_w, ssm_conv_b, ssm_dt_bias, ssm_a_log, ssm_d,
              ssm_norm_g, ssm_out_w, kv_ln_g, kv_w, k_norm_g, rel_bias, attn_ln_g, q_w,
              q_norm_g, lam_vecs, subln_g, attn_out_w, ffn_ln_g, ffn_up_w, ffn_conv_w,
              ffn_conv_b, ffn_down_w):
    k_sh, v_sh = None, None
    for layer in range(DEPTH):
        if layer < N_A_LAYERS:
            i = layer
            mix = mamba2_mixer(x, ssm_ln_g[i], ssm_in_w[i], ssm_conv_w[i], ssm_conv_b[i],
                               ssm_dt_bias[i], ssm_a_log[i], ssm_d[i], ssm_norm_g[i],
                               ssm_out_w[i])
        else:
            j = layer - N_A_LAYERS
            if j == 0:
                k_sh, v_sh = shared_kv(x, kv_ln_g, kv_w, k_norm_g)
            lam_init = 0.8 - 0.6 * math.exp(-0.3 * layer)
            mix = diff_attention(x, k_sh, v_sh, rel_bias, attn_ln_g[j], q_w[j], q_norm_g[j],
                                 lam_vecs[j], subln_g[j], attn_out_w[j], lam_init)
        x = x + mix.astype(x.dtype)
        ff = conv_ffn(x, ffn_ln_g[layer], ffn_up_w[layer], ffn_conv_w[layer],
                      ffn_conv_b[layer], ffn_down_w[layer])
        x = x + ff.astype(x.dtype)
    return x


DEPTH_2 = 1

M_HEADS = 4
M_HEAD_DIM = 256
M_WIDTH = M_HEADS * M_HEAD_DIM
M_CHUNK = 64
CONV_WIDTH = 4
N_HEADS = 8
N_KV_GROUPS = 2
N_HPG = N_HEADS // N_KV_GROUPS
N_HEAD_DIM = 64
N_WIDTH = N_HEADS * N_HEAD_DIM
N_KV_WIDTH = N_KV_GROUPS * N_HEAD_DIM
CMP_BLOCK = 32
CMP_STRIDE = 16
CMP_HIDDEN = 128
SEL_BLOCK = 64
SEL_TOPK = 16
WINDOW = 512
Q_BLOCK = 128
ROPE_THETA = 500000.0
ROPE_DIM = N_HEAD_DIM // 4
NORM_EPS = 1e-6
NEG = -1e30
FORCE = 1e9

IN_SPLITS = (
    ("m_q", M_WIDTH), ("m_k", M_WIDTH), ("m_v", M_WIDTH), ("m_o", M_WIDTH), ("m_z", M_WIDTH),
    ("m_i", M_HEADS), ("m_f", M_HEADS),
    ("n_q", N_WIDTH), ("n_kc", N_KV_WIDTH), ("n_vc", N_KV_WIDTH),
    ("n_ks", N_KV_WIDTH), ("n_vs", N_KV_WIDTH), ("n_kw", N_KV_WIDTH), ("n_vw", N_KV_WIDTH),
    ("n_g", 3 * N_HEADS), ("n_z", N_WIDTH),
    ("g_a", D_MODEL), ("g_b", D_MODEL),
)
IN_WIDTH = sum(w for _, w in IN_SPLITS)


def _rmsnorm(x, g):
    xf = x.astype(jnp.float32)
    r = lax.rsqrt(jnp.mean(xf * xf, axis=-1, keepdims=True) + NORM_EPS)
    return (xf * r * g).astype(x.dtype)

def _split_in(u):
    names = [n for n, _ in IN_SPLITS]
    cuts = np.cumsum([w for _, w in IN_SPLITS])[:-1].tolist()
    return dict(zip(names, jnp.split(u, cuts, axis=-1)))

def _causal_dwconv(u, w, b):
    K = w.shape[0]
    T = u.shape[1]
    up = jnp.pad(u, ((0, 0), (K - 1, 0), (0, 0)))
    return b + sum(up[:, j:j + T] * w[j] for j in range(K))

def _partial_rope(u, pos):
    half = ROPE_DIM // 2
    inv = jnp.power(jnp.float32(ROPE_THETA), -jnp.arange(half, dtype=jnp.float32) * (2.0 / ROPE_DIM))
    ang = pos.astype(jnp.float32)[..., None] * inv
    cos = jnp.cos(ang)[:, :, None, :]
    sin = jnp.sin(ang)[:, :, None, :]
    u1 = u[..., :half]
    u2 = u[..., half:ROPE_DIM]
    r1 = u1 * cos - u2 * sin
    r2 = u2 * cos + u1 * sin
    return jnp.concatenate([r1.astype(u.dtype), r2.astype(u.dtype), u[..., ROPE_DIM:]], axis=-1)

def _mlstm(q, k, v, i_pre, f_pre):
    B, T, H, d = q.shape
    L = M_CHUNK
    NC = T // L
    k = k * (d ** -0.5)

    def to_chunks(a):
        a = a.reshape((B, NC, L, H) + a.shape[3:])
        return jnp.moveaxis(a, (1, 3), (0, 2))

    log_f = jax.nn.log_sigmoid(f_pre)
    log_i = i_pre
    causal = jnp.tril(jnp.ones((L, L), dtype=bool))

    def step(carry, xs):
        C, n, m = carry
        qc, kc, vc, li, lf = xs
        a = jnp.cumsum(lf, axis=-1)
        A = a[..., -1]
        logD = a[..., :, None] - a[..., None, :] + li[..., None, :]
        logD = jnp.where(causal, logD, -jnp.inf)
        inter = a + m[..., None]
        m_t = jnp.maximum(inter, jnp.max(logD, axis=-1))
        w_inter = jnp.exp(inter - m_t)
        s = jnp.einsum('bhld,bhsd->bhls', qc, kc) * jnp.exp(logD - m_t[..., None])
        num = w_inter[..., None] * jnp.einsum('bhld,bhde->bhle', qc, C) + jnp.einsum('bhls,bhse->bhle', s, vc)
        den = w_inter * jnp.einsum('bhld,bhd->bhl', qc, n) + jnp.sum(s, axis=-1)
        h = num / jnp.maximum(jnp.abs(den), jnp.exp(-m_t))[..., None]
        logw = A[..., None] - a + li
        m_new = jnp.maximum(A + m, jnp.max(logw, axis=-1))
        wk = jnp.exp(logw - m_new[..., None])
        decay = jnp.exp(A + m - m_new)
        C_new = decay[..., None, None] * C + jnp.einsum('bhs,bhsd,bhse->bhde', wk, kc, vc)
        n_new = decay[..., None] * n + jnp.einsum('bhs,bhsd->bhd', wk, kc)
        return (C_new, n_new, m_new), h

    init = (jnp.zeros((B, H, d, d), jnp.float32), jnp.zeros((B, H, d), jnp.float32),
            jnp.zeros((B, H), jnp.float32))
    xs = (to_chunks(q), to_chunks(k), to_chunks(v), to_chunks(log_i), to_chunks(log_f))
    _, hs = lax.scan(step, init, xs)
    hs = jnp.moveaxis(hs, (0, 2), (1, 3))
    return hs.reshape(B, T, H, d)

def _head_layernorm(h, g):
    B, T = h.shape[0], h.shape[1]
    mu = jnp.mean(h, axis=-1, keepdims=True)
    var = jnp.mean(jnp.square(h - mu), axis=-1, keepdims=True)
    hn = (h - mu) * lax.rsqrt(var + NORM_EPS)
    return hn.reshape(B, T, -1) * g

def _compress(kv, pos_emb, w1, w2):
    B, T, G, dk = kv.shape
    n_cmp = (T - CMP_BLOCK) // CMP_STRIDE + 1
    idx = jnp.arange(n_cmp)[:, None] * CMP_STRIDE + jnp.arange(CMP_BLOCK)[None, :]
    blocks = kv[:, idx] + pos_emb[None, None, :, None, :]
    blocks = jnp.moveaxis(blocks, 3, 1).reshape(B, G, n_cmp, CMP_BLOCK * dk)
    return jax.nn.gelu(blocks @ w1) @ w2

def _nsa(q_raw, q_rope, kc, vc, ks, vs, kw, vw, gates):
    B, G, h, T, dk = q_raw.shape
    n_cmp = kc.shape[2]
    n_sel = T // SEL_BLOCK
    n_top = min(SEL_TOPK, n_sel)
    scale = dk ** -0.5
    cmp_end = jnp.arange(n_cmp) * CMP_STRIDE + (CMP_BLOCK - 1)
    ci = jnp.arange(n_cmp)[:, None] * CMP_STRIDE
    sj = jnp.arange(n_sel)[None, :] * SEL_BLOCK
    overlap = ((ci < sj + SEL_BLOCK) & (ci + CMP_BLOCK > sj)).astype(jnp.float32)
    ks_blocks = ks.reshape(B, G, n_sel, SEL_BLOCK, dk)
    vs_blocks = vs.reshape(B, G, n_sel, SEL_BLOCK, dk)
    kw_pad = jnp.pad(kw, ((0, 0), (0, 0), (WINDOW, 0), (0, 0)))
    vw_pad = jnp.pad(vw, ((0, 0), (0, 0), (WINDOW, 0), (0, 0)))
    bi = jnp.arange(B)[:, None, None, None]
    gi = jnp.arange(G)[None, :, None, None]
    blk = jnp.arange(n_sel)

    def block(i):
        t0 = i * Q_BLOCK
        tq = t0 + jnp.arange(Q_BLOCK)
        qr = lax.dynamic_slice_in_dim(q_raw, t0, Q_BLOCK, axis=3)
        qp = lax.dynamic_slice_in_dim(q_rope, t0, Q_BLOCK, axis=3)
        g = lax.dynamic_slice_in_dim(gates, t0, Q_BLOCK, axis=3)
        s_c = jnp.einsum('bghqd,bgnd->bghqn', qr, kc).astype(jnp.float32) * scale
        m_c = cmp_end[None, :] <= tq[:, None]
        p_c = jax.nn.softmax(jnp.where(m_c, s_c, NEG), axis=-1) * m_c
        o_c = jnp.einsum('bghqn,bgnd->bghqd', p_c.astype(vc.dtype), vc)
        imp = jnp.einsum('bghqn,ns->bgqs', p_c, overlap)
        cur = tq // SEL_BLOCK
        forced = (blk[None, :] == 0) | (blk[None, :] == cur[:, None]) | (blk[None, :] == cur[:, None] - 1)
        valid = blk[None, :] * SEL_BLOCK <= tq[:, None]
        score = jnp.where(forced, FORCE, jnp.where(valid, imp, -1.0))
        _, idx = lax.top_k(score, n_top)
        kg = ks_blocks[bi, gi, idx]
        vg = vs_blocks[bi, gi, idx]
        kpos = idx[..., None] * SEL_BLOCK + jnp.arange(SEL_BLOCK)
        m_s = kpos <= tq[:, None, None]
        s_s = jnp.einsum('bghqd,bgqnsd->bghqns', qp, kg).astype(jnp.float32) * scale
        s_s = jnp.where(m_s[:, :, None], s_s, NEG).reshape(B, G, h, Q_BLOCK, n_top * SEL_BLOCK)
        p_s = jax.nn.softmax(s_s, axis=-1).reshape(B, G, h, Q_BLOCK, n_top, SEL_BLOCK)
        o_s = jnp.einsum('bghqns,bgqnsd->bghqd', p_s.astype(vg.dtype), vg)
        kwb = lax.dynamic_slice_in_dim(kw_pad, t0, Q_BLOCK + WINDOW, axis=2)
        vwb = lax.dynamic_slice_in_dim(vw_pad, t0, Q_BLOCK + WINDOW, axis=2)
        wpos = t0 - WINDOW + jnp.arange(Q_BLOCK + WINDOW)
        diff = tq[:, None] - wpos[None, :]
        m_w = (diff >= 0) & (diff < WINDOW) & (wpos[None, :] >= 0)
        s_w = jnp.einsum('bghqd,bgkd->bghqk', qp, kwb).astype(jnp.float32) * scale
        p_w = jax.nn.softmax(jnp.where(m_w, s_w, NEG), axis=-1)
        o_w = jnp.einsum('bghqk,bgkd->bghqd', p_w.astype(vwb.dtype), vwb)
        return g[..., 0:1] * o_c + g[..., 1:2] * o_s + g[..., 2:3] * o_w

    out = lax.map(block, jnp.arange(T // Q_BLOCK))
    out = jnp.moveaxis(out, 0, 3).reshape(B, G, h, T, dk)
    return out.transpose(0, 3, 1, 2, 4).reshape(B, T, G * h * dk)

def second_inputs(seed: int = 0) -> dict:
    key = jax.random.key(seed)
    ks = jax.random.split(key, 24)
    f32 = jnp.float32

    def nrm(k, shape, scale):
        return jax.random.normal(k, shape, f32) * scale

    x = nrm(ks[0], (BATCH, SEQ, D_MODEL), 1.0)
    positions = jnp.tile(jnp.arange(SEQ, dtype=jnp.int32)[None, :], (BATCH, 1))
    norm_g = 1.0 + nrm(ks[1], (DEPTH_2, D_MODEL), 0.05)
    w_in = nrm(ks[2], (DEPTH_2, D_MODEL, IN_WIDTH), D_MODEL ** -0.5)
    conv_q_w = nrm(ks[3], (DEPTH_2, CONV_WIDTH, M_WIDTH), CONV_WIDTH ** -0.5)
    conv_q_b = nrm(ks[4], (DEPTH_2, M_WIDTH), 0.02)
    conv_k_w = nrm(ks[5], (DEPTH_2, CONV_WIDTH, M_WIDTH), CONV_WIDTH ** -0.5)
    conv_k_b = nrm(ks[6], (DEPTH_2, M_WIDTH), 0.02)
    b_igate = nrm(ks[7], (DEPTH_2, M_HEADS), 0.1)
    b_fgate = jnp.linspace(3.0, 6.0, M_HEADS, dtype=f32)[None, :] + nrm(ks[8], (DEPTH_2, M_HEADS), 0.1)
    mh_norm_g = 1.0 + nrm(ks[9], (DEPTH_2, M_WIDTH), 0.05)
    cmp_pos_k = nrm(ks[10], (DEPTH_2, CMP_BLOCK, N_HEAD_DIM), 0.1)
    cmp_w1_k = nrm(ks[11], (DEPTH_2, CMP_BLOCK * N_HEAD_DIM, CMP_HIDDEN), (CMP_BLOCK * N_HEAD_DIM) ** -0.5)
    cmp_w2_k = nrm(ks[12], (DEPTH_2, CMP_HIDDEN, N_HEAD_DIM), CMP_HIDDEN ** -0.5)
    cmp_pos_v = nrm(ks[13], (DEPTH_2, CMP_BLOCK, N_HEAD_DIM), 0.1)
    cmp_w1_v = nrm(ks[14], (DEPTH_2, CMP_BLOCK * N_HEAD_DIM, CMP_HIDDEN), (CMP_BLOCK * N_HEAD_DIM) ** -0.5)
    cmp_w2_v = nrm(ks[15], (DEPTH_2, CMP_HIDDEN, N_HEAD_DIM), CMP_HIDDEN ** -0.5)
    b_nsa_gate = nrm(ks[16], (DEPTH_2, 3 * N_HEADS), 0.1)
    w_branch_a = nrm(ks[17], (DEPTH_2, M_WIDTH, D_MODEL), M_WIDTH ** -0.5)
    w_branch_b = nrm(ks[18], (DEPTH_2, N_WIDTH, D_MODEL), N_WIDTH ** -0.5)
    w_out = nrm(ks[19], (DEPTH_2, D_MODEL, D_MODEL), D_MODEL ** -0.5)
    final_norm_g = 1.0 + nrm(ks[20], (D_MODEL,), 0.05)
    return {"x": x, "positions": positions, "norm_g": norm_g, "w_in": w_in,
            "conv_q_w": conv_q_w, "conv_q_b": conv_q_b, "conv_k_w": conv_k_w, "conv_k_b": conv_k_b,
            "b_igate": b_igate, "b_fgate": b_fgate, "mh_norm_g": mh_norm_g,
            "cmp_pos_k": cmp_pos_k, "cmp_w1_k": cmp_w1_k, "cmp_w2_k": cmp_w2_k,
            "cmp_pos_v": cmp_pos_v, "cmp_w1_v": cmp_w1_v, "cmp_w2_v": cmp_w2_v,
            "b_nsa_gate": b_nsa_gate, "w_branch_a": w_branch_a, "w_branch_b": w_branch_b,
            "w_out": w_out, "final_norm_g": final_norm_g}

def second_block(x, positions, norm_g, w_in, conv_q_w, conv_q_b, conv_k_w, conv_k_b, b_igate, b_fgate,
              mh_norm_g, cmp_pos_k, cmp_w1_k, cmp_w2_k, cmp_pos_v, cmp_w1_v, cmp_w2_v, b_nsa_gate,
              w_branch_a, w_branch_b, w_out, final_norm_g):
    B, T, _ = x.shape
    f32 = jnp.float32
    for l in range(DEPTH_2):
        hN = _rmsnorm(x, norm_g[l])
        p = _split_in(hN @ w_in[l])
        mq = jax.nn.silu(_causal_dwconv(p["m_q"], conv_q_w[l], conv_q_b[l]))
        mk = jax.nn.silu(_causal_dwconv(p["m_k"], conv_k_w[l], conv_k_b[l]))
        mh = _mlstm(mq.reshape(B, T, M_HEADS, M_HEAD_DIM).astype(f32),
                    mk.reshape(B, T, M_HEADS, M_HEAD_DIM).astype(f32),
                    p["m_v"].reshape(B, T, M_HEADS, M_HEAD_DIM).astype(f32),
                    (p["m_i"] + b_igate[l]).astype(f32),
                    (p["m_f"] + b_fgate[l]).astype(f32))
        mh = _head_layernorm(mh, mh_norm_g[l]).astype(x.dtype)
        ya = jax.nn.sigmoid(p["m_o"]) * mh * jax.nn.silu(p["m_z"])
        nq = p["n_q"].reshape(B, T, N_HEADS, N_HEAD_DIM)
        q_raw = nq.reshape(B, T, N_KV_GROUPS, N_HPG, N_HEAD_DIM).transpose(0, 2, 3, 1, 4)
        q_rope = _partial_rope(nq, positions).reshape(B, T, N_KV_GROUPS, N_HPG, N_HEAD_DIM).transpose(0, 2, 3, 1, 4)

        def kvh(a):
            return a.reshape(B, T, N_KV_GROUPS, N_HEAD_DIM)

        kc = _compress(kvh(p["n_kc"]), cmp_pos_k[l], cmp_w1_k[l], cmp_w2_k[l])
        vc = _compress(kvh(p["n_vc"]), cmp_pos_v[l], cmp_w1_v[l], cmp_w2_v[l])
        ks = _partial_rope(kvh(p["n_ks"]), positions).transpose(0, 2, 1, 3)
        vs = kvh(p["n_vs"]).transpose(0, 2, 1, 3)
        kw = _partial_rope(kvh(p["n_kw"]), positions).transpose(0, 2, 1, 3)
        vw = kvh(p["n_vw"]).transpose(0, 2, 1, 3)
        gates = jax.nn.sigmoid(p["n_g"] + b_nsa_gate[l]).reshape(B, T, N_KV_GROUPS, N_HPG, 3).transpose(0, 2, 3, 1, 4)
        yn = _nsa(q_raw, q_rope, kc, vc, ks, vs, kw, vw, gates)
        yb = yn * jax.nn.silu(p["n_z"])
        merged = (jax.nn.sigmoid(p["g_a"]) * (ya @ w_branch_a[l])
                  + jax.nn.sigmoid(p["g_b"]) * (yb @ w_branch_b[l]))
        x = x + merged @ w_out[l]
    return _rmsnorm(x, final_norm_g)


def setup_inputs(seed=0):
    out = dict(first_inputs(seed))
    for name, value in second_inputs(seed + 1).items():
        if name != "x":
            out[name + "_2"] = value
    return out


def reference(
    x, ssm_ln_g, ssm_in_w, ssm_conv_w, ssm_conv_b, ssm_dt_bias, ssm_a_log, ssm_d, ssm_norm_g,
    ssm_out_w, kv_ln_g, kv_w, k_norm_g, rel_bias, attn_ln_g, q_w, q_norm_g, lam_vecs, subln_g,
    attn_out_w, ffn_ln_g, ffn_up_w, ffn_conv_w, ffn_conv_b, ffn_down_w, positions_2, norm_g_2,
    w_in_2, conv_q_w_2, conv_q_b_2, conv_k_w_2, conv_k_b_2, b_igate_2, b_fgate_2, mh_norm_g_2,
    cmp_pos_k_2, cmp_w1_k_2, cmp_w2_k_2, cmp_pos_v_2, cmp_w1_v_2, cmp_w2_v_2, b_nsa_gate_2,
    w_branch_a_2, w_branch_b_2, w_out_2, final_norm_g_2,
):
    x = first_block(
        x, ssm_ln_g, ssm_in_w, ssm_conv_w, ssm_conv_b, ssm_dt_bias, ssm_a_log, ssm_d,
        ssm_norm_g, ssm_out_w, kv_ln_g, kv_w, k_norm_g, rel_bias, attn_ln_g, q_w, q_norm_g,
        lam_vecs, subln_g, attn_out_w, ffn_ln_g, ffn_up_w, ffn_conv_w, ffn_conv_b, ffn_down_w,
    )
    return second_block(
        x, positions_2, norm_g_2, w_in_2, conv_q_w_2, conv_q_b_2, conv_k_w_2, conv_k_b_2,
        b_igate_2, b_fgate_2, mh_norm_g_2, cmp_pos_k_2, cmp_w1_k_2, cmp_w2_k_2, cmp_pos_v_2,
        cmp_w1_v_2, cmp_w2_v_2, b_nsa_gate_2, w_branch_a_2, w_branch_b_2, w_out_2,
        final_norm_g_2,
    )


_drawn_inputs = setup_inputs


def setup_inputs(seed=0):
    import zlib

    import numpy as np

    out = dict(_drawn_inputs(seed))
    spreads = {}
    factors = {'ssm_d': 4.701,
     'ssm_norm_g': 3.002,
     'kv_ln_g': 4.612,
     'k_norm_g': 6.817,
     'attn_ln_g': 6.865,
     'q_norm_g': 6.907,
     'subln_g': 6.675,
     'ffn_ln_g': 3.232,
     'ffn_conv_b': 3.224,
     'norm_g_2': 6.024,
     'conv_q_b_2': 200.0,
     'conv_k_b_2': 200.0,
     'b_igate_2': 200.0,
     'mh_norm_g_2': 8.0,
     'cmp_pos_k_2': 8.0,
     'cmp_w1_k_2': 5.703,
     'cmp_w2_k_2': 5.787,
     'cmp_pos_v_2': 8.0,
     'b_nsa_gate_2': 8.0}
    for name, (base, spread) in spreads.items():
        noise = np.random.default_rng([zlib.crc32(name.encode()), seed]).standard_normal(out[name].shape)
        drawn = base * np.exp(spread * noise) if base else spread * noise
        out[name] = jnp.asarray(drawn.astype(out[name].dtype))
    for name, factor in factors.items():
        out[name] = (out[name] * factor).astype(out[name].dtype)
    return out
```

```python
import concourse.bass as bass
from concourse import mybir
from contextlib import ExitStack
import numpy as np
import math

F32 = mybir.dt.float32
ACT = mybir.ActivationFunctionType
ALU = mybir.AluOpType
AX = mybir.AxisListType

T = 512
P = 128
NT = T // P
DM = 1024
KD = DM // P
SSM_G, SSM_HG = 4, 8
SSM_H = SSM_G * SSM_HG
GT = 4
GROUP_TILES = 2 * GT + 2
FF_TILES = 22
AH = 8
MH = 4
NP_ = 4
NCMP = (T - 32) // 16 + 1
CMPL = 32
EPS = 1e-6
NEG = -1e30
LAM_INIT = 0.8 - 0.6 * math.exp(-0.3)
SLOTS = 4
CELLS = 11


def layout(spec):
    at, out = 0, {}
    for name, n in spec:
        out[name] = (at, n)
        at += n
    out[None] = at
    return out


CONST = layout([("ident", P), ("half_ones", P), ("causal_st", P), ("future_neg", P), ("rope_turn", P),
                ("rope_freq", 1), ("cmp_seen", NT * NCMP), ("cmp_neg", NT * NCMP)])
PARAM = layout([("ssm_ln", KD), ("kv_ln", KD), ("attn_ln", KD), ("ffn_ln0", KD), ("ffn_ln1", KD),
                ("norm2", KD), ("final", KD), ("ssm_d", 16), ("ssm_norm", 16), ("k_norm", 1),
                ("q_norm", 1), ("subln", 1), ("mh_norm", 8), ("ssm_conv", 24 * 5),
                ("ffn_conv0", 44 * 4), ("ffn_conv1", 44 * 4), ("qk_conv", 16 * 5),
                ("gate_bias", 1), ("dt_bias", 1), ("a_log", 1), ("cmp_pos", 2 * CMPL), ("lam", 256)])


class Count:

    def __init__(self, eng, sem):
        self.eng, self.sem, self.n, self.k = eng, sem, 0, 0

    def step(self, ins):
        ins.then_inc(self.sem, 1)
        self.n = self.n + 1
        self.k += 1
        self.eng.wait_ge(self.sem, self.n)

    def enter(self, i, per):
        self.base, self.per, self.k = self.n, per, 0
        self.n = i * per + self.base

    def leave(self, turns):
        assert self.k == self.per, (self.k, self.per)
        self.n = self.base + turns * self.per


def three_parts(nc, A, out):
    ctx = ExitStack()
    with ctx:
        def sb(name, shape, dt=F32):
            return ctx.enter_context(nc.sbuf_tensor(name, shape, dt))

        def sem(name):
            return ctx.enter_context(nc.semaphore(name))

        X = sb("residual", [P, KD, T])
        H = sb("scaled_in", [P, KD, T])
        RING = sb("weight_ring", [P, SLOTS, CELLS * P])
        SQ = sb("squares", [P, KD, T])
        RS = sb("inv_rms", [P, T])
        STD = sb("rms", [P, T])
        CST = sb("constants", [P, CONST[None]])
        PAR = sb("params", [P, PARAM[None]])
        ONES = sb("ones", [P, P])
        SMALL = sb("small_weights", [P, KD, 32 + 88])
        EPSC = sb("eps_column", [P, 1])
        U = sb("padded_rows", [P, 2, T + 4])
        CV = sb("conv_rows", [P, 2, T])
        CW2B = sb("compress_w2", [P, 2 * 64])
        HGB = sb("compress_hidden", [P, P])
        VCCB = sb("compressed_values", [P, P])
        EMB = sb("floor", [P, T])
        RDB = sb("reciprocals", [P, T])
        ARENA = sb("arena", [P, 27600])
        BANK = [ctx.enter_context(nc.psum_tensor(f"bank{i}", [P, T], F32)) for i in range(8)]

        def const(name, parts=P):
            a, n = CONST[name]
            return CST[0:parts, a:a + n]

        def par(name, i=0, n=1, parts=P):
            a, _ = PARAM[name]
            return PAR[0:parts, a + i:a + i + n]

        class Carve:

            def __init__(self):
                self.at = 0

            def __call__(self, *shape):
                n = int(np.prod(shape))
                v = ARENA[:, self.at:self.at + n]
                self.at += n
                assert self.at <= 27600, self.at
                if len(shape) == 2:
                    v = v.rearrange("p (a b) -> p a b", b=shape[1])
                if len(shape) == 3:
                    v = v.rearrange("p (a b c) -> p a b c", b=shape[1], c=shape[2])
                return v

        IDENT = const("ident")

        loaded = sem("loaded")
        w_ready = [sem(f"weights_in_slot{i}") for i in range(SLOTS)]
        gemm_done = sem("gemm_tile_done")
        half_done = sem("first_block_used")
        gemm_free = sem("gemm_bank_read")
        ones_set = sem("ones_set")
        h_ready = sem("scaled_in_ready")
        ff_ready = sem("gated_ready")
        sq_ready = sem("squares_ready")
        ssq_done = sem("square_sum_done")
        std_ready = sem("rms_ready")
        rs_ready = sem("inv_rms_ready")
        row_used = sem("tile_rows_used")
        conv_ready = sem("tile_rows_ready")
        dve_step = sem("dve_step")
        act_step = sem("act_step")
        dt_done = sem("dt_product_done")
        dt_row = sem("dt_rows_step")
        dt_act = sem("dt_act_step")
        dtT_done = sem("dt_turned")
        p1_done = sem("ssd_inputs_done")
        e_ready = sem("ssd_exps_of_sums")
        d_ready = sem("ssd_exponents_ready")
        d_exp = sem("ssd_decay_ready")
        mce_ready = sem("ssd_operands_ready")
        xf_ready = sem("ssd_state_input_ready")
        y_done = sem("ssd_y_done")
        st_done = sem("ssd_state_done")
        y_read = sem("ssd_y_read")
        s_ready = sem("ssd_state_ready")
        yb_ready = sem("ssd_y_ready")
        gsq_ready = sem("group_squares_ready")
        gss_done = sem("group_square_sum_done")
        gstd_ready = sem("group_rms_ready")
        yn_ready = sem("normed_y_ready")

        block = ctx.enter_context(nc.Block())

        STREAM = [("in_w", 40, 8, 1), ("out_w", 16, 8, 2), ("up0", 44, 8, 1), ("down0", 16, 11, 2),
                  ("kvq", 24, 8, 1), ("attn_out", 8, 8, 1), ("up1", 44, 8, 1), ("down1", 16, 11, 2),
                  ("w_in2", 70, 8, 1), ("ab", 16, 8, 1), ("w_out2", 8, 8, 1)]
        BASE, TILE0, HALF0 = {}, {}, {}
        b = t = h = 0
        for name, n, cells, per in STREAM:
            BASE[name], TILE0[name], HALF0[name] = b, t, h
            b, t, h = b + n, t + n // per, h + (n // 2 if per == 2 else 0)

        def gemm_tile(pe, name, i, j, rhs, cells=8, per=1):
            turn = SLOTS // per
            n = TILE0[name] + j + i * turn
            bank = (TILE0[name] + j) % 2
            if TILE0[name] + j >= 2:
                pe.wait_ge(gemm_free, n - 1)
            for part in range(per):
                b = BASE[name] + per * j + part
                slot = b % SLOTS
                pe.wait_ge(w_ready[slot], i * 16 + 16 * (b // SLOTS + 1))
                for c in range(cells):
                    k = part * cells + c
                    mm = nc.tensor.matmul(BANK[bank][:, :], RING[:, slot, c * P:(c + 1) * P], rhs(k),
                                          start=(k == 0), stop=(k == per * cells - 1))
                if part < per - 1:
                    mm.then_inc(half_done, 1)
            mm.then_inc(gemm_done, 1)

        def norm_sums(pe, turn):
            for k in range(KD):
                pe.wait_ge(sq_ready, KD * turn + k + 1)
                mm = nc.tensor.matmul(BANK[7][:, :], ONES[:, :], SQ[:, k, :],
                                      start=(k == 0), stop=(k == KD - 1))
            mm.then_inc(ssq_done, 1)

        def norm_scale_act(act, turn):
            act.wait_ge(ssq_done, turn + 1)
            nc.scalar.activation(STD[:, :], BANK[7][:, :], ACT.Sqrt, bias=EPSC[:, 0:1],
                                 scale=1.0 / DM).then_inc(std_ready, 1)

        def norm_scale_dve(dve, turn, rs):
            dve.wait_ge(std_ready, turn + 1)
            rs.step(nc.vector.reciprocal(RS[:, :], STD[:, :]))

        def conv(dve, step, done, b, taps_and_bias, taps, out=None):
            u, y = U[:, b, :], CV[:, b, :] if out is None else out
            step.step(nc.vector.tensor_scalar(y, u[:, 3:3 + T], taps_and_bias(taps - 1), taps_and_bias(taps),
                                              ALU.mult, ALU.add))
            for k in range(taps - 1):
                at = 3 - (taps - 1) + k
                (done if k == taps - 2 else step).step(nc.vector.scalar_tensor_tensor(
                    y, u[:, at:at + T], taps_and_bias(k), y, ALU.mult, ALU.add))

        mb = Carve()
        YB = mb(4 * GT, T)
        ZS = [mb(GT, T) for _ in range(2)]
        XSB = [mb(GT + 2, T) for _ in range(2)]
        XDT = [mb(SSM_HG, 64) for _ in range(2)]
        XF = [mb(SSM_HG, 64) for _ in range(2)]
        DEC = [mb(SSM_HG, P) for _ in range(2)]
        ECS = [mb(SSM_HG, P) for _ in range(2)]
        CBM = mb(P)
        BTOK = [mb(P) for _ in range(2)]
        FX = [mb(SSM_HG) for _ in range(2)]
        ETOT = [mb(SSM_HG) for _ in range(2)]
        STATE = mb(T)
        RSG = RDB[:, :]
        TMPY = mb(GT, P)
        DTR = mb(T)
        CSR = mb(T)
        DTA, DTB, DTC = (YB[:, i, :] for i in range(3))
        ALOG = mb(1)
        DTT = mb(NT, 32)
        CSTK = mb(NT, 32)
        UNITS = SSM_G * NT
        FILL = [3, 2, 3, 2]

        def norm_head(dve, count_h, gains, src=None):
            for k in range(KD):
                count_h.step(nc.vector.tensor_scalar(H[:, k, :], X[:, k, :], par(gains, k), None, ALU.mult))


        def add_pe(pe, name, rhs, cells, ready=None):
            per = 2 if name != "attn_out" and name != "w_out2" else 1
            turn = SLOTS // per
            with pe.Fori(0, KD // turn) as i:
                for j in range(turn):
                    gemm_tile(pe, name, i, j, lambda k: rhs(pe, k, j), cells, per)

        def add_act(act, name, turn):
            with act.Fori(0, KD) as k:
                act.wait_ge(gemm_free, k + (TILE0[name] + 1))
                nc.scalar.activation(SQ[:, bass.ds(k, 1), :], X[:, bass.ds(k, 1), :], ACT.Square).then_inc(sq_ready, 1)
            norm_scale_act(act, turn)

        def add_dve(dve, name, turn, gains, hr, fr, rs, extra=None):
            with dve.Fori(0, KD // 2) as i:
                fr.enter(i, 2)
                hr.enter(i, 2 if extra is None else 4)
                for j in range(2):
                    k = i * 2 + j
                    dve.wait_ge(gemm_done, i * 2 + (TILE0[name] + j + 1))
                    x = X[:, bass.ds(k, 1), :]
                    fr.step(nc.vector.tensor_tensor(x, x, BANK[(TILE0[name] + j) % 2][:, :].unsqueeze(1), ALU.add))
                    a, _ = PARAM[gains]
                    hr.step(nc.vector.tensor_scalar(H[:, bass.ds(k, 1), :], x, PAR[:, bass.ds(k + a, 1)], None, ALU.mult))
                    if extra is not None:
                        a, _ = PARAM[extra[0]]
                        hr.step(nc.vector.tensor_scalar(extra[1][:, bass.ds(k, 1), :], x, PAR[:, bass.ds(k + a, 1)],
                                                        None, ALU.mult))
                fr.leave(KD // 2)
                hr.leave(KD // 2)
            norm_scale_dve(dve, turn, rs)

        ff = Carve()
        FF = ff(FF_TILES, T)
        GATE = ff(T)

        def ffn_pe(pe, layer):
            norm_sums(pe, 2 * layer + 1)
            pe.wait_ge(h_ready, H_READY[2 * layer + 1])
            with pe.Fori(0, 2 * FF_TILES // SLOTS) as i:
                for j in range(SLOTS):
                    gemm_tile(pe, f"up{layer}", i, j, lambda k: H[:, k, :])

            def gated(pe, k, j):
                if j == 0 and (k == 0 or k >= FF_TILES - 3):
                    pe.wait_ge(ff_ready, FF_TILES * layer + max(k + 1, FF_TILES - 3))
                return FF[:, k, :]
            add_pe(pe, f"down{layer}", gated, 11)

        def ffn_act(act, layer):
            c0, _ = COUNT0[f"conv{layer}"]
            with act.Fori(0, FF_TILES) as m:
                act.wait_ge(conv_ready, m + (c0 + 1))
                nc.scalar.activation(GATE, CV[:, 0, :], ACT.Silu).then_inc(row_used, 1)
            add_act(act, f"down{layer}", 2 * layer + 2)

        def ffn_dve(dve, layer, gains, step, rs, hr, fr, cv, extra=None):
            name = f"up{layer}"
            _, r0 = COUNT0[f"conv{layer}"]
            ffr = Count(dve, ff_ready)
            ffr.n = FF_TILES * layer
            a, _ = PARAM[f"ffn_conv{layer}"]
            with dve.Fori(0, FF_TILES // 2) as i:
                for c, per in ((fr, 4), (step, 10), (cv, 2), (ffr, 2)):
                    c.enter(i, per)
                for j in range(4):
                    b = j % 2
                    dve.wait_ge(gemm_done, i * 4 + (TILE0[name] + j + 1))
                    if b == 0:
                        dve.wait_ge(row_used, i * 2 + (r0 + j // 2))
                    fr.step(nc.vector.tensor_tensor(U[:, b, 3:3 + T], BANK[(TILE0[name] + j) % 2][:, :], RS[:, :], ALU.mult))
                    conv(dve, step, cv if b == 0 else step, b,
                         lambda k: PAR[:, bass.ds(i * 16 + (a + 4 * j + k), 1)], 3)
                    if b == 1:
                        dve.wait_ge(row_used, i * 2 + (r0 + j // 2 + 1))
                        ffr.step(nc.vector.tensor_tensor(FF[:, bass.ds(i * 2 + j // 2, 1), :], GATE.unsqueeze(1),
                                                         CV[:, 1, :].unsqueeze(1), ALU.mult))
                for c in (fr, step, cv, ffr):
                    c.leave(FF_TILES // 2)
            add_dve(dve, f"down{layer}", 2 * layer + 2, gains, hr, fr, rs, extra)

        at = Carve()
        at.at = ff.at
        HQ = at(KD, T)
        BIAS = at(AH, T)
        BUCK = at(640)
        REL = at(AH)
        assert at.at <= 27600
        at.at = 0
        BROW = at(AH, 640)
        KN = [at(T) for _ in range(2)]
        QN = [at(T) for _ in range(2)]
        VT = [at(NT, P) for _ in range(2)]
        assert at.at <= ff.at
        at.at = 22600
        PR = [[at(T) for _ in range(2)] for _ in range(2)]
        ATT = [at(T) for _ in range(2)]
        OB = at(T)
        RH, OSTD = RDB[:, :], EMB[:, :]
        NM = [at(2) for _ in range(2)]
        SUMS = [at(2) for _ in range(2)]
        LAM = at(72)
        assert at.at <= 27600
        oh = Carve()
        OH = oh(AH, T)
        assert oh.at <= 5120

        aux_in = sem("bucket_rows_in")
        brow_done = sem("bias_row_done")
        brow_ready = sem("bias_row_ready")
        brow_out = sem("bias_rows_in_dram")
        bias_in = sem("bias_table_in")
        lam_step = sem("lambda_step")
        lam_exp = sem("lambda_exps")
        lam_act = sem("lambda_act_step")
        hsq = sem("head_squares_ready")
        hss = sem("head_square_sum_done")
        hstd = sem("head_rms_ready")
        kq_ready = sem("head_kq_ready")
        vt_done = sem("v_turned")
        v_ready = sem("v_ready")
        s_done = sem("scores_done")
        l_ready = sem("logits_ready")
        p_ready = sem("exps_ready")
        a_ready = sem("attn_ready")
        t_done = sem("attn_turned")
        t_ready = sem("attn_turned_ready")
        o_done = sem("attn_out_done")
        ob_ready = sem("head_out_ready")
        oss_done = sem("head_out_square_sum")
        ostd_ready = sem("head_out_rms")
        oh_ready = sem("head_out_normed")
        DSCR = nc.dram_tensor("bias_scratch", (AH, P, 640), F32, kind="Internal").ap()

        def attention_pool(pool):
            pool.wait_ge(gemm_done, TILE0["up0"] + 1)
            pool.dma_start(BUCK[0:33, :], A["bucket"]).then_inc(aux_in, 16)
            pool.dma_start(REL[0:33, :], A["rel"]).then_inc(aux_in, 16)
            pool.wait_ge(brow_ready, 2 * AH)
            pool.dma_start(DSCR.rearrange("h p m -> p h m"), BROW).then_inc(brow_out, 16)
            pool.wait_ge(brow_out, 16)
            skewed = bass.AP(tensor=DSCR.tensor, offset=P - 1, ap=[[639, P], [P * 640, AH], [1, T]])
            pool.dma_start(BIAS, skewed).then_inc(bias_in, 16)

        def attention_pe(pe):
            norm_sums(pe, 2)
            pe.wait_ge(aux_in, 32)
            for h in range(AH):
                if h >= 1:
                    pe.wait_ge(brow_ready, 2 * h)
                nc.tensor.matmul(BANK[2][:, :], REL[0:33, h:h + 1].to_broadcast([33, P]), BUCK[0:33, 0:T],
                                 start=True, stop=True)
                nc.tensor.matmul(BANK[3][:, 0:P], REL[0:33, h:h + 1].to_broadcast([33, P]), BUCK[0:33, T:640],
                                 start=True, stop=True).then_inc(brow_done, 1)
            pe.wait_ge(h_ready, H_READY[2])

            def tile(h, j):
                gemm_tile(pe, "kvq", 0, 3 * h + j, lambda k: (HQ if j == 2 else H)[:, k, :])

            def head_sums(h, which):
                if which == 1:
                    pe.wait_ge(v_ready, h + 1)
                elif h >= 1:
                    pe.wait_ge(hstd, 2 * h)
                pe.wait_ge(hsq, 2 * h + which + 1)
                nc.tensor.matmul(BANK[6][:, :], const("half_ones"), SQ[:, which, :], start=True, stop=True).then_inc(hss, 1)

            def turn_v(h):
                pe.wait_ge(hstd, 2 * h + 1)
                pe.wait_ge(gemm_free, TILE0["kvq"] + 3 * h + 2)
                for c in range(NT):
                    mm = nc.tensor.transpose(BANK[6][:, c * P:(c + 1) * P], U[:, 1, 3 + c * P:3 + (c + 1) * P], IDENT)
                mm.then_inc(vt_done, 1)

            def scores(h, i):
                w = NT * h + i
                if w >= 1:
                    pe.wait_ge(l_ready, w)
                else:
                    pe.wait_ge(brow_ready, 2 * AH)
                pe.wait_ge(kq_ready, 2 * h + 2)
                n = (i + 1) * P
                for c in range(2):
                    mm = nc.tensor.matmul(BANK[2 + c][:, 0:n], QN[h % 2][64 * c:64 * c + 64, i * P:(i + 1) * P],
                                          KN[h % 2][64 * c:64 * c + 64, 0:n], start=True, stop=True)
                mm.then_inc(s_done, 1)

            def turn_attn(h, i):
                w = NT * h + i
                pe.wait_ge(a_ready, w + 1)
                if w >= 1:
                    pe.wait_ge(t_ready, w)
                for kb in range(i + 1):
                    mm = nc.tensor.transpose(BANK[4][:, kb * P:(kb + 1) * P], PR[w % 2][0][:, kb * P:(kb + 1) * P], IDENT)
                mm.then_inc(t_done, 1)

            def attn_v(h, i):
                w = NT * h + i
                pe.wait_ge(t_ready, w + 1)
                pe.wait_ge(v_ready, h + 1)
                if i == 0 and h >= 1:
                    pe.wait_ge(ob_ready, 2 * h)
                for kb in range(i + 1):
                    mm = nc.tensor.matmul(BANK[5][:, i * P:(i + 1) * P], VT[h % 2][:, kb, :],
                                          ATT[w % 2][:, kb * P:(kb + 1) * P], start=(kb == 0), stop=(kb == i))
                mm.then_inc(o_done, 1)

            def out_sums(h):
                pe.wait_ge(ob_ready, 2 * h + 2)
                nc.tensor.matmul(BANK[7][:, :], ONES[:, :], SQ[:, 2, :], start=True, stop=True).then_inc(oss_done, 1)

            for j in range(3):
                tile(0, j)
            head_sums(0, 0)
            turn_v(0)
            head_sums(0, 1)
            for h in range(AH + 1):
                for i in range(NT):
                    w = NT * h + i
                    if h + 1 < AH and i < 3:
                        tile(h + 1, i)
                    if h < AH:
                        scores(h, i)
                    if 1 <= w < NT * AH + 1:
                        turn_attn((w - 1) // NT, (w - 1) % NT)
                    if 2 <= w < NT * AH + 2:
                        attn_v((w - 2) // NT, (w - 2) % NT)
                    if h + 1 < AH:
                        if i == 1:
                            head_sums(h + 1, 0)
                        if i == 2:
                            turn_v(h + 1)
                        if i == 3:
                            head_sums(h + 1, 1)
                    if i == 2 and h >= 1:
                        out_sums(h - 1)

            def normed(pe, k, j):
                if j == 0:
                    pe.wait_ge(oh_ready, k + 1)
                return OH[:, k, :]
            add_pe(pe, "attn_out", normed, 8)

        def attention_act(act):
            la = Count(act, lam_act)
            act.wait_ge(lam_step, 4)
            la.step(nc.scalar.activation(LAM[:, 66:68], LAM[:, 64:66], ACT.Exp))
            for h in range(AH):
                act.wait_ge(brow_done, h + 1)
                nc.scalar.activation(BROW[:, h, 0:T], BANK[2][:, :], ACT.Copy).then_inc(brow_ready, 1)
                nc.scalar.activation(BROW[:, h, T:640], BANK[3][:, 0:P], ACT.Copy).then_inc(brow_ready, 1)

            def squares(h, which):
                act.wait_ge(gemm_free, TILE0["kvq"] + 3 * h + 1 + 2 * which)
                if h >= 1:
                    act.wait_ge(hss, 2 * h + which - 1)
                nc.scalar.activation(SQ[:, which, :], U[:, 0, 3:3 + T] if which == 0 else CV[:, 0, :],
                                     ACT.Square).then_inc(hsq, 1)

            def rms(h, which):
                act.wait_ge(hss, 2 * h + which + 1)
                if 2 * h + which >= 1:
                    act.wait_ge(kq_ready, 2 * h + which)
                nc.scalar.activation(STD[:, :], BANK[6][:, :], ACT.Sqrt, bias=EPSC[:, 0:1], scale=1.0 / 64).then_inc(hstd, 1)

            def v_out(h):
                act.wait_ge(vt_done, h + 1)
                if h >= 2:
                    act.wait_ge(o_done, NT * (h - 1))
                nc.scalar.activation(VT[h % 2], BANK[6][:, :].rearrange("p (c d) -> p c d", d=P), ACT.Copy).then_inc(v_ready, 1)

            def exps(h, i):
                w = NT * h + i
                act.wait_ge(l_ready, w + 1)
                n = (i + 1) * P
                for c in range(2):
                    p = PR[w % 2][c][:, 0:n]
                    nc.scalar.activation(p, p, ACT.Exp, bias=NM[w % 2][:, c:c + 1],
                                         accum_out=SUMS[w % 2][:, c:c + 1]).then_inc(p_ready, 1)

            def turned(h, i):
                w = NT * h + i
                act.wait_ge(t_done, w + 1)
                if w >= 2:
                    act.wait_ge(o_done, w - 1)
                nc.scalar.activation(ATT[w % 2][:, 0:(i + 1) * P], BANK[4][:, 0:(i + 1) * P], ACT.Copy).then_inc(t_ready, 1)

            def head_out(h):
                act.wait_ge(o_done, NT * (h + 1))
                if h >= 1:
                    act.wait_ge(oh_ready, h)
                nc.scalar.activation(OB, BANK[5][:, :], ACT.Copy).then_inc(ob_ready, 1)
                nc.scalar.activation(SQ[:, 2, :], BANK[5][:, :], ACT.Square).then_inc(ob_ready, 1)

            def head_rms(h):
                act.wait_ge(oss_done, h + 1)
                nc.scalar.activation(OSTD, BANK[7][:, :], ACT.Sqrt, bias=EPSC[:, 0:1], scale=1.0 / P).then_inc(ostd_ready, 1)

            squares(0, 0)
            squares(0, 1)
            rms(0, 0)
            v_out(0)
            rms(0, 1)
            for h in range(AH + 1):
                for i in range(NT):
                    w = NT * h + i
                    if h + 1 < AH and i in (0, 2):
                        squares(h + 1, i // 2)
                    if 1 <= w < NT * AH + 1:
                        turned((w - 1) // NT, (w - 1) % NT)
                    if i == 1 and h >= 1:
                        head_out(h - 1)
                    if h < AH:
                        exps(h, i)
                    if h + 1 < AH:
                        if i == 1:
                            rms(h + 1, 0)
                        if i == 2:
                            v_out(h + 1)
                        if i == 3:
                            rms(h + 1, 1)
                    if i == 2 and h >= 1:
                        head_rms(h - 1)
            add_act(act, "attn_out", 3)

        def attention_dve(dve, step, rs, hr, fr, cv):
            ls, kq, lr, ar, ohr = (Count(dve, s) for s in (lam_step, kq_ready, l_ready, a_ready, oh_ready))
            for m in range(2):
                ls.step(nc.vector.tensor_tensor(LAM[:, 0:64], par("lam", 128 * m, 64), par("lam", 128 * m + 64, 64), ALU.mult))
                ls.step(nc.vector.tensor_reduce(LAM[:, 64 + m:65 + m], LAM[:, 0:64], AX.X, ALU.add))
            dve.wait_ge(lam_act, 1)
            ls.step(nc.vector.tensor_tensor(LAM[:, 68:69], LAM[:, 67:68], LAM[:, 66:67], ALU.subtract))
            ls.step(nc.vector.tensor_scalar(LAM[:, 68:69], LAM[:, 68:69], -LAM_INIT, None, ALU.add))
            ls.step(nc.vector.tensor_scalar(LAM[:, 69:70], par("subln"), 1.0 - LAM_INIT, None, ALU.mult))

            def evac(h, j):
                dve.wait_ge(gemm_done, TILE0["kvq"] + 3 * h + j + 1)
                if j == 1 and h >= 1:
                    dve.wait_ge(vt_done, h)
                dst = (U[:, 0, 3:3 + T], U[:, 1, 3:3 + T], CV[:, 0, :])[j]
                fr.step(nc.vector.tensor_tensor(dst, BANK[(TILE0["kvq"] + 3 * h + j) % 2][:, :], RS[:, :], ALU.mult))

            def head_norm(h, which):
                dve.wait_ge(hstd, 2 * h + which + 1)
                step.step(nc.vector.reciprocal(RH, STD[:, :]))
                if h >= 2:
                    dve.wait_ge(s_done, NT * (h - 1))
                src, dst = ((U[:, 0, 3:3 + T], KN[h % 2]), (CV[:, 0, :], QN[h % 2]))[which]
                kq.step(nc.vector.scalar_tensor_tensor(dst, src, par("q_norm" if which else "k_norm"), RH, ALU.mult, ALU.mult))

            def logits(h, i):
                w = NT * h + i
                n = (i + 1) * P
                if w == 0:
                    dve.wait_ge(bias_in, 16)
                dve.wait_ge(s_done, w + 1)
                if w >= 2:
                    dve.wait_ge(t_done, w - 1)
                for c in range(2):
                    p = PR[w % 2][c][:, 0:n]
                    step.step(nc.vector.scalar_tensor_tensor(p, BANK[2 + c][:, 0:n], 0.125, BIAS[:, h, T - n:T],
                                                             ALU.mult, ALU.add))
                    red = nc.vector.tensor_reduce(NM[w % 2][:, c:c + 1], p, AX.X, ALU.max, negate=True)
                    (lr if c else step).step(red)

            def combine(h, i):
                w = NT * h + i
                n = (i + 1) * P
                dve.wait_ge(p_ready, 2 * w + 2)
                s, (p0, p1) = SUMS[w % 2], PR[w % 2]
                step.step(nc.vector.reciprocal(s, s))
                step.step(nc.vector.tensor_tensor(s[:, 1:2], s[:, 1:2], LAM[:, 68:69], ALU.mult))
                step.step(nc.vector.tensor_scalar(p1[:, 0:n], p1[:, 0:n], s[:, 1:2], None, ALU.mult))
                ar.step(nc.vector.scalar_tensor_tensor(p0[:, 0:n], p0[:, 0:n], s[:, 0:1], p1[:, 0:n], ALU.mult, ALU.add))

            def out_norm(h):
                dve.wait_ge(ostd_ready, h + 1)
                step.step(nc.vector.reciprocal(RH, OSTD))
                if h == 0:
                    dve.wait_ge(brow_out, 16)
                ohr.step(nc.vector.scalar_tensor_tensor(OH[:, h, :], OB, LAM[:, 69:70], RH, ALU.mult, ALU.mult))

            for j in range(3):
                evac(0, j)
            head_norm(0, 0)
            for h in range(AH + 1):
                for i in range(NT):
                    w = NT * h + i
                    if 1 <= w < NT * AH + 1:
                        combine((w - 1) // NT, (w - 1) % NT)
                    if i == 0 and h < AH:
                        head_norm(h, 1)
                    if h + 1 < AH and i < 3:
                        evac(h + 1, i)
                    if h < AH:
                        logits(h, i)
                    if h + 1 < AH and i == 2:
                        head_norm(h + 1, 0)
                    if i == 3 and h >= 1:
                        out_norm(h - 1)
            add_dve(dve, "attn_out", 3, "ffn_ln1", hr, fr, rs)

        sec = Carve()
        YA = sec(2 * MH, T)
        YN = sec(NP_, T)
        GR, FA, FW, FC = (YN[:, i, :] for i in range(NP_))
        NZ = sec(NP_, T)
        HB = []
        for _ in range(2):
            HB.append(dict(q=sec(2, T), k=sec(2, T), v=sec(NT, 2 * P), o=sec(2, T), z=sec(2, T)))
        head_end = sec.at
        SW = sec(NT, T)
        DW = [sec(T) for _ in range(2)]
        HN = sec(2, T)
        after_heads = sec.at
        KS, KW = sec(T), sec(T)
        VS, VW = sec(NT, P), sec(NT, P)
        COS, SIN = sec(T), sec(T)
        rows_at = sec.at
        HC = sec(2, T)
        GK = sec(NT, 4)
        GN = sec(NT, 24)
        KCC = sec(NCMP)
        assert sec.at <= 27600, sec.at
        sec.at = 8 * T * 2
        QRAW = sec(NP_, T)
        QR = sec(NP_, T)
        KVC = sec(2, T)
        CW1V = sec(CMPL, P)
        SGA = CW1V.rearrange("p a b -> p (a b)").rearrange("p (a b) -> p a b", b=T)
        CW1K = SQ[:, :, :].rearrange("p a b -> p (a b)").rearrange("p (a b) -> p a b", b=P)
        SGB = SQ
        pb_at = sec.at
        PB = [[sec(T) for _ in range(2)] for _ in range(2)]
        AT2 = [[sec(T) for _ in range(2)] for _ in range(2)]
        NM2 = [sec(2) for _ in range(2)]
        SM2 = [sec(2) for _ in range(2)]
        CL = sec(NT, NCMP)
        CMX, CSM = sec(NT), sec(NT)
        assert sec.at <= after_heads, (sec.at, after_heads)
        PCT = [HC[:, i, :] for i in range(2)]
        sec.at = pb_at
        UC = [sec(CMPL, NCMP) for _ in range(2)]
        sec.at = 8 * T * 2
        MG = sec(KD, T)
        CW2 = CW2B[:, :]
        HG = HGB[:, :]
        VCC = VCCB[:, :]
        EM, RDEN = EMB[:, :], RDB[:, :]

        gates_done = sem("gate_rows_done")
        g_row = sem("gate_rows_step")
        g_act = sem("gate_act_step")
        gT_done = sem("gates_turned")
        pos_in = sem("positions_in")
        rope_step = sem("rope_step")
        rope_act = sem("rope_act_step")
        bc_done = sem("maxima_spread")
        em_ready = sem("floor_ready")
        dw_ready = sem("mlstm_exponents")
        dwe_ready = sem("mlstm_decay")
        s2_done = sem("mlstm_scores")
        sw_ready = sem("mlstm_weights")
        nd_done = sem("mlstm_sums")
        hn_ready = sem("mlstm_heads")
        mean_done = sem("head_mean_sum")
        hc_ready = sem("head_centered")
        hcsq = sem("head_centered_squares")
        var_done = sem("head_variance_sum")
        vstd = sem("head_deviation")
        ya_ready = sem("mlstm_out_ready")
        vt2_done = sem("values_turned")
        cmp_w_in = sem("compress_weights_in")
        turn_done = sem("rope_turn_done")
        roped = sem("rope_ready")
        vsw_done = sem("nsa_values_turned")
        vsw_ready = sem("nsa_values_ready")
        uc_ready = sem("compress_blocks_ready")
        hid_done = sem("compress_hidden_done")
        hid_ready = sem("compress_hidden_ready")
        kvc_done = sem("compressed_done")
        kvc_ready = sem("compressed_ready")
        cs_done = sem("compressed_scores")
        cl_ready = sem("compressed_logits")
        ce_ready = sem("compressed_exps")
        cp_ready = sem("compressed_probs")
        ct_done = sem("compressed_turned")
        pct_ready = sem("compressed_turned_ready")
        n_s = sem("nsa_scores")
        n_l = sem("nsa_maxima")
        n_p = sem("nsa_exps")
        n_a = sem("nsa_probs")
        n_t = sem("nsa_turned")
        n_tc = sem("nsa_turned_ready")
        n_o = sem("nsa_out")
        yn_out = sem("nsa_gated")
        mg_ready = sem("merged_ready")
        out_ready = sem("output_ready")
        stored = sem("output_stored")

        HT = 10
        NQ0, NZ0, GA0 = 40, 50, 54
        R0, C0 = 84, 68
        W2 = "w_in2"

        def used(n):
            return R0 + min(n, NQ0) + max(n - NZ0, 0)

        def convs(n):
            return C0 + 4 * (n // HT) + min(n % HT, 4)

        def second_pool(pool):
            pool.wait_ge(gemm_done, TILE0[W2] + 1)
            pool.dma_start(COS.bitcast(mybir.dt.int32), A["pos"]).then_inc(pos_in, 16)
            pool.dma_start(CW2, A["cmp_w2"]).then_inc(cmp_w_in, 16)
            pool.wait_ge(ya_ready, 2 * MH)
            pool.dma_start(CW1K, A["cmp_w1"][0]).then_inc(cmp_w_in, 16)
            pool.dma_start(CW1V, A["cmp_w1"][1]).then_inc(cmp_w_in, 16)

        def second_pe(pe):
            norm_sums(pe, 4)
            pe.wait_ge(h_ready, H_READY[4])
            for k in range(KD):
                mm = nc.tensor.matmul(BANK[6][0:88, :], SMALL[:, k, 32:120], H[:, k, :], start=(k == 0), stop=(k == KD - 1))
            mm.then_inc(gates_done, 1)

            def tile(n):
                gemm_tile(pe, W2, 0, n, lambda k: H[:, k, :])

            def turn_value(n):
                pe.wait_ge(gemm_free, TILE0[W2] + n + 1)
                pe.wait_ge(row_used, used(n))
                for c in range(NT):
                    mm = nc.tensor.transpose(BANK[4][:, c * P:(c + 1) * P], U[:, n % 2, 3 + c * P:3 + (c + 1) * P], IDENT)
                mm.then_inc(vt2_done, 1)

            def spread(h):
                if h >= 1:
                    pe.wait_ge(vstd, h)
                pe.wait_ge(row_used, used(HT * h + 6))
                nc.tensor.matmul(BANK[2][:, :], IDENT[0:4, h:h + 1].to_broadcast([4, P]), FW[0:4, :], start=True, stop=True)
                nc.tensor.matmul(BANK[4][:, :], IDENT[0:4, h:h + 1].to_broadcast([4, P]), FA[0:4, :],
                                 start=True, stop=True).then_inc(bc_done, 1)

            def scores(h, sb):
                if h or sb:
                    pe.wait_ge(sw_ready, NT * h + sb)
                pe.wait_ge(row_used, used(HT * h + 4))
                b = HB[h % 2]
                for e in range(2):
                    mm = nc.tensor.matmul(BANK[3][:, 0:T - sb * P], b["k"][:, e, sb * P:(sb + 1) * P], b["q"][:, e, sb * P:T],
                                          start=(e == 0), stop=(e == 1))
                mm.then_inc(s2_done, 1)

            def sums(h, sb):
                pe.wait_ge(sw_ready, NT * h + sb + 1)
                if sb == 0 and h >= 1:
                    pe.wait_ge(hn_ready, 2 * h)
                pe.wait_ge(row_used, used(HT * h + 6))
                first, last = sb == 0, sb == NT - 1
                at = slice(sb * P, T)
                for e in range(2):
                    nc.tensor.matmul(BANK[5 + e][:, at], HB[h % 2]["v"][:, sb, e * P:(e + 1) * P], SW[:, sb, 0:T - sb * P],
                                     start=first, stop=last)
                mm = nc.tensor.matmul(BANK[7][:, at], ONES[:, :], SW[:, sb, 0:T - sb * P], start=first, stop=last)
                if last:
                    mm.then_inc(nd_done, 1)

            def mean(h):
                pe.wait_ge(hn_ready, 2 * h + 2)
                for e in range(2):
                    mm = nc.tensor.matmul(BANK[2][:, :], ONES[:, :], HN[:, e, :], start=(e == 0), stop=(e == 1))
                mm.then_inc(mean_done, 1)

            def variance(h):
                pe.wait_ge(hcsq, h + 1)
                for e in range(2):
                    mm = nc.tensor.matmul(BANK[2][:, :], ONES[:, :], SQ[:, e, :], start=(e == 0), stop=(e == 1))
                mm.then_inc(var_done, 1)

            for n in range(HT):
                tile(n)
                if n in (5, 6):
                    turn_value(n - 1)
            pe.wait_ge(g_row, 15)
            pe.wait_ge(g_act, 1)
            for c in range(NT):
                tok = slice(c * P, (c + 1) * P)
                nc.tensor.transpose(BANK[6][:, 32 * c:32 * c + 4], GR[0:4, tok], IDENT[0:4, 0:4])
                mm = nc.tensor.transpose(BANK[5][:, 32 * c:32 * c + 24], GR[64:88, tok], IDENT[64:88, 64:88])
            mm.then_inc(gT_done, 1)
            pe.wait_ge(g_row, 17)
            for h in range(MH):
                m = HT * (h + 1)
                spread(h)
                tile(m)
                scores(h, 0)
                tile(m + 1)
                for sb in range(1, NT):
                    sums(h, sb - 1)
                    scores(h, sb)
                    tile(m + 1 + sb)
                sums(h, NT - 1)
                tile(m + 5)
                if h + 1 < MH:
                    turn_value(m + 4)
                mean(h)
                tile(m + 6)
                if h + 1 < MH:
                    turn_value(m + 5)
                variance(h)
                for n in range(7, HT):
                    tile(m + n)
            def turn_nsa_value(x):
                pe.wait_ge(gemm_free, TILE0[W2] + 49 + x)
                if x:
                    pe.wait_ge(vsw_ready, 1)
                for c in range(NT):
                    mm = nc.tensor.transpose(BANK[4][:, c * P:(c + 1) * P], CV[:, x, c * P:(c + 1) * P], IDENT)
                mm.then_inc(vsw_done, 1)

            def turn_rope(x):
                if x >= 2:
                    pe.wait_ge(roped, x - 1)
                pe.wait_ge(vstd, MH)
                src = QRAW[:, x, :] if x < NP_ else (KS, KW)[x - NP_]
                nc.tensor.matmul(BANK[2 + x % 2][:, :], const("rope_turn"), src, start=True, stop=True).then_inc(turn_done, 1)

            turn_rope(0)
            turn_rope(1)
            tile(NZ0)
            turn_nsa_value(0)
            turn_rope(2)
            turn_rope(3)
            tile(NZ0 + 1)
            turn_nsa_value(1)
            turn_rope(4)
            turn_rope(5)
            tile(NZ0 + 2)
            pe.wait_ge(cmp_w_in, 48)
            pe.wait_ge(uc_ready, 2)
            for x in range(2):
                for g in range(2):
                    half = slice(64 * g, 64 * g + 64)
                    at = 32 * x
                    for l in range(CMPL):
                        mm = nc.tensor.matmul(BANK[7 if g else 5][:, at:at + NCMP], (CW1K, CW1V)[x][half, l, :], UC[x][half, l, :],
                                              start=(l == 0), stop=(l == CMPL - 1))
            mm.then_inc(hid_done, 1)
            tile(NZ0 + 3)
            pe.wait_ge(hid_ready, 2)
            for g in range(2):
                nc.tensor.matmul(BANK[7][64 * g:64 * g + 64, 128:128 + NCMP], CW2[:, 0:64], HG[:, 32 * g:32 * g + NCMP],
                                 start=True, stop=True)
                mm = nc.tensor.matmul(BANK[7][0:NCMP, 192 + 64 * g:256 + 64 * g], HG[:, 64 + 32 * g:64 + 32 * g + NCMP],
                                      CW2[:, 64:128], start=True, stop=True)
            mm.then_inc(kvc_done, 1)

            def cmp_scores(s):
                g, j = s % 2, s // 2
                half = slice(64 * g, 64 * g + 64)
                pe.wait_ge(kvc_ready, 2)
                if s >= 1:
                    pe.wait_ge(pct_ready, s)
                for i in range(NT):
                    mm = nc.tensor.matmul(BANK[7][:, NCMP * i:NCMP * (i + 1)], QRAW[half, j, i * P:(i + 1) * P],
                                          KCC[half, :], start=True, stop=True)
                mm.then_inc(cs_done, 1)

            def cmp_turn(s):
                pe.wait_ge(cp_ready, s + 1)
                for i in range(NT):
                    mm = nc.tensor.transpose(BANK[7][0:NCMP, i * P:(i + 1) * P], CL[:, i, :], IDENT)
                mm.then_inc(ct_done, 1)

            def nsa_scores(w):
                s, i = w // NT, w % NT
                g, j = s % 2, s // 2
                half = slice(64 * g, 64 * g + 64)
                pe.wait_ge(roped, 6)
                if w >= 1:
                    pe.wait_ge(n_p, 2 * w)
                for c, keys in enumerate((KS, KW)):
                    nc.tensor.matmul(BANK[2 + c][:, 0:(i + 1) * P], QR[half, j, i * P:(i + 1) * P], keys[half, 0:(i + 1) * P],
                                     start=True, stop=False)
                    mm = nc.tensor.matmul(BANK[2 + c][:, i * P:(i + 1) * P], IDENT, const("future_neg"), start=False, stop=True)
                mm.then_inc(n_s, 1)

            def nsa_turn(w):
                i = w % NT
                pe.wait_ge(n_a, w + 1)
                if w >= 1:
                    pe.wait_ge(n_tc, 2 * w)
                else:
                    pe.wait_ge(vsw_ready, 2)
                for c in range(2):
                    for kb in range(i + 1):
                        mm = nc.tensor.transpose(BANK[4 + c][:, kb * P:(kb + 1) * P], PB[w % 2][c][:, kb * P:(kb + 1) * P], IDENT)
                mm.then_inc(n_t, 1)

            def nsa_v(w):
                s, i = w // NT, w % NT
                g, j = s % 2, s // 2
                pe.wait_ge(n_tc, 2 * w + 2)
                pe.wait_ge(pct_ready, s + 1)
                if w % 8 == 0 and w:
                    pe.wait_ge(yn_out, j)
                out_t = BANK[6][64 * g:64 * g + 64, i * P:(i + 1) * P]
                nc.tensor.matmul(out_t, VCC[0:NCMP, 64 * g:64 * g + 64], PCT[s % 2][0:NCMP, i * P:(i + 1) * P],
                                 start=True, stop=False)
                for c, values in enumerate((VS, VW)):
                    for kb in range(i + 1):
                        mm = nc.tensor.matmul(out_t, values[:, kb, 64 * g:64 * g + 64], AT2[w % 2][c][:, kb * P:(kb + 1) * P],
                                              start=False, stop=(c == 1 and kb == i))
                mm.then_inc(n_o, 1)

            cmp_scores(0)
            cmp_turn(0)
            for w in range(NT * 8 + 2):
                if w % 2 == 0 and w < 32:
                    tile(GA0 + w // 2)
                if w < 32:
                    nsa_scores(w)
                if 1 <= w < 33:
                    nsa_turn(w - 1)
                if w >= 2:
                    nsa_v(w - 2)
                if w < 28 and w % NT == 0:
                    cmp_scores(w // NT + 1)
                if w < 28 and w % NT == 2:
                    cmp_turn(w // NT + 1)
            pe.wait_ge(ya_ready, 2 * MH)
            with pe.Fori(0, KD // 2) as i:
                for j in range(4):
                    if j % 2 == 1:
                        pe.wait_ge(yn_out, NP_)
                    gemm_tile(pe, "ab", i, j, lambda k: (YN if j % 2 else YA)[:, k, :], 4 if j % 2 else 8)

            def merged(pe, k, j):
                if j == 0:
                    pe.wait_ge(mg_ready, k + 1)
                return MG[:, k, :]
            add_pe(pe, "w_out2", merged, 8)
            norm_sums(pe, 5)

        def second_act(act):
            ga = Count(act, g_act)
            act.wait_ge(g_row, 2)
            ga.step(nc.scalar.activation(GR[64:88, :], GR[64:88, :], ACT.Sigmoid))
            ga.step(nc.scalar.activation(FA[32:36, :], GR[32:36, :], ACT.Abs))
            ga.step(nc.scalar.activation(FA[32:36, :], FA[32:36, :], ACT.Exp, scale=-1.0))
            act.wait_ge(g_row, 3)
            ga.step(nc.scalar.activation(HC[32:36, 0, :], FW[32:36, :], ACT.Ln))
            ra = Count(act, rope_act)
            act.wait_ge(rope_step, 8)
            ra.step(nc.scalar.activation(SIN, HC[:, 1, :], ACT.Sin))
            ra.step(nc.scalar.activation(COS, HC[:, 1, :], ACT.Abs))
            act.wait_ge(rope_step, 9)
            ra.step(nc.scalar.activation(COS, COS, ACT.Sin))

            def rows(n):
                h, j = n // HT, n % HT
                b = HB[h % 2]
                if n < NQ0:
                    if h >= 2 and j == 0:
                        act.wait_ge(ya_ready, 2 * (h - 1))
                    if j < 4:
                        act.wait_ge(conv_ready, convs(n) + 1)
                        ins = nc.scalar.activation(b["q" if j < 2 else "k"][:, j % 2, :], CV[:, n % 2, :], ACT.Silu)
                    elif j < 6:
                        act.wait_ge(vt2_done, 2 * h + j - 3)
                        ins = nc.scalar.activation(b["v"][:, :, (j - 4) * P:(j - 3) * P],
                                                   BANK[4][:, :].rearrange("p (c d) -> p c d", d=P), ACT.Copy)
                    else:
                        act.wait_ge(gemm_free, TILE0[W2] + n + 1)
                        ins = nc.scalar.activation(b["o" if j < 8 else "z"][:, j % 2, :], U[:, n % 2, 3:3 + T],
                                                   ACT.Sigmoid if j < 8 else ACT.Silu)
                else:
                    act.wait_ge(gemm_free, TILE0[W2] + n + 1)
                    if n >= GA0:
                        act.wait_ge(hid_done, 1)
                        k = n - GA0
                        ins = nc.scalar.activation((SGA if k < KD else SGB)[:, k % KD, :], U[:, n % 2, 3:3 + T], ACT.Sigmoid)
                    else:
                        ins = nc.scalar.activation(NZ[:, n - NZ0, :], U[:, n % 2, 3:3 + T], ACT.Silu)
                ins.then_inc(row_used, 1)

            def decay(h, sb):
                act.wait_ge(dw_ready, NT * h + sb + 1)
                d = DW[sb % 2][:, 0:T - sb * P]
                nc.scalar.activation(d, d, ACT.Exp).then_inc(dwe_ready, 1)

            for n in range(HT):
                rows(n)
            for h in range(MH):
                m = HT * (h + 1)
                act.wait_ge(bc_done, h + 1)
                if h >= 1:
                    act.wait_ge(hn_ready, 2 * h)
                nc.scalar.activation(EM, BANK[4][:, :], ACT.Exp, scale=-1.0).then_inc(em_ready, 1)

                def next_rows(*js):
                    if h + 1 < MH:
                        for j in js:
                            rows(m + j)
                next_rows(0)
                decay(h, 0)
                next_rows(1)
                for sb in range(1, NT):
                    decay(h, sb)
                    if sb < 3:
                        next_rows(1 + sb)
                next_rows(4)
                act.wait_ge(hc_ready, 2 * h + 2)
                nc.scalar.activation(SQ[:, 0:2, :], HC, ACT.Square).then_inc(hcsq, 1)
                next_rows(5)
                act.wait_ge(var_done, h + 1)
                nc.scalar.activation(STD[:, :], BANK[2][:, :], ACT.Sqrt, bias=EPSC[:, 0:1], scale=1.0 / 256).then_inc(vstd, 1)
                next_rows(6, 7, 8, 9)

            def nsa_value(x):
                act.wait_ge(vsw_done, x + 1)
                nc.scalar.activation((VS, VW)[x], BANK[4][:, :].rearrange("p (c d) -> p c d", d=P), ACT.Copy).then_inc(vsw_ready, 1)

            nsa_value(0)
            rows(NZ0)
            nsa_value(1)
            rows(NZ0 + 1)
            rows(NZ0 + 2)
            act.wait_ge(hid_done, 1)
            for g in range(2):
                nc.scalar.activation(HG.rearrange("p (a g n) -> p a g n", g=2, n=32)[:, :, g, 0:NCMP],
                                     BANK[7 if g else 5][:, 0:64].rearrange("p (a n) -> p a n", n=32)[:, :, 0:NCMP],
                                     ACT.Gelu_apprx_tanh).then_inc(hid_ready, 1)
            rows(NZ0 + 3)

            def cmp_exp(s):
                act.wait_ge(cl_ready, s + 1)
                nc.scalar.activation(CL, CL, ACT.Exp).then_inc(ce_ready, 1)

            def cmp_turned(s):
                act.wait_ge(ct_done, s + 1)
                if s >= 2:
                    act.wait_ge(n_o, NT * (s - 1))
                nc.scalar.activation(PCT[s % 2][0:NCMP, :], BANK[7][0:NCMP, :], ACT.Copy).then_inc(pct_ready, 1)

            def exps(w):
                n = (w % NT + 1) * P
                act.wait_ge(n_l, w + 1)
                if w >= 2:
                    act.wait_ge(n_t, w - 1)
                for c in range(2):
                    nc.scalar.activation(PB[w % 2][c][:, 0:n], BANK[2 + c][:, 0:n], ACT.Exp, bias=NM2[w % 2][:, c:c + 1],
                                         scale=0.125, accum_out=SM2[w % 2][:, c:c + 1]).then_inc(n_p, 1)

            def turned(w):
                n = (w % NT + 1) * P
                act.wait_ge(n_t, w + 1)
                if w >= 2:
                    act.wait_ge(n_o, w - 1)
                for c in range(2):
                    nc.scalar.activation(AT2[w % 2][c][:, 0:n], BANK[4 + c][:, 0:n], ACT.Copy).then_inc(n_tc, 1)

            cmp_exp(0)
            cmp_turned(0)
            for w in range(NT * 8 + 2):
                if 1 <= w < 33:
                    turned(w - 1)
                if w < 32:
                    exps(w)
                if w % 2 == 0 and w < 32:
                    rows(GA0 + w // 2)
                if w < 28 and w % NT == 0:
                    cmp_exp(w // NT + 1)
                if w < 28 and w % NT == 2:
                    cmp_turned(w // NT + 1)
            add_act(act, "w_out2", 5)

        def second_dve(dve, step, rs, hr, fr, cv):
            gr, rp = Count(dve, g_row), Count(dve, rope_step)
            dve.wait_ge(gates_done, 1)
            gr.step(nc.vector.tensor_tensor(GR[0:88, :], BANK[6][0:88, :], RS[0:88, :], ALU.mult))
            gr.step(nc.vector.tensor_scalar(GR[0:88, :], GR[0:88, :], par("gate_bias", parts=88), None, ALU.add))
            f, fa, fw, fc = (b[32:36, :] for b in (GR, FA, FW, FC))
            dve.wait_ge(g_act, 3)
            gr.step(nc.vector.tensor_scalar(fw, fa, 1.0, None, ALU.add))
            gr.step(nc.vector.tensor_scalar(fc, fw, -1.0, None, ALU.add))
            gr.step(nc.vector.tensor_tensor(fa, fa, fc, ALU.subtract))
            gr.step(nc.vector.tensor_scalar(f, f, 0.0, None, ALU.min))
            dve.wait_ge(g_act, 4)
            gr.step(nc.vector.tensor_tensor(fa, fa, HC[32:36, 0, :], ALU.add))
            gr.step(nc.vector.tensor_tensor(f, f, fa, ALU.subtract))
            gr.step(nc.vector.memset(fw, 1.0))
            gr.step(nc.vector.tensor_tensor_scan(fc, fw, f, 0.0, ALU.mult, ALU.add))
            li, f0, mx, mt = GR[0:4, :], FC[0:4, :], FW[0:4, :], FA[0:4, :]
            gr.step(nc.vector.tensor_copy(f0, fc))
            gr.step(nc.vector.tensor_tensor(li, li, f0, ALU.subtract))
            gr.step(nc.vector.tensor_tensor_scan(mx, li, li, 0.0, ALU.max, ALU.max))
            gr.step(nc.vector.tensor_tensor(mt, mx, f0, ALU.add))
            gr.step(nc.vector.tensor_scalar(mx, mx, -1.0, None, ALU.mult))
            ang, turns = HC[:, 1, :], SIN
            dve.wait_ge(pos_in, 16)
            dve.wait_ge(row_used, R0)
            rp.step(nc.vector.tensor_copy(ang, COS.bitcast(mybir.dt.int32)))
            rp.step(nc.vector.tensor_scalar(ang, ang, const("rope_freq"), None, ALU.mult))
            rp.step(nc.vector.tensor_scalar(turns, ang, 1.0 / (2 * math.pi), 1.5 * 2 ** 23, ALU.mult, ALU.add))
            rp.step(nc.vector.tensor_scalar(turns, turns, -1.5 * 2 ** 23, None, ALU.add))
            p1, p2 = 6.28125, float(np.float32(2 * math.pi - 6.28125).view(np.uint32).__and__(np.uint32(0xFFFFF000)).view(np.float32))
            for part in (p1, p2, 2 * math.pi - p1 - p2):
                rp.step(nc.vector.scalar_tensor_tensor(ang, turns, -part, ang, ALU.mult, ALU.add))
            rp.step(nc.vector.tensor_scalar(ang, ang, 3.1415925, -3.1415925, ALU.min, ALU.max))
            dve.wait_ge(rope_act, 2)
            rp.step(nc.vector.tensor_scalar(COS, COS, -1.0, math.pi / 2, ALU.mult, ALU.add))

            def evac(n, dst):
                dve.wait_ge(gemm_done, TILE0[W2] + n + 1)
                fr.step(nc.vector.tensor_tensor(dst, BANK[(TILE0[W2] + n) % 2][:, :], RS[:, :], ALU.mult))

            def rows(n):
                h, j = n // HT, n % HT
                if n < NQ0 or n >= NZ0:
                    if n >= 2:
                        dve.wait_ge(row_used, used(n - 1))
                    evac(n, U[:, n % 2, 3:3 + T])
                    if n < NQ0 and j < 4:
                        t = 2 * h + j % 2 + (8 if j >= 2 else 0)
                        conv(dve, step, cv, n % 2, lambda k: par("qk_conv", 5 * t + k), 4)
                    return
                k = n - NQ0
                if k == 8:
                    dve.wait_ge(row_used, used(NQ0))
                evac(n, [QRAW[:, 0, :], QRAW[:, 1, :], QRAW[:, 2, :], QRAW[:, 3, :], KVC[:, 0, :], KVC[:, 1, :],
                         KS, KW, CV[:, 0, :], CV[:, 1, :]][k])

            dw, sw, hn, hc, ya = (Count(dve, s) for s in (dw_ready, sw_ready, hn_ready, hc_ready, ya_ready))

            def exponents(h, sb):
                if sb == 0:
                    dve.wait_ge(bc_done, h + 1)
                n = T - sb * P
                dw.step(nc.vector.tensor_scalar(DW[sb % 2][:, 0:n], BANK[2][:, sb * P:T], GK[:, sb, h:h + 1], 0.0,
                                                ALU.add, ALU.min))

            def weights(h, sb):
                n = T - sb * P
                dve.wait_ge(dwe_ready, NT * h + sb + 1)
                dve.wait_ge(s2_done, NT * h + sb + 1)
                step.step(nc.vector.scalar_tensor_tensor(SW[:, sb, 0:n], BANK[3][:, 0:n], 1.0 / 16, DW[sb % 2][:, 0:n],
                                                         ALU.mult, ALU.mult))
                sw.step(nc.vector.tensor_tensor(SW[:, sb, 0:P], SW[:, sb, 0:P], const("causal_st"), ALU.mult))

            def divide(h):
                dve.wait_ge(nd_done, h + 1)
                dve.wait_ge(em_ready, h + 1)
                step.step(nc.vector.tensor_scalar(RDEN, BANK[7][:, :], -1.0, None, ALU.mult))
                step.step(nc.vector.tensor_tensor(RDEN, RDEN, BANK[7][:, :], ALU.max))
                step.step(nc.vector.tensor_tensor(RDEN, RDEN, EM, ALU.max))
                step.step(nc.vector.reciprocal(RDEN, RDEN))
                for e in range(2):
                    hn.step(nc.vector.tensor_tensor(HN[:, e, :], BANK[5 + e][:, :], RDEN, ALU.mult))

            def center(h):
                dve.wait_ge(mean_done, h + 1)
                for e in range(2):
                    hc.step(nc.vector.scalar_tensor_tensor(HC[:, e, :], BANK[2][:, :], -1.0 / 256, HN[:, e, :], ALU.mult, ALU.add))

            def gated(h):
                dve.wait_ge(vstd, h + 1)
                dve.wait_ge(row_used, used(HT * (h + 1)))
                step.step(nc.vector.reciprocal(RDEN, STD[:, :]))
                for e in range(2):
                    step.step(nc.vector.scalar_tensor_tensor(HC[:, e, :], HC[:, e, :], par("mh_norm", 2 * h + e), RDEN, ALU.mult, ALU.mult))
                    step.step(nc.vector.tensor_tensor(HC[:, e, :], HC[:, e, :], HB[h % 2]["o"][:, e, :], ALU.mult))
                    ya.step(nc.vector.tensor_tensor(YA[:, 2 * h + e, :], HC[:, e, :], HB[h % 2]["z"][:, e, :], ALU.mult))

            for n in range(HT):
                rows(n)
            dve.wait_ge(gT_done, 1)
            b6 = BANK[6][:, 0:P].rearrange("p (c w) -> p c w", w=32)
            gr.step(nc.vector.tensor_copy(GK, b6[:, :, 0:4]))
            b5 = BANK[5][:, 0:P].rearrange("p (c w) -> p c w", w=32)
            gr.step(nc.vector.tensor_copy(GN, b5[:, :, 0:24]))
            for h in range(MH):
                m = HT * (h + 1)
                exponents(h, 0)
                rows(m)
                weights(h, 0)
                exponents(h, 1)
                rows(m + 1)
                for sb in range(1, NT):
                    weights(h, sb)
                    if sb + 1 < NT:
                        exponents(h, sb + 1)
                    rows(m + 1 + sb)
                divide(h)
                rows(m + 5)
                center(h)
                rows(m + 6)
                gated(h)
                for n in range(7, HT):
                    rows(m + n)

            ro, uc, kvc = (Count(dve, s) for s in (roped, uc_ready, kvc_ready))

            def rotate(x):
                dve.wait_ge(turn_done, x + 1)
                dve.wait_ge(rope_act, 3)
                src, dst = (QRAW[:, x, :], QR[:, x, :]) if x < NP_ else ((KS, KW)[x - NP_],) * 2
                step.step(nc.vector.tensor_tensor(RDEN, BANK[2 + x % 2][:, :], SIN, ALU.mult))
                step.step(nc.vector.tensor_tensor(dst, src, COS, ALU.mult))
                ro.step(nc.vector.tensor_tensor(dst, dst, RDEN, ALU.add))

            rotate(0)
            rotate(1)
            rows(NZ0)
            rotate(2)
            rotate(3)
            rows(NZ0 + 1)
            for x in range(2):
                blocks = bass.AP(tensor=KVC.tensor, offset=KVC[:, x, :].offset, ap=[KVC.ap[0], [1, CMPL], [16, NCMP]])
                uc.step(nc.vector.tensor_tensor(UC[x], blocks, par("cmp_pos", CMPL * x, CMPL).unsqueeze(2)
                                                .to_broadcast([P, CMPL, NCMP]), ALU.add))
            rotate(4)
            rotate(5)
            rows(NZ0 + 2)
            rows(NZ0 + 3)
            dve.wait_ge(kvc_done, 1)
            kvc.step(nc.vector.tensor_copy(KCC, BANK[7][:, 128:128 + NCMP]))
            kvc.step(nc.vector.tensor_copy(VCC[0:NCMP, :], BANK[7][0:NCMP, 192:320]))

            cl, cp, nl, na, yo, mg = (Count(dve, s) for s in (cl_ready, cp_ready, n_l, n_a, yn_out, mg_ready))
            cells = [P, NT, NCMP]

            def head_of(s):
                return s // 2 + 4 * (s % 2)

            def cmp_logits(s):
                dve.wait_ge(cs_done, s + 1)
                if s >= 1:
                    dve.wait_ge(ct_done, s)
                sc = BANK[7][:, 0:NT * NCMP].rearrange("p (i n) -> p i n", n=NCMP)
                neg = const("cmp_neg").rearrange("p (i n) -> p i n", n=NCMP)
                step.step(nc.vector.scalar_tensor_tensor(CL, sc, 0.125, neg, ALU.mult, ALU.add))
                step.step(nc.vector.tensor_reduce(CMX, CL, AX.X, ALU.max))
                cl.step(nc.vector.tensor_tensor(CL, CL, CMX.unsqueeze(2).to_broadcast(cells), ALU.subtract))

            def cmp_probs(s):
                dve.wait_ge(ce_ready, s + 1)
                h = head_of(s)
                step.step(nc.vector.tensor_reduce(CSM, CL, AX.X, ALU.add))
                step.step(nc.vector.reciprocal(CSM, CSM))
                step.step(nc.vector.tensor_tensor(CSM, CSM, GN[:, :, 3 * h], ALU.mult))
                step.step(nc.vector.tensor_tensor(CL, CL, const("cmp_seen").rearrange("p (i n) -> p i n", n=NCMP), ALU.mult))
                cp.step(nc.vector.tensor_tensor(CL, CL, CSM.unsqueeze(2).to_broadcast(cells), ALU.mult))

            def maxima(w):
                n = (w % NT + 1) * P
                dve.wait_ge(n_s, w + 1)
                for c in range(2):
                    step.step(nc.vector.tensor_reduce(NM2[w % 2][:, c:c + 1], BANK[2 + c][:, 0:n], AX.X, ALU.max, negate=True))
                nl.step(nc.vector.tensor_scalar(NM2[w % 2], NM2[w % 2], 0.125, None, ALU.mult))

            def probs(w):
                s, i = w // NT, w % NT
                h, n = head_of(s), (i + 1) * P
                dve.wait_ge(n_p, 2 * w + 2)
                sm = SM2[w % 2]
                step.step(nc.vector.reciprocal(sm, sm))
                step.step(nc.vector.tensor_tensor(sm, sm, GN[:, i, 3 * h + 1:3 * h + 3], ALU.mult))
                for c in range(2):
                    p = PB[w % 2][c][:, 0:n]
                    (na if c else step).step(nc.vector.tensor_scalar(p, p, sm[:, c:c + 1], None, ALU.mult))

            cmp_logits(0)
            cmp_probs(0)
            for w in range(NT * 8 + 2):
                if 1 <= w < 33:
                    probs(w - 1)
                if w % 2 == 0 and w < 32:
                    rows(GA0 + w // 2)
                if w < 32:
                    maxima(w)
                if w < 28 and w % NT == 0:
                    cmp_logits(w // NT + 1)
                if w < 28 and w % NT == 1:
                    cmp_probs(w // NT + 1)
                if w >= 2 and (w - 2) % 8 == 7:
                    j = (w - 2) // 8
                    dve.wait_ge(n_o, w - 1)
                    yo.step(nc.vector.tensor_tensor(YN[:, j, :], BANK[6][:, :], NZ[:, j, :], ALU.mult))

            dve.wait_ge(row_used, used(70))
            with dve.Fori(0, KD // 2) as i:
                for c, per in ((fr, 4), (mg, 2)):
                    c.enter(i, per)
                for j in range(4):
                    k = i * 2 + j // 2
                    dve.wait_ge(gemm_done, i * 4 + (TILE0["ab"] + j + 1))
                    gate = (SGB if j % 2 else SGA)[:, bass.ds(k, 1), :]
                    fr.step(nc.vector.tensor_tensor(CV[:, j % 2:j % 2 + 1, :], BANK[(TILE0["ab"] + j) % 2][:, :].unsqueeze(1), gate, ALU.mult))
                    if j % 2:
                        mg.step(nc.vector.tensor_tensor(MG[:, bass.ds(k, 1), :], CV[:, 0:1, :], CV[:, 1:2, :], ALU.add))
                for c in (fr, mg):
                    c.leave(KD // 2)
            add_dve(dve, "w_out2", 5, "final", hr, fr, rs)
            for k in range(KD):
                nc.vector.tensor_tensor(H[:, k, :], H[:, k, :], RS[:, :], ALU.mult).then_inc(out_ready, 1)

        COUNT0 = {"conv0": (24, 40), "conv1": (46, 62)}
        H_READY = {1: 16, 2: 32, 3: 40, 4: 48, 5: 56}

        def finish(sp):
            for k in range(KD):
                sp.wait_ge(out_ready, k + 1)
                sp.dma_start(out[:, k, :], H[:, k, :]).then_inc(stored, 16)
            sp.wait_ge(stored, 16 * KD)

        def rest_pe(pe):
            def ynorm(pe, k, j):
                if j == 0:
                    pe.wait_ge(yn_ready, k + 1)
                return YB[:, k, :]
            add_pe(pe, "out_w", ynorm, 8)
            ffn_pe(pe, 0)
            attention_pe(pe)
            ffn_pe(pe, 1)
            second_pe(pe)


        def rest_act(act):
            add_act(act, "out_w", 1)
            ffn_act(act, 0)
            attention_act(act)
            ffn_act(act, 1)
            second_act(act)

        def rest_dve(dve, step, rs, hr, fr, cv):
            add_dve(dve, "out_w", 1, "ffn_ln0", hr, fr, rs)
            ffn_dve(dve, 0, "kv_ln", step, rs, hr, fr, cv, ("attn_ln", HQ))
            attention_dve(dve, step, rs, hr, fr, cv)
            ffn_dve(dve, 1, "norm2", step, rs, hr, fr, cv)
            second_dve(dve, step, rs, hr, fr, cv)

        @block.sync
        def _(sp):
            sp.dma_start(CST[:, :], A["const"]).then_inc(loaded, 16)
            sp.dma_start(PAR[:, :], A["param"]).then_inc(loaded, 16)
            sp.dma_start(X[:, :, :], A["xT"]).then_inc(loaded, 16)
            sp.dma_start(SMALL[:, :, :], A["small"]).then_inc(loaded, 16)

            def block_in(name, cells, per, i, j, when):
                slot = (BASE[name] + j) % SLOTS
                if when is not None:
                    which, count = when
                    sp.wait_ge(which, count)
                sp.dma_start(RING[:, slot, 0:cells * P], A[name][bass.ds(i + j, 1), :, :]
                             .rearrange("a p n -> (a p) n")).then_inc(w_ready[slot], 16)

            def last_use(b):
                for name, n, cells, per in STREAM:
                    if BASE[name] <= b < BASE[name] + n:
                        k = b - BASE[name]
                        if per == 1:
                            return gemm_done, TILE0[name] + k + 1
                        if k % 2 == 0:
                            return half_done, HALF0[name] + k // 2 + 1
                        return gemm_done, TILE0[name] + k // 2 + 1

            for name, n, cells, per in STREAM:
                for j in range(SLOTS):
                    b = BASE[name] + j
                    block_in(name, cells, per, 0, j, last_use(b - SLOTS) if b >= SLOTS else None)
                turns = n // SLOTS - 1
                if turns:
                    with sp.Fori(0, turns) as i:
                        for j in range(SLOTS):
                            if per == 1:
                                when = (gemm_done, i * SLOTS + (TILE0[name] + j + 1))
                            elif j % 2 == 0:
                                when = (half_done, i * (SLOTS // 2) + (HALF0[name] + j // 2 + 1))
                            else:
                                when = (gemm_done, i * (SLOTS // 2) + (TILE0[name] + j // 2 + 1))
                            block_in(name, cells, per, i * SLOTS, SLOTS + j, when)
                for j in range(SLOTS * (turns + 1), n):
                    block_in(name, cells, per, 0, j, last_use(BASE[name] + j - SLOTS))
            finish(sp)

        @block.gpsimd
        def _(pool):
            attention_pool(pool)
            second_pool(pool)

        @block.tensor
        def _(pe):
            pe.wait_ge(ones_set, 3)
            pe.wait_ge(loaded, 64)
            for k in range(KD):
                pe.wait_ge(h_ready, k + 1)
                mm = nc.tensor.matmul(BANK[6][0:32, :], SMALL[:, k, 0:32], H[:, k, :],
                                      start=(k == 0), stop=(k == KD - 1))
            mm.then_inc(dt_done, 1)
            norm_sums(pe, 0)

            def in_tile(g, j):
                gemm_tile(pe, "in_w", 0, GROUP_TILES * g + j, lambda k: H[:, k, :])

            for j in range(GROUP_TILES):
                in_tile(0, j)
            pe.wait_ge(dt_row, 10 + NT)
            for c in range(NT):
                nc.tensor.transpose(BANK[6][:, c * 64:c * 64 + 32], DTR[0:32, c * P:(c + 1) * P], IDENT[0:32, 0:32])
                mm = nc.tensor.transpose(BANK[6][:, c * 64 + 32:c * 64 + 64], CSR[0:32, c * P:(c + 1) * P], IDENT[0:32, 0:32])
            mm.then_inc(dtT_done, 1)

            def group_sums(g):
                pe.wait_ge(gsq_ready, g + 1)
                for k in range(GT):
                    mm = nc.tensor.matmul(BANK[7][:, :], ONES[:, :], SQ[:, k, :], start=(k == 0), stop=(k == GT - 1))
                mm.then_inc(gss_done, 1)

            for g in range(SSM_G):
                xb = XSB[g % 2]
                for c in range(NT):
                    u = NT * g + c
                    tok = slice(c * P, (c + 1) * P)
                    if c == 0:
                        pe.wait_ge(row_used, GROUP_TILES * (g + 1))
                        pe.wait_ge(dt_row, 12 + NT)
                    if u >= 1:
                        pe.wait_ge(d_ready, u)
                        pe.wait_ge(e_ready, 3 * u)
                    for h in range(SSM_HG):
                        nc.tensor.matmul(BANK[2 + h // 4][:, (h % 4) * P:(h % 4 + 1) * P],
                                         IDENT[0:32, SSM_HG * g + h:SSM_HG * g + h + 1].to_broadcast([32, P]),
                                         CSR[0:32, tok], start=True, stop=True)
                    nc.tensor.matmul(BANK[4][:, 0:P], xb[:, GT, tok], xb[:, GT + 1, tok], start=True, stop=True)
                    nc.tensor.transpose(BANK[4][:, P:2 * P], xb[:, GT, tok], IDENT)
                    for j in range(GT):
                        mm = nc.tensor.transpose(BANK[5][:, j * P:(j + 1) * P], xb[:, j, tok], IDENT)
                    mm.then_inc(p1_done, 1)
                    if g + 1 < SSM_G:
                        for j in range(sum(FILL[:c]), sum(FILL[:c + 1])):
                            in_tile(g + 1, j)
                    if c == 1 and g >= 1:
                        pe.wait_ge(s_ready, 3 * g + 1)
                        group_sums(g - 1)
                    pe.wait_ge(mce_ready, u + 1)
                    if u >= 1:
                        pe.wait_ge(y_read, u)
                    if c >= 1:
                        pe.wait_ge(s_ready, 3 * g + c)
                    for h in range(SSM_HG):
                        y = BANK[6][64 * (h % 2):64 * (h % 2) + 64, (h // 2) * P:(h // 2 + 1) * P]
                        mm = nc.tensor.matmul(y, XDT[u % 2][:, h, :], DEC[u % 2][:, h, :], start=True, stop=(c == 0))
                        if c >= 1:
                            mm = nc.tensor.matmul(y, STATE[:, h * 64:(h + 1) * 64], ECS[u % 2][:, h, :],
                                                  start=False, stop=True)
                    mm.then_inc(y_done, 1)
                    if c < NT - 1:
                        pe.wait_ge(xf_ready, 3 * g + c + 1)
                        if c >= 1:
                            pe.wait_ge(s_ready, 3 * g + c)
                        if c == 1 and g >= 1:
                            pe.wait_ge(gstd_ready, g)
                        nc.tensor.matmul(BANK[7][:, :], BTOK[u % 2], XF[u % 2].rearrange("p a b -> p (a b)"),
                                         start=True, stop=True).then_inc(st_done, 1)
            pe.wait_ge(s_ready, 3 * SSM_G)
            group_sums(SSM_G - 1)
            rest_pe(pe)

        @block.scalar
        def _(act):
            a_step = Count(act, act_step)
            act.wait_ge(loaded, 64)
            act.wait_ge(ones_set, 3)
            for k in range(KD):
                nc.scalar.activation(SQ[:, k, :], X[:, k, :], ACT.Square).then_inc(sq_ready, 1)
            norm_scale_act(act, 0)
            dt = Count(act, dt_act)
            dt.step(nc.scalar.activation(ALOG[0:32, :], par("a_log", parts=32), ACT.Exp))
            act.wait_ge(dt_row, 2)
            dt.step(nc.scalar.activation(DTB[0:32, :], DTA[0:32, :], ACT.Abs))
            dt.step(nc.scalar.activation(DTB[0:32, :], DTB[0:32, :], ACT.Exp, scale=-1.0))
            act.wait_ge(dt_row, 3)
            dt.step(nc.scalar.activation(STD[0:32, :], DTC[0:32, :], ACT.Ln))

            def rows(g, j):
                n = GROUP_TILES * g + j
                if j < GT:
                    act.wait_ge(gemm_free, n + 1)
                else:
                    act.wait_ge(conv_ready, (GT + 2) * g + j - GT + 1)
                if g >= 2 and j == 0:
                    act.wait_ge(yb_ready, NT * (g - 1))
                src, dst = (U[:, n % 2, 3:3 + T], ZS[g % 2][:, j, :]) if j < GT else \
                           (CV[:, n % 2, :], XSB[g % 2][:, j - GT, :])
                nc.scalar.activation(dst, src, ACT.Silu).then_inc(row_used, 1)

            for j in range(GROUP_TILES):
                rows(0, j)
            gsq = Count(act, gsq_ready)
            for g in range(SSM_G):
                for c in range(NT):
                    u = NT * g + c
                    act.wait_ge(p1_done, u + 1)
                    if u >= 2:
                        act.wait_ge(y_done, u - 1)
                        act.wait_ge(st_done, 3 * ((u - 2) // NT) + min((u - 2) % NT + 1, 3))
                    nc.scalar.activation(BTOK[u % 2], BANK[4][:, P:2 * P], ACT.Copy).then_inc(e_ready, 1)
                    for q in range(2):
                        nc.scalar.activation(ECS[u % 2][:, 4 * q:4 * q + 4, :],
                                             BANK[2 + q][:, :].rearrange("p (h t) -> p h t", t=P),
                                             ACT.Exp).then_inc(e_ready, 1)
                    act.wait_ge(d_ready, u + 1)
                    nc.scalar.activation(DEC[u % 2], DEC[u % 2], ACT.Exp).then_inc(d_exp, 1)
                    nc.scalar.activation(FX[u % 2], FX[u % 2], ACT.Exp).then_inc(d_exp, 1)
                    if g + 1 < SSM_G:
                        for j in range(sum(FILL[:c]), sum(FILL[:c + 1])):
                            rows(g + 1, j)
                    if c == 1 and g >= 1:
                        act.wait_ge(gss_done, g)
                        nc.scalar.activation(STD[:, :], BANK[7][:, :], ACT.Sqrt, bias=EPSC[:, 0:1],
                                             scale=1.0 / (GT * P)).then_inc(gstd_ready, 1)
                act.wait_ge(yb_ready, NT * (g + 1))
                nc.scalar.activation(SQ[:, 0:GT, :], YB[:, GT * g:GT * (g + 1), :], ACT.Square).then_inc(gsq_ready, 1)
            act.wait_ge(gss_done, SSM_G)
            nc.scalar.activation(STD[:, :], BANK[7][:, :], ACT.Sqrt, bias=EPSC[:, 0:1],
                                 scale=1.0 / (GT * P)).then_inc(gstd_ready, 1)
            rest_act(act)

        @block.vector
        def _(dve):
            step, rs, hr, fr = (Count(dve, s) for s in (dve_step, rs_ready, h_ready, gemm_free))
            nc.vector.memset(ONES[:, :], 1.0).then_inc(ones_set, 1)
            nc.vector.memset(EPSC[:, :], EPS).then_inc(ones_set, 1)
            nc.vector.memset(U[:, :, 0:3], 0.0).then_inc(ones_set, 1)
            dve.wait_ge(ones_set, 3)
            dve.wait_ge(loaded, 64)
            norm_head(dve, hr, "ssm_ln")
            norm_scale_dve(dve, 0, rs)
            r = Count(dve, dt_row)
            dve.wait_ge(dt_done, 1)
            r.step(nc.vector.tensor_tensor(DTA[0:32, :], BANK[6][0:32, :], RS[0:32, :], ALU.mult))
            r.step(nc.vector.tensor_scalar(DTA[0:32, :], DTA[0:32, :], par("dt_bias", parts=32), None, ALU.add))
            dve.wait_ge(dt_act, 3)
            r.step(nc.vector.tensor_scalar(DTC[0:32, :], DTB[0:32, :], 1.0, None, ALU.add))
            r.step(nc.vector.tensor_scalar(CSR[0:32, :], DTC[0:32, :], -1.0, None, ALU.add))
            r.step(nc.vector.tensor_tensor(DTB[0:32, :], DTB[0:32, :], CSR[0:32, :], ALU.subtract))
            r.step(nc.vector.tensor_scalar(DTA[0:32, :], DTA[0:32, :], 0.0, None, ALU.max))
            dve.wait_ge(dt_act, 4)
            r.step(nc.vector.tensor_tensor(DTB[0:32, :], DTB[0:32, :], STD[0:32, :], ALU.add))
            r.step(nc.vector.tensor_tensor(DTR[0:32, :], DTA[0:32, :], DTB[0:32, :], ALU.add))
            r.step(nc.vector.tensor_scalar(DTA[0:32, :], DTR[0:32, :], ALOG[0:32, 0:1], -1.0, ALU.mult, ALU.mult))
            r.step(nc.vector.memset(DTC[0:32, :], 1.0))
            for c in range(NT):
                tok = slice(c * P, (c + 1) * P)
                r.step(nc.vector.tensor_tensor_scan(CSR[0:32, tok], DTC[0:32, tok], DTA[0:32, tok], 0.0,
                                                    ALU.mult, ALU.add))

            cv = Count(dve, conv_ready)

            def rows(g, j):
                n = GROUP_TILES * g + j
                dve.wait_ge(gemm_done, n + 1)
                if n >= 2:
                    dve.wait_ge(row_used, n - 1)
                u = U[:, n % 2, :]
                fr.step(nc.vector.tensor_tensor(u[:, 3:3 + T], BANK[n % 2][:, :], RS[:, :], ALU.mult))
                if j >= GT:
                    conv(dve, step, cv, n % 2, lambda k: par("ssm_conv", 5 * ((GT + 2) * g + j - GT) + k), 4)

            for j in range(GROUP_TILES):
                rows(0, j)
            dve.wait_ge(dtT_done, 1)
            b6 = BANK[6][:, 0:NT * 64].rearrange("p (c w) -> p c w", w=64)
            tt = Count(dve, dt_row)
            tt.n = r.n
            tt.step(nc.vector.tensor_copy(DTT, b6[:, :, 0:32]))
            tt.step(nc.vector.tensor_copy(CSTK, b6[:, :, 32:64]))
            mce, xf, yr, yb, sr, dr, yn = (Count(dve, s) for s in (mce_ready, xf_ready, y_read, yb_ready, s_ready,
                                                                  d_ready, yn_ready))

            def group_norm(g):
                dve.wait_ge(gstd_ready, g + 1)
                rs.step(nc.vector.reciprocal(RSG[:, :], STD[:, :]))
                for k in range(GT * g, GT * (g + 1)):
                    yn.step(nc.vector.scalar_tensor_tensor(YB[:, k, :], YB[:, k, :], par("ssm_norm", k), RSG[:, :],
                                                           ALU.mult, ALU.mult))

            for g in range(SSM_G):
                xb = XSB[g % 2]
                heads = slice(SSM_HG * g, SSM_HG * (g + 1))
                for c in range(NT):
                    u = NT * g + c
                    tok = slice(c * P, (c + 1) * P)
                    xdt, x_f, dec, ecs, fx, etot = XDT[u % 2], XF[u % 2], DEC[u % 2], ECS[u % 2], FX[u % 2], ETOT[u % 2]
                    dve.wait_ge(p1_done, u + 1)
                    if u >= 2:
                        dve.wait_ge(y_done, u - 1)
                        dve.wait_ge(st_done, 3 * ((u - 2) // NT) + min((u - 2) % NT + 1, 3))
                    step.step(nc.vector.tensor_tensor(xdt, BANK[5][:, :].rearrange("p (h d) -> p h d", d=64),
                                                      DTT[:, c, heads].unsqueeze(2).to_broadcast([P, SSM_HG, 64]), ALU.mult))
                    dve.wait_ge(e_ready, 3 * u + 1)
                    step.step(nc.vector.tensor_tensor(CBM, BANK[4][:, 0:P], const("causal_st"), ALU.mult))
                    dve.wait_ge(e_ready, 3 * u + 3)
                    for q in range(2):
                        step.step(nc.vector.tensor_copy(etot[:, 4 * q:4 * q + 4], BANK[2 + q][:, P - 1:T:P]))
                    step.step(nc.vector.tensor_tensor(fx, etot, CSTK[:, c, heads], ALU.subtract))
                    for h in range(SSM_HG):
                        ins = nc.vector.tensor_scalar(dec[:, h, :], BANK[2 + h // 4][:, (h % 4) * P:(h % 4 + 1) * P],
                                                      CSTK[:, c, SSM_HG * g + h:SSM_HG * g + h + 1], 0.0,
                                                      ALU.subtract, ALU.min)
                    dr.step(ins)
                    dve.wait_ge(d_exp, 2 * u + 2)
                    step.step(nc.vector.tensor_tensor(dec, dec, CBM.unsqueeze(1).to_broadcast([P, SSM_HG, P]), ALU.mult))
                    step.step(nc.vector.tensor_copy(etot, ecs[:, :, P - 1]))
                    mce.step(nc.vector.tensor_tensor(ecs, ecs, xb[:, GT + 1, tok].unsqueeze(1).to_broadcast([P, SSM_HG, P]),
                                                     ALU.mult))
                    if c < NT - 1:
                        xf.step(nc.vector.tensor_tensor(x_f, xdt, fx.unsqueeze(2).to_broadcast([P, SSM_HG, 64]), ALU.mult))
                    if g + 1 < SSM_G:
                        for j in range(sum(FILL[:c]), sum(FILL[:c + 1])):
                            rows(g + 1, j)
                    step.step(nc.vector.tensor_tensor(TMPY, xb[:, 0:GT, tok],
                                                      par("ssm_d", GT * g, GT).unsqueeze(2).to_broadcast([P, GT, P]), ALU.mult))
                    dve.wait_ge(y_done, u + 1)
                    yr.step(nc.vector.tensor_tensor(TMPY, TMPY, BANK[6][:, :].rearrange("p (j t) -> p j t", t=P), ALU.add))
                    yb.step(nc.vector.tensor_tensor(YB[:, GT * g:GT * (g + 1), tok], TMPY, ZS[g % 2][:, :, tok], ALU.mult))
                    if c < NT - 1:
                        dve.wait_ge(st_done, 3 * g + c + 1)
                        st3 = STATE.rearrange("p (h d) -> p h d", d=64)
                        if c == 0:
                            sr.step(nc.vector.tensor_copy(STATE, BANK[7][:, :]))
                        else:
                            step.step(nc.vector.tensor_tensor(st3, st3, etot.unsqueeze(2).to_broadcast([P, SSM_HG, 64]), ALU.mult))
                            sr.step(nc.vector.tensor_tensor(STATE, STATE, BANK[7][:, :], ALU.add))
                    if c == 1 and g >= 1:
                        group_norm(g - 1)
            group_norm(SSM_G - 1)
            rest_dve(dve, step, rs, hr, fr, cv)


def _tiles(v):
    return np.asarray(v).reshape(-1, P).T


def _blocks(w, cells=8):
    k, n = w.shape
    b = w.reshape(k // (cells * P), cells, P, n // P, P).transpose(3, 0, 2, 1, 4)
    return np.ascontiguousarray(b).reshape(-1, P, cells * P)


def _constants():
    c = np.zeros((P, CONST[None]), np.float32)

    def put(name, v):
        a, n = CONST[name]
        c[:, a:a + n] = v.reshape(P, n)

    i = np.arange(P)
    put("ident", np.eye(P))
    put("half_ones", (i[:, None] // 64 == i[None, :] // 64) * 1.0)
    put("causal_st", (i[:, None] <= i[None, :]) * 1.0)
    put("future_neg", (i[None, :] > i[:, None]) * NEG)
    turn = np.zeros((P, P))
    freq = np.zeros(P)
    inv = np.power(np.float32(500000.0), -np.arange(8, dtype=np.float32) * np.float32(2.0 / 16)).astype(np.float32)
    for half in (0, 64):
        for d in range(8):
            turn[half + d + 8, half + d] = -1.0
            turn[half + d, half + d + 8] = 1.0
            freq[half + d] = freq[half + d + 8] = inv[d]
    put("rope_turn", turn)
    put("rope_freq", freq)
    t = np.arange(T).reshape(NT, P)
    seen = (np.arange(NCMP)[None, None, :] * 16 + 31 <= t.T[:, :, None]) * 1.0
    put("cmp_seen", seen)
    put("cmp_neg", (1.0 - seen) * NEG)
    return c


def _bucket_rows():
    n = np.maximum(T - 1 - np.arange(640), 0)
    nf = np.maximum(n, 1).astype(np.float32)
    large = 16 + (np.log(nf / np.float32(16)).astype(np.float32) / np.float32(math.log(8.0)) * np.float32(16)).astype(np.int32)
    bucket = np.where(n < 16, n, np.minimum(large, 31))
    rows = np.zeros((33, 640), np.float32)
    rows[bucket, np.arange(640)] = 1.0
    rows[32] = np.where(T - 1 - np.arange(640) < 0, NEG, 0.0)
    return rows


def _arrays(d):
    d = {k: np.asarray(v) for k, v in d.items()}
    f32 = np.float32
    par = np.zeros((P, PARAM[None]), f32)

    def put(name, v):
        a, n = PARAM[name]
        par[:v.shape[0], a:a + n] = v.reshape(v.shape[0], n)

    def conv(w, b, order):
        v = np.concatenate([w, b[None]], 0)[:, order]
        return v.reshape(v.shape[0], -1, P).transpose(2, 1, 0)

    for name, v in (("ssm_ln", d["ssm_ln_g"][0]), ("kv_ln", d["kv_ln_g"]), ("attn_ln", d["attn_ln_g"][0]),
                    ("ffn_ln0", d["ffn_ln_g"][0]), ("ffn_ln1", d["ffn_ln_g"][1]), ("norm2", d["norm_g_2"][0]),
                    ("final", d["final_norm_g_2"]), ("ssm_d", np.repeat(d["ssm_d"][0], 64)),
                    ("ssm_norm", d["ssm_norm_g"][0]), ("k_norm", np.tile(d["k_norm_g"], 2)),
                    ("q_norm", np.tile(d["q_norm_g"][0], 2)), ("subln", d["subln_g"][0]),
                    ("mh_norm", d["mh_norm_g_2"][0])):
        put(name, _tiles(v))
    z0, x0, b0, c0 = 0, 2048, 4096, 4608
    groups = [np.concatenate([z0 + 512 * g + np.arange(512), x0 + 512 * g + np.arange(512),
                              b0 + 128 * g + np.arange(128), c0 + 128 * g + np.arange(128)]) for g in range(4)]
    put("ssm_conv", conv(d["ssm_conv_w"][0], d["ssm_conv_b"][0], np.concatenate([g[512:] - 2048 for g in groups])))
    ffo = (np.arange(22)[:, None, None] * P + np.arange(2)[None, :, None] * 2816 + np.arange(P)).reshape(-1)
    for i in range(2):
        put(f"ffn_conv{i}", conv(d["ffn_conv_w"][i], d["ffn_conv_b"][i], ffo))
    put("qk_conv", np.concatenate([conv(d["conv_q_w_2"][0], d["conv_q_b_2"][0], np.arange(1024)),
                                   conv(d["conv_k_w_2"][0], d["conv_k_b_2"][0], np.arange(1024))], 1))
    gate = np.zeros((P, 1), f32)
    gate[0:4, 0] = d["b_igate_2"][0]
    gate[32:36, 0] = d["b_fgate_2"][0]
    gate[64:88, 0] = d["b_nsa_gate_2"][0]
    put("gate_bias", gate)
    put("dt_bias", d["ssm_dt_bias"][0][:, None])
    put("a_log", d["ssm_a_log"][0][:, None])
    put("cmp_pos", np.tile(np.concatenate([d["cmp_pos_k_2"][0].T, d["cmp_pos_v_2"][0].T], 1), (2, 1)))
    put("lam", np.tile(d["lam_vecs"][0].reshape(1, 256), (P, 1)))

    w2 = d["w_in_2"][0]
    small = np.zeros((1024, 120), f32)
    small[:, 0:32] = d["ssm_in_w"][0][:, 5120:5152]
    small[:, 32:36] = w2[:, 5120:5124]
    small[:, 64:68] = w2[:, 5124:5128]
    nq, nz, ng = 5128, 5128 + 512 + 768 + 24, 5128 + 512 + 768
    small[:, 96:120] = w2[:, ng:ng + 24]
    kc, vc, ks, vs, kw, vw = (5640 + 128 * i + np.arange(128) for i in range(6))
    pair = np.concatenate([np.concatenate([64 * j + np.arange(64), 64 * (j + 4) + np.arange(64)]) for j in range(4)])
    m = [np.arange(1024) + 1024 * i for i in range(5)]
    ga = nz + 512 + np.arange(1024)
    head = [np.concatenate([x[256 * h:256 * h + 256] for x in m]) for h in range(4)]
    order = np.concatenate(head + [nq + pair, kc, vc, ks, kw, vs, vw, nz + pair, ga, ga + 1024])
    kvw = d["kv_w"]
    kvq = np.concatenate([np.concatenate([kvw[:, 128 * h:128 * h + 128], kvw[:, 1024 + 128 * h:1152 + 128 * h],
                                          d["q_w"][0][:, 128 * h:128 * h + 128]], 1) for h in range(8)], 1)
    wa, wb = _blocks(d["w_branch_a_2"][0]), _blocks(d["w_branch_b_2"][0][pair], 4)
    ab = np.zeros((16, P, 8 * P), f32)
    ab[0::2], ab[1::2, :, 0:4 * P] = wa, wb
    return {
        "const": _constants(), "param": par, "bucket": _bucket_rows(),
        "rel": np.concatenate([d["rel_bias"], np.ones((1, 8), f32)], 0),
        "pos": np.broadcast_to(d["positions_2"].reshape(1, T), (P, T)),
        "xT": d["x"][0].T.reshape(KD, P, T).transpose(1, 0, 2),
        "small": small.reshape(KD, P, 120).transpose(1, 0, 2),
        "in_w": _blocks(d["ssm_in_w"][0][:, np.concatenate(groups)]), "out_w": _blocks(d["ssm_out_w"][0]),
        "up0": _blocks(d["ffn_up_w"][0][:, ffo]), "down0": _blocks(d["ffn_down_w"][0], 11),
        "kvq": _blocks(kvq), "attn_out": _blocks(d["attn_out_w"][0]),
        "up1": _blocks(d["ffn_up_w"][1][:, ffo]), "down1": _blocks(d["ffn_down_w"][1], 11),
        "w_in2": _blocks(w2[:, order]), "ab": ab, "w_out2": _blocks(d["w_out_2"][0]),
        "cmp_w1": np.stack([np.tile(d[f"cmp_w1_{x}_2"][0].reshape(CMPL, 64, P).transpose(1, 0, 2), (2, 1, 1))
                            for x in "kv"], 0),
        "cmp_w2": np.concatenate([d["cmp_w2_k_2"][0], d["cmp_w2_v_2"][0]], 1),
    }


def kernel(**inputs):
    import concourse.bacc as bacc
    from concourse.bass_utils import run_bass_kernel_spmd

    nc = bacc.Bacc("TRN2", target_bir_lowering=False, num_devices=1)
    arrays = {f"{k}_dram": np.ascontiguousarray(v) for k, v in _arrays(inputs).items()}
    aps = {k[:-5]: nc.dram_tensor(k, v.shape, mybir.dt.from_np(v.dtype), kind="ExternalInput").ap()
           for k, v in arrays.items()}
    out = nc.dram_tensor("out_dram", (P, KD, T), F32, kind="ExternalOutput").ap()
    three_parts(nc, aps, out)
    r = run_bass_kernel_spmd(nc, [arrays], core_ids=[0])
    return r.results[0]["out_dram"].transpose(1, 0, 2).reshape(1, DM, T).transpose(0, 2, 1)
```

```python
import concourse.bass as bass
from concourse import mybir
from contextlib import ExitStack
import numpy as np
import math

F32 = mybir.dt.float32
F32R = mybir.dt.float32r
ACT = mybir.ActivationFunctionType
ALU = mybir.AluOpType
AX = mybir.AxisListType

T = 512
P = 128
NT = T // P
DM = 1024
KD = DM // P
SSM_G, SSM_HG = 4, 8
SSM_H = SSM_G * SSM_HG
GT = 4
GROUP_TILES = 2 * GT + 2
FF_TILES = 22
AH = 8
MH = 4
NP_ = 4
NCMP = (T - 32) // 16 + 1
CMPL = 32
EPS = 1e-6
NEG = -1e30
LAM_INIT = 0.8 - 0.6 * math.exp(-0.3)
TURN = 4
SLOTS = 2
CELLS = 11


def layout(spec):
    at, out = 0, {}
    for name, n in spec:
        out[name] = (at, n)
        at += n
    out[None] = at
    return out


CONST = layout([("ident", P), ("half_ones", P), ("causal_st", P), ("future_neg", P), ("rope_turn", P),
                ("rope_freq", 1), ("cmp_seen", NT * NCMP), ("cmp_neg", NT * NCMP)])
PARAM = layout([("ssm_ln", KD), ("kv_ln", KD), ("attn_ln", KD), ("ffn_ln0", KD), ("ffn_ln1", KD),
                ("norm2", KD), ("final", KD), ("ssm_d", 16), ("ssm_norm", 16), ("k_norm", 1),
                ("q_norm", 1), ("subln", 1), ("mh_norm", 8), ("ssm_conv", 24 * 5),
                ("ffn_conv0", 44 * 4), ("ffn_conv1", 44 * 4), ("qk_conv", 16 * 5),
                ("gate_bias", 1), ("dt_bias", 1), ("a_log", 1), ("cmp_pos", 2 * CMPL), ("lam", 256)])


class Count:

    def __init__(self, eng, sem):
        self.eng, self.sem, self.n, self.k = eng, sem, 0, 0

    def step(self, ins):
        ins.then_inc(self.sem, 1)
        self.n = self.n + 1
        self.k += 1
        self.eng.wait_ge(self.sem, self.n)

    def enter(self, i, per):
        self.base, self.per, self.k = self.n, per, 0
        self.n = i * per + self.base

    def leave(self, turns):
        assert self.k == self.per, (self.k, self.per)
        self.n = self.base + turns * self.per


def three_parts(nc, A, out):
    ctx = ExitStack()
    with ctx:
        def sb(name, shape, dt=F32):
            return ctx.enter_context(nc.sbuf_tensor(name, shape, dt))

        def sem(name):
            return ctx.enter_context(nc.semaphore(name))

        X = sb("residual", [P, KD, T])
        HH = sb("scaled_in_high", [P, KD, T], F32R)
        HL = sb("scaled_in_low", [P, KD, T], F32R)
        RAW = sb("weight_ring", [P, SLOTS, CELLS * P])
        WH = sb("weights_high", [P, SLOTS, CELLS * P], F32R)
        WL = sb("weights_low", [P, SLOTS, CELLS * P], F32R)
        SQ = sb("squares", [P, 2, T])
        ACC = sb("square_sums", [P, T])
        RS = sb("inv_rms", [P, T])
        STD = sb("rms", [P, T])
        CST = sb("constants", [P, CONST[None]])
        PAR = sb("params", [P, PARAM[None]])
        ONES = sb("ones", [P, P])
        SMALL = sb("small_weights", [P, KD, 32 + 88])
        EPSC = sb("eps_column", [P, 1])
        U = sb("padded_rows", [P, 2, T + 4])
        CV = sb("conv_rows", [P, 2, T])
        EMB = sb("floor", [P, T])
        RDB = sb("reciprocals", [P, T])
        AREA = 23860
        with ExitStack() as plain:
            ARENA = plain.enter_context(nc.sbuf_tensor("arena", [P, AREA], F32))
        with ExitStack() as ffn_parts:
            FFH = ffn_parts.enter_context(nc.sbuf_tensor("gated_high", [P, FF_TILES, T], F32R))
            FFL = ffn_parts.enter_context(nc.sbuf_tensor("gated_low", [P, FF_TILES, T], F32R))
        with ExitStack() as query_parts:
            HQH = query_parts.enter_context(nc.sbuf_tensor("query_in_high", [P, KD, T], F32R))
            HQL = query_parts.enter_context(nc.sbuf_tensor("query_in_low", [P, KD, T], F32R))
        BANK = [ctx.enter_context(nc.psum_tensor(f"bank{i}", [P, T], F32)) for i in range(8)]

        def const(name, parts=P):
            a, n = CONST[name]
            return CST[0:parts, a:a + n]

        def par(name, i=0, n=1, parts=P):
            a, _ = PARAM[name]
            return PAR[0:parts, a + i:a + i + n]

        class Carve:

            def __init__(self):
                self.at = 0

            def __call__(self, *shape):
                n = int(np.prod(shape))
                v = ARENA[:, self.at:self.at + n]
                self.at += n
                assert self.at <= AREA, self.at
                if len(shape) == 2:
                    v = v.rearrange("p (a b) -> p a b", b=shape[1])
                if len(shape) == 3:
                    v = v.rearrange("p (a b c) -> p a b c", b=shape[1], c=shape[2])
                return v

        IDENT = const("ident")

        loaded = sem("loaded")
        w_ready = [sem(f"weights_in_slot{i}") for i in range(SLOTS)]
        high_ready = sem("weights_high_ready")
        split_done = sem("weights_split")
        acc_ready = sem("square_sums_ready")
        gemm_done = sem("gemm_tile_done")
        half_done = sem("first_block_used")
        gemm_free = sem("gemm_bank_read")
        ones_set = sem("ones_set")
        h_ready = sem("scaled_in_ready")
        ff_ready = sem("gated_ready")
        sq_ready = sem("squares_ready")
        ssq_done = sem("square_sum_done")
        std_ready = sem("rms_ready")
        rs_ready = sem("inv_rms_ready")
        row_used = sem("tile_rows_used")
        conv_ready = sem("tile_rows_ready")
        dve_step = sem("dve_step")
        act_step = sem("act_step")
        dt_done = sem("dt_product_done")
        dt_row = sem("dt_rows_step")
        dt_act = sem("dt_act_step")
        dtT_done = sem("dt_turned")
        p1_done = sem("ssd_inputs_done")
        e_ready = sem("ssd_exps_of_sums")
        d_ready = sem("ssd_exponents_ready")
        d_exp = sem("ssd_decay_ready")
        mce_ready = sem("ssd_operands_ready")
        xf_ready = sem("ssd_state_input_ready")
        y_done = sem("ssd_y_done")
        st_done = sem("ssd_state_done")
        y_read = sem("ssd_y_read")
        s_ready = sem("ssd_state_ready")
        yb_ready = sem("ssd_y_ready")
        gsq_ready = sem("group_squares_ready")
        usum_done = sem("unit_square_sum_done")
        gs_read = sem("unit_square_sum_read")
        aux_in = sem("bucket_rows_in")
        brow_done = sem("bias_row_done")
        brow_ready = sem("bias_row_ready")
        brow_out = sem("bias_rows_in_dram")
        DSCR = nc.dram_tensor("bias_scratch", (AH, P, 640), F32, kind="Internal").ap()
        gstd_ready = sem("group_rms_ready")
        yn_ready = sem("normed_y_ready")

        block = ctx.enter_context(nc.Block())

        STREAM = [("in_w", 40, 8, 1, True), ("out_w", 16, 8, 2, False), ("up0", 44, 8, 1, True), ("down0", 16, 11, 2, True),
                  ("kvq", 24, 8, 1, True), ("attn_out", 8, 8, 1, False), ("up1", 44, 8, 1, True), ("down1", 16, 11, 2, True),
                  ("w_in2", 70, 8, 1, True), ("ab", 16, 8, 1, False), ("w_out2", 8, 8, 1, False)]
        BASE, TILE0, HALF0, PART0 = {}, {}, {}, {}
        b = t = h = q = 0
        for name, n, cells, per, parts in STREAM:
            BASE[name], TILE0[name], HALF0[name], PART0[name] = b, t, h, q
            b, t, h, q = b + n, t + n // per, h + (n // 2 if per == 2 else 0), q + (n if parts else 0)
        PARTED = {x[0]: x[4] for x in STREAM}

        def products_done(name, per, k, i=0):
            if per == 1:
                return gemm_done, TILE0[name] + k + 1 + i * TURN
            if k % 2 == 0:
                return half_done, HALF0[name] + k // 2 + 1 + i * (TURN // 2)
            return gemm_done, TILE0[name] + k // 2 + 1 + i * (TURN // 2)

        def loaded_used(name, per, k, i=0):
            if PARTED[name]:
                return split_done, PART0[name] + k + 1 + i * TURN
            return products_done(name, per, k, i)

        def gemm_tile(pe, name, i, j, rhs, cells=8, per=1):
            turn = TURN // per
            n = TILE0[name] + j + i * turn
            bank = BANK[(TILE0[name] + j) % 2][:, :]
            if TILE0[name] + j >= 2:
                pe.wait_ge(gemm_free, n - 1)
            for part in range(per):
                k0 = per * j + part
                slot = k0 % SLOTS
                if PARTED[name]:
                    pe.wait_ge(split_done, PART0[name] + k0 + 1 + i * TURN)
                else:
                    pe.wait_ge(w_ready[slot], (BASE[name] + k0) // SLOTS * 16 + 16 + i * (16 * TURN // SLOTS))
                for c in range(cells):
                    k = part * cells + c
                    first, last = k == 0, k == per * cells - 1
                    cell = slice(c * P, (c + 1) * P)
                    if PARTED[name]:
                        high, low = rhs(k)
                        nc.tensor.matmul(bank, WH[:, slot, cell], high, start=first, stop=False)
                        nc.tensor.matmul(bank, WH[:, slot, cell], low, start=False, stop=False)
                        mm = nc.tensor.matmul(bank, WL[:, slot, cell], high, start=False, stop=last)
                    else:
                        mm = nc.tensor.matmul(bank, RAW[:, slot, cell], rhs(k), start=first, stop=last)
                if part < per - 1:
                    mm.then_inc(half_done, 1)
            mm.then_inc(gemm_done, 1)

        def small_product(pe, out_rows, cols):
            for k in range(KD):
                for part in (HH, HL):
                    mm = nc.tensor.matmul(out_rows, SMALL[:, k, cols], part[:, k, :].bitcast(F32),
                                          start=(k == 0 and part is HH), stop=(k == KD - 1 and part is HL))
            return mm

        def norm_sum(pe, turn):
            pe.wait_ge(acc_ready, (KD + 1) * (turn + 1))
            nc.tensor.matmul(BANK[7][:, :], ONES[:, :], ACC[:, :], start=True, stop=True).then_inc(ssq_done, 1)

        def split_scaled(hr, high, low, x, gain):
            hr.step(nc.vector.tensor_scalar(high, x, gain, None, ALU.mult))
            hr.step(nc.vector.scalar_tensor_tensor(low, x, gain, high.bitcast(F32), ALU.mult, ALU.subtract))

        def add_squares(dve, ac, turn, k, sq):
            dve.wait_ge(sq_ready, k + (KD * turn + 1))
            ac.step(nc.vector.tensor_tensor(ACC[:, :].unsqueeze(1), ACC[:, :].unsqueeze(1), sq, ALU.add))

        def norm_scale_act(act, turn):
            act.wait_ge(ssq_done, turn + 1)
            nc.scalar.activation(STD[:, :], BANK[7][:, :], ACT.Sqrt, bias=EPSC[:, 0:1],
                                 scale=1.0 / DM).then_inc(std_ready, 1)

        def norm_scale_dve(dve, turn, rs):
            dve.wait_ge(std_ready, turn + 1)
            rs.step(nc.vector.reciprocal(RS[:, :], STD[:, :]))

        def conv(dve, step, done, b, taps_and_bias, taps, out=None):
            u, y = U[:, b, :], CV[:, b, :] if out is None else out
            step.step(nc.vector.tensor_scalar(y, u[:, 3:3 + T], taps_and_bias(taps - 1), taps_and_bias(taps),
                                              ALU.mult, ALU.add))
            for k in range(taps - 1):
                at = 3 - (taps - 1) + k
                (done if k == taps - 2 else step).step(nc.vector.scalar_tensor_tensor(
                    y, u[:, at:at + T], taps_and_bias(k), y, ALU.mult, ALU.add))

        mb = Carve()
        YB = mb(4 * GT, T)
        ZS = [mb(GT, T) for _ in range(2)]
        XSB = [mb(GT + 2, T) for _ in range(2)]
        XDT = mb(SSM_HG, 64)
        XF = mb(SSM_HG, 64)
        DEC = mb(SSM_HG, P)
        ECS = mb(SSM_HG, P)
        CBM = mb(P)
        BTOK = mb(P)
        FX = mb(SSM_HG)
        ETOT = mb(SSM_HG)
        STATE = EMB[:, :]
        RSG = RDB[:, :]
        TMPY = ACC[:, :].rearrange("p (j t) -> p j t", t=P)
        YSQ = SQ[:, 0, :].rearrange("p (j t) -> p j t", t=P)
        GSS = SQ[:, 1, :]
        DTR = mb(T)
        CSR = mb(T)
        DTA, DTB, DTC = (YB[:, i, :] for i in range(3))
        ALOG = mb(1)
        DTT = mb(NT, 32)
        CSTK = mb(NT, 32)
        UNITS = SSM_G * NT
        FILL = [3, 2, 3, 2]

        bb = Carve()
        bb.at = 3 * T
        BROW = bb(AH, 640)
        BUCK = bb(640)
        REL = bb(AH)

        def norm_head(dve, count_h, gains):
            ac = Count(dve, acc_ready)
            ac.step(nc.vector.memset(ACC[:, :], 0.0))
            for k in range(KD):
                split_scaled(count_h, HH[:, k, :], HL[:, k, :], X[:, k, :], par(gains, k))
                add_squares(dve, ac, 0, k, SQ[:, k % 2:k % 2 + 1, :])


        def add_pe(pe, name, rhs, cells, ready=None):
            per = 2 if name not in ("attn_out", "w_out2") else 1
            turn = TURN // per
            with pe.Fori(0, KD // turn) as i:
                for j in range(turn):
                    gemm_tile(pe, name, i, j, lambda k: rhs(pe, k, j), cells, per)

        def add_act(act, name, turn):
            with act.Fori(0, KD // 2) as i:
                for j in range(2):
                    act.wait_ge(gemm_free, i * 2 + (TILE0[name] + j + 1))
                    act.wait_ge(acc_ready, i * 2 + ((KD + 1) * turn + j))
                    nc.scalar.activation(SQ[:, j:j + 1, :], X[:, bass.ds(i * 2 + j, 1), :], ACT.Square).then_inc(sq_ready, 1)
            norm_scale_act(act, turn)

        def add_dve(dve, name, turn, gains, hr, fr, rs):
            ac = Count(dve, acc_ready)
            ac.n = (KD + 1) * turn
            ac.step(nc.vector.memset(ACC[:, :], 0.0))
            with dve.Fori(0, KD // 2) as i:
                fr.enter(i, 2)
                hr.enter(i, 4)
                ac.enter(i, 2)
                for j in range(2):
                    k = i * 2 + j
                    dve.wait_ge(gemm_done, i * 2 + (TILE0[name] + j + 1))
                    x = X[:, bass.ds(k, 1), :]
                    fr.step(nc.vector.tensor_tensor(x, x, BANK[(TILE0[name] + j) % 2][:, :].unsqueeze(1), ALU.add))
                    a, _ = PARAM[gains]
                    split_scaled(hr, HH[:, bass.ds(k, 1), :], HL[:, bass.ds(k, 1), :], x, PAR[:, bass.ds(k + a, 1)])
                    add_squares(dve, ac, turn, k, SQ[:, j:j + 1, :])
                fr.leave(KD // 2)
                hr.leave(KD // 2)
                ac.leave(KD // 2)
            norm_scale_dve(dve, turn, rs)

        ff = Carve()
        ff.at = FF_TILES * T * 2
        GATE = ff(T)

        def ffn_pe(pe, layer):
            norm_sum(pe, 2 * layer + 1)
            pe.wait_ge(h_ready, H_READY[2 * layer + 1])
            with pe.Fori(0, 2 * FF_TILES // TURN) as i:
                for j in range(TURN):
                    gemm_tile(pe, f"up{layer}", i, j, lambda k: (HH[:, k, :], HL[:, k, :]))

            def gated(pe, k, j):
                if j == 0 and (k == 0 or k >= FF_TILES - 3):
                    pe.wait_ge(ff_ready, 2 * (FF_TILES * layer + max(k + 1, FF_TILES - 3)))
                return FFH[:, k, :], FFL[:, k, :]
            add_pe(pe, f"down{layer}", gated, 11)

        def ffn_act(act, layer):
            c0, _ = COUNT0[f"conv{layer}"]
            with act.Fori(0, FF_TILES) as m:
                act.wait_ge(conv_ready, m + (c0 + 1))
                nc.scalar.activation(GATE, CV[:, 0, :], ACT.Silu).then_inc(row_used, 1)
            add_act(act, f"down{layer}", 2 * layer + 2)

        def ffn_dve(dve, layer, gains, step, rs, hr, fr, cv):
            name = f"up{layer}"
            _, r0 = COUNT0[f"conv{layer}"]
            ffr = Count(dve, ff_ready)
            ffr.n = 2 * FF_TILES * layer
            a, _ = PARAM[f"ffn_conv{layer}"]
            with dve.Fori(0, FF_TILES // 2) as i:
                for c, per in ((fr, 4), (step, 12), (cv, 2), (ffr, 4)):
                    c.enter(i, per)
                for j in range(4):
                    b = j % 2
                    dve.wait_ge(gemm_done, i * 4 + (TILE0[name] + j + 1))
                    if b == 0:
                        dve.wait_ge(row_used, i * 2 + (r0 + j // 2))
                    fr.step(nc.vector.tensor_tensor(U[:, b, 3:3 + T], BANK[(TILE0[name] + j) % 2][:, :], RS[:, :], ALU.mult))
                    conv(dve, step, cv if b == 0 else step, b,
                         lambda k: PAR[:, bass.ds(i * 16 + (a + 4 * j + k), 1)], 3)
                    if b == 1:
                        dve.wait_ge(row_used, i * 2 + (r0 + j // 2 + 1))
                        product = CV[:, 1:2, :]
                        high, low = (f[:, bass.ds(i * 2 + j // 2, 1), :] for f in (FFH, FFL))
                        step.step(nc.vector.tensor_tensor(product, product, GATE.unsqueeze(1), ALU.mult))
                        ffr.step(nc.vector.tensor_copy(high, product))
                        ffr.step(nc.vector.tensor_tensor(low, product, high.bitcast(F32), ALU.subtract))
                for c in (fr, step, cv, ffr):
                    c.leave(FF_TILES // 2)
            add_dve(dve, f"down{layer}", 2 * layer + 2, gains, hr, fr, rs)

        at = Carve()
        at.at = 2 * KD * T
        BIAS = at(AH, T)
        OH = at(AH, T)
        KN = [at(T) for _ in range(2)]
        QN = [at(T) for _ in range(2)]
        VT = [at(NT, P) for _ in range(2)]
        PR = [[at(T) for _ in range(2)] for _ in range(2)]
        ATT = [at(T) for _ in range(2)]
        OB = at(T)
        RH, OSTD = RDB[:, :], EMB[:, :]
        SQO = ACC[:, :]
        NM = [at(2) for _ in range(2)]
        SUMS = [at(2) for _ in range(2)]
        LAM = at(72)

        bias_in = sem("bias_table_in")
        hq_ready = sem("query_in_ready")
        lam_step = sem("lambda_step")
        lam_exp = sem("lambda_exps")
        lam_act = sem("lambda_act_step")
        hsq = sem("head_squares_ready")
        hss = sem("head_square_sum_done")
        hstd = sem("head_rms_ready")
        kq_ready = sem("head_kq_ready")
        vt_done = sem("v_turned")
        v_ready = sem("v_ready")
        s_done = sem("scores_done")
        l_ready = sem("logits_ready")
        p_ready = sem("exps_ready")
        a_ready = sem("attn_ready")
        t_done = sem("attn_turned")
        t_ready = sem("attn_turned_ready")
        o_done = sem("attn_out_done")
        ob_ready = sem("head_out_ready")
        oss_done = sem("head_out_square_sum")
        ostd_ready = sem("head_out_rms")
        oh_ready = sem("head_out_normed")

        def attention_pe(pe):
            norm_sum(pe, 2)
            pe.wait_ge(h_ready, H_READY[2])

            def tile(h, j):
                if j == 2:
                    pe.wait_ge(hq_ready, 2 * KD)
                high, low = (HQH, HQL) if j == 2 else (HH, HL)
                gemm_tile(pe, "kvq", 0, 3 * h + j, lambda k: (high[:, k, :], low[:, k, :]))

            def head_sums(h, which):
                if which == 1:
                    pe.wait_ge(v_ready, h + 1)
                elif h >= 1:
                    pe.wait_ge(hstd, 2 * h)
                pe.wait_ge(hsq, 2 * h + which + 1)
                nc.tensor.matmul(BANK[6][:, :], const("half_ones"), SQ[:, which, :], start=True, stop=True).then_inc(hss, 1)

            def turn_v(h):
                pe.wait_ge(hstd, 2 * h + 1)
                pe.wait_ge(gemm_free, TILE0["kvq"] + 3 * h + 2)
                for c in range(NT):
                    mm = nc.tensor.transpose(BANK[6][:, c * P:(c + 1) * P], U[:, 1, 3 + c * P:3 + (c + 1) * P], IDENT)
                mm.then_inc(vt_done, 1)

            def scores(h, i):
                w = NT * h + i
                if w >= 1:
                    pe.wait_ge(l_ready, w)
                pe.wait_ge(kq_ready, 2 * h + 2)
                n = (i + 1) * P
                for c in range(2):
                    mm = nc.tensor.matmul(BANK[2 + c][:, 0:n], QN[h % 2][64 * c:64 * c + 64, i * P:(i + 1) * P],
                                          KN[h % 2][64 * c:64 * c + 64, 0:n], start=True, stop=True)
                mm.then_inc(s_done, 1)

            def turn_attn(h, i):
                w = NT * h + i
                pe.wait_ge(a_ready, w + 1)
                if w >= 1:
                    pe.wait_ge(t_ready, w)
                for kb in range(i + 1):
                    mm = nc.tensor.transpose(BANK[4][:, kb * P:(kb + 1) * P], PR[w % 2][0][:, kb * P:(kb + 1) * P], IDENT)
                mm.then_inc(t_done, 1)

            def attn_v(h, i):
                w = NT * h + i
                pe.wait_ge(t_ready, w + 1)
                pe.wait_ge(v_ready, h + 1)
                if i == 0 and h >= 1:
                    pe.wait_ge(ob_ready, 2 * h)
                for kb in range(i + 1):
                    mm = nc.tensor.matmul(BANK[5][:, i * P:(i + 1) * P], VT[h % 2][:, kb, :],
                                          ATT[w % 2][:, kb * P:(kb + 1) * P], start=(kb == 0), stop=(kb == i))
                mm.then_inc(o_done, 1)

            def out_sums(h):
                pe.wait_ge(ob_ready, 2 * h + 2)
                nc.tensor.matmul(BANK[7][:, :], ONES[:, :], SQO, start=True, stop=True).then_inc(oss_done, 1)

            for j in range(3):
                tile(0, j)
            head_sums(0, 0)
            turn_v(0)
            head_sums(0, 1)
            for h in range(AH + 1):
                for i in range(NT):
                    w = NT * h + i
                    if h + 1 < AH and i < 3:
                        tile(h + 1, i)
                    if h < AH:
                        scores(h, i)
                    if 1 <= w < NT * AH + 1:
                        turn_attn((w - 1) // NT, (w - 1) % NT)
                    if 2 <= w < NT * AH + 2:
                        attn_v((w - 2) // NT, (w - 2) % NT)
                    if h + 1 < AH:
                        if i == 1:
                            head_sums(h + 1, 0)
                        if i == 2:
                            turn_v(h + 1)
                        if i == 3:
                            head_sums(h + 1, 1)
                    if i == 2 and h >= 1:
                        out_sums(h - 1)

            def normed(pe, k, j):
                if j == 0:
                    pe.wait_ge(oh_ready, k + 1)
                return OH[:, k, :]
            add_pe(pe, "attn_out", normed, 8)

        def attention_act(act):
            la = Count(act, lam_act)
            act.wait_ge(lam_step, 4)
            la.step(nc.scalar.activation(LAM[:, 66:68], LAM[:, 64:66], ACT.Exp))
            act.wait_ge(gemm_free, TILE0["kvq"])
            skewed = bass.AP(tensor=DSCR.tensor, offset=P - 1, ap=[[639, P], [P * 640, AH], [1, T]])
            act.dma_start(BIAS, skewed).then_inc(bias_in, 16)

            def squares(h, which):
                act.wait_ge(gemm_free, TILE0["kvq"] + 3 * h + 1 + 2 * which)
                if h >= 1:
                    act.wait_ge(hss, 2 * h + which - 1)
                nc.scalar.activation(SQ[:, which, :], U[:, 0, 3:3 + T] if which == 0 else CV[:, 0, :],
                                     ACT.Square).then_inc(hsq, 1)

            def rms(h, which):
                act.wait_ge(hss, 2 * h + which + 1)
                if 2 * h + which >= 1:
                    act.wait_ge(kq_ready, 2 * h + which)
                nc.scalar.activation(STD[:, :], BANK[6][:, :], ACT.Sqrt, bias=EPSC[:, 0:1], scale=1.0 / 64).then_inc(hstd, 1)

            def v_out(h):
                act.wait_ge(vt_done, h + 1)
                if h >= 2:
                    act.wait_ge(o_done, NT * (h - 1))
                nc.scalar.activation(VT[h % 2], BANK[6][:, :].rearrange("p (c d) -> p c d", d=P), ACT.Copy).then_inc(v_ready, 1)

            def exps(h, i):
                w = NT * h + i
                act.wait_ge(l_ready, w + 1)
                n = (i + 1) * P
                for c in range(2):
                    p = PR[w % 2][c][:, 0:n]
                    nc.scalar.activation(p, p, ACT.Exp, bias=NM[w % 2][:, c:c + 1],
                                         accum_out=SUMS[w % 2][:, c:c + 1]).then_inc(p_ready, 1)

            def turned(h, i):
                w = NT * h + i
                act.wait_ge(t_done, w + 1)
                if w >= 2:
                    act.wait_ge(o_done, w - 1)
                nc.scalar.activation(ATT[w % 2][:, 0:(i + 1) * P], BANK[4][:, 0:(i + 1) * P], ACT.Copy).then_inc(t_ready, 1)

            def head_out(h):
                act.wait_ge(o_done, NT * (h + 1))
                if h >= 1:
                    act.wait_ge(oh_ready, h)
                nc.scalar.activation(OB, BANK[5][:, :], ACT.Copy).then_inc(ob_ready, 1)
                nc.scalar.activation(SQO, BANK[5][:, :], ACT.Square).then_inc(ob_ready, 1)

            def head_rms(h):
                act.wait_ge(oss_done, h + 1)
                nc.scalar.activation(OSTD, BANK[7][:, :], ACT.Sqrt, bias=EPSC[:, 0:1], scale=1.0 / P).then_inc(ostd_ready, 1)

            squares(0, 0)
            squares(0, 1)
            rms(0, 0)
            v_out(0)
            rms(0, 1)
            for h in range(AH + 1):
                for i in range(NT):
                    w = NT * h + i
                    if h + 1 < AH and i in (0, 2):
                        squares(h + 1, i // 2)
                    if 1 <= w < NT * AH + 1:
                        turned((w - 1) // NT, (w - 1) % NT)
                    if i == 1 and h >= 1:
                        head_out(h - 1)
                    if h < AH:
                        exps(h, i)
                    if h + 1 < AH:
                        if i == 1:
                            rms(h + 1, 0)
                        if i == 2:
                            v_out(h + 1)
                        if i == 3:
                            rms(h + 1, 1)
                    if i == 2 and h >= 1:
                        head_rms(h - 1)
            add_act(act, "attn_out", 3)

        def attention_dve(dve, step, rs, hr, fr, cv):
            ls, kq, lr, ar, ohr, hq = (Count(dve, s) for s in (lam_step, kq_ready, l_ready, a_ready, oh_ready, hq_ready))
            for m in range(2):
                ls.step(nc.vector.tensor_tensor(LAM[:, 0:64], par("lam", 128 * m, 64), par("lam", 128 * m + 64, 64), ALU.mult))
                ls.step(nc.vector.tensor_reduce(LAM[:, 64 + m:65 + m], LAM[:, 0:64], AX.X, ALU.add))
            dve.wait_ge(lam_act, 1)
            ls.step(nc.vector.tensor_tensor(LAM[:, 68:69], LAM[:, 67:68], LAM[:, 66:67], ALU.subtract))
            ls.step(nc.vector.tensor_scalar(LAM[:, 68:69], LAM[:, 68:69], -LAM_INIT, None, ALU.add))
            ls.step(nc.vector.tensor_scalar(LAM[:, 69:70], par("subln"), 1.0 - LAM_INIT, None, ALU.mult))

            def evac(h, j):
                dve.wait_ge(gemm_done, TILE0["kvq"] + 3 * h + j + 1)
                if j == 1 and h >= 1:
                    dve.wait_ge(vt_done, h)
                dst = (U[:, 0, 3:3 + T], U[:, 1, 3:3 + T], CV[:, 0, :])[j]
                fr.step(nc.vector.tensor_tensor(dst, BANK[(TILE0["kvq"] + 3 * h + j) % 2][:, :], RS[:, :], ALU.mult))

            def head_norm(h, which):
                dve.wait_ge(hstd, 2 * h + which + 1)
                step.step(nc.vector.reciprocal(RH, STD[:, :]))
                if h >= 2:
                    dve.wait_ge(s_done, NT * (h - 1))
                src, dst = ((U[:, 0, 3:3 + T], KN[h % 2]), (CV[:, 0, :], QN[h % 2]))[which]
                kq.step(nc.vector.scalar_tensor_tensor(dst, src, par("q_norm" if which else "k_norm"), RH, ALU.mult, ALU.mult))

            def logits(h, i):
                w = NT * h + i
                n = (i + 1) * P
                if w == 0:
                    dve.wait_ge(bias_in, 16)
                dve.wait_ge(s_done, w + 1)
                if w >= 2:
                    dve.wait_ge(t_done, w - 1)
                for c in range(2):
                    p = PR[w % 2][c][:, 0:n]
                    step.step(nc.vector.scalar_tensor_tensor(p, BANK[2 + c][:, 0:n], 0.125, BIAS[:, h, T - n:T],
                                                             ALU.mult, ALU.add))
                    red = nc.vector.tensor_reduce(NM[w % 2][:, c:c + 1], p, AX.X, ALU.max, negate=True)
                    (lr if c else step).step(red)

            def combine(h, i):
                w = NT * h + i
                n = (i + 1) * P
                dve.wait_ge(p_ready, 2 * w + 2)
                s, (p0, p1) = SUMS[w % 2], PR[w % 2]
                step.step(nc.vector.reciprocal(s, s))
                step.step(nc.vector.tensor_tensor(s[:, 1:2], s[:, 1:2], LAM[:, 68:69], ALU.mult))
                step.step(nc.vector.tensor_scalar(p1[:, 0:n], p1[:, 0:n], s[:, 1:2], None, ALU.mult))
                ar.step(nc.vector.scalar_tensor_tensor(p0[:, 0:n], p0[:, 0:n], s[:, 0:1], p1[:, 0:n], ALU.mult, ALU.add))

            def out_norm(h):
                dve.wait_ge(ostd_ready, h + 1)
                step.step(nc.vector.reciprocal(RH, OSTD))
                ohr.step(nc.vector.scalar_tensor_tensor(OH[:, h, :], OB, LAM[:, 69:70], RH, ALU.mult, ALU.mult))

            evac(0, 0)
            evac(0, 1)
            for k in range(KD):
                split_scaled(hq, HQH[:, k, :], HQL[:, k, :], X[:, k, :], par("attn_ln", k))
            evac(0, 2)
            head_norm(0, 0)
            for h in range(AH + 1):
                for i in range(NT):
                    w = NT * h + i
                    if 1 <= w < NT * AH + 1:
                        combine((w - 1) // NT, (w - 1) % NT)
                    if i == 0 and h < AH:
                        head_norm(h, 1)
                    if h + 1 < AH and i < 3:
                        evac(h + 1, i)
                    if h < AH:
                        logits(h, i)
                    if h + 1 < AH and i == 2:
                        head_norm(h + 1, 0)
                    if i == 3 and h >= 1:
                        out_norm(h - 1)
            add_dve(dve, "attn_out", 3, "ffn_ln1", hr, fr, rs)

        sec = Carve()
        YA = sec(2 * MH, T)
        YN = sec(NP_, T)
        GR, FA, FW, FC = (YN[:, i, :] for i in range(NP_))
        nz_at = sec.at
        NZ = sec(NP_, T)
        head_at = sec.at
        HB = []
        for _ in range(2):
            HB.append(dict(q=sec(2, T), k=sec(2, T), v=sec(NT, 2 * P), o=sec(2, T), z=sec(2, T)))
        SW = sec(NT, T)
        cos_at = AREA - 2 * T
        assert sec.at <= cos_at
        sec.at = nz_at
        DW = [sec(T) for _ in range(2)]
        HN = sec(2, T)
        sec.at = head_at
        QRAW = sec(NP_, T)
        KVC = sec(2, T)
        KS, KW = sec(T), sec(T)
        VS, VW = sec(NT, P), sec(NT, P)
        QR = sec(NP_, T)
        cw_at = sec.at
        CW1K = sec(CMPL, P)
        assert sec.at <= cos_at
        CW1V = sec(CMPL, P)
        sec.at = cos_at
        COS, SIN = sec(T), sec(T)
        sec.at = cw_at
        SGA = sec(KD, T)
        pb_at = sec.at
        PB = [[sec(T) for _ in range(2)] for _ in range(2)]
        AT2 = [sec(T) for _ in range(2)]
        NM2 = [sec(2) for _ in range(2)]
        SM2 = [sec(2) for _ in range(2)]
        CL = sec(NT, NCMP)
        CMX, CSM = sec(NT), sec(NT)
        sec.at = pb_at
        SGB = sec(KD, T)
        sec.at = 8 * T
        UC = [sec(CMPL, NCMP) for _ in range(2)]
        sec.at = head_at
        MG = sec(KD, T)
        PCT = [EMB[:, :], RDB[:, :]]
        EM, RDEN, HG = EMB[:, :], RDB[:, :], STD[:, 0:P]
        flat = SMALL[:, :, :].rearrange("p k c -> p (k c)")
        GK = flat[:, 0:16].rearrange("p (c h) -> p c h", h=4)
        GN = flat[:, 16:112].rearrange("p (c h) -> p c h", h=24)
        KCC = flat[:, 112:112 + NCMP]
        VCC = flat[:, 144:272]
        CW2 = flat[:, 272:400]

        gates_done = sem("gate_rows_done")
        g_row = sem("gate_rows_step")
        g_act = sem("gate_act_step")
        gT_done = sem("gates_turned")
        pos_in = sem("positions_in")
        rope_step = sem("rope_step")
        rope_act = sem("rope_act_step")
        bc_done = sem("maxima_spread")
        em_ready = sem("floor_ready")
        dw_ready = sem("mlstm_exponents")
        dwe_ready = sem("mlstm_decay")
        s2_done = sem("mlstm_scores")
        sw_ready = sem("mlstm_weights")
        nd_done = sem("mlstm_sums")
        hn_ready = sem("mlstm_heads")
        mean_done = sem("head_mean_sum")
        hc_ready = sem("head_centered")
        hcsq = sem("head_centered_squares")
        var_done = sem("head_variance_sum")
        vstd = sem("head_deviation")
        ya_ready = sem("mlstm_out_ready")
        vt2_done = sem("values_turned")
        cmp_w_in = sem("compress_weights_in")
        turn_done = sem("rope_turn_done")
        roped = sem("rope_ready")
        vsw_done = sem("nsa_values_turned")
        vsw_ready = sem("nsa_values_ready")
        uc_ready = sem("compress_blocks_ready")
        hid_done = sem("compress_hidden_done")
        hid_ready = sem("compress_hidden_ready")
        kvc_done = sem("compressed_done")
        kvc_ready = sem("compressed_ready")
        cs_done = sem("compressed_scores")
        cl_ready = sem("compressed_logits")
        ce_ready = sem("compressed_exps")
        cp_ready = sem("compressed_probs")
        ct_done = sem("compressed_turned")
        pct_ready = sem("compressed_turned_ready")
        n_s = sem("nsa_scores")
        n_l = sem("nsa_maxima")
        n_p = sem("nsa_exps")
        n_a = sem("nsa_probs")
        n_t = sem("nsa_turned")
        n_tc = sem("nsa_turned_ready")
        n_o = sem("nsa_out")
        yn_out = sem("nsa_gated")
        mg_ready = sem("merged_ready")
        out_ready = sem("output_ready")
        stored = sem("output_stored")

        HT = 10
        NQ0, NZ0, GA0 = 40, 50, 54
        R0, C0 = 84, 68
        W2 = "w_in2"

        def used(n):
            return R0 + min(n, NQ0) + max(n - NZ0, 0)

        def convs(n):
            return C0 + 4 * (n // HT) + min(n % HT, 4)

        def second_pe(pe):
            norm_sum(pe, 4)
            pe.wait_ge(h_ready, H_READY[4])
            small_product(pe, BANK[6][0:88, :], slice(32, 120)).then_inc(gates_done, 1)

            def tile(n):
                gemm_tile(pe, W2, 0, n, lambda k: (HH[:, k, :], HL[:, k, :]))

            def turn_value(n):
                pe.wait_ge(gemm_free, TILE0[W2] + n + 1)
                pe.wait_ge(row_used, used(n))
                for c in range(NT):
                    mm = nc.tensor.transpose(BANK[4][:, c * P:(c + 1) * P], U[:, n % 2, 3 + c * P:3 + (c + 1) * P], IDENT)
                mm.then_inc(vt2_done, 1)

            def spread(h):
                if h >= 1:
                    pe.wait_ge(vstd, h)
                pe.wait_ge(row_used, used(HT * h + 6))
                nc.tensor.matmul(BANK[2][:, :], IDENT[0:4, h:h + 1].to_broadcast([4, P]), FW[0:4, :], start=True, stop=True)
                nc.tensor.matmul(BANK[4][:, :], IDENT[0:4, h:h + 1].to_broadcast([4, P]), FA[0:4, :],
                                 start=True, stop=True).then_inc(bc_done, 1)

            def scores(h, sb):
                if h or sb:
                    pe.wait_ge(sw_ready, NT * h + sb)
                pe.wait_ge(row_used, used(HT * h + 4))
                b = HB[h % 2]
                for e in range(2):
                    mm = nc.tensor.matmul(BANK[3][:, 0:T - sb * P], b["k"][:, e, sb * P:(sb + 1) * P], b["q"][:, e, sb * P:T],
                                          start=(e == 0), stop=(e == 1))
                mm.then_inc(s2_done, 1)

            def sums(h, sb):
                pe.wait_ge(sw_ready, NT * h + sb + 1)
                if sb == 0 and h >= 1:
                    pe.wait_ge(hn_ready, 2 * h)
                pe.wait_ge(row_used, used(HT * h + 6))
                first, last = sb == 0, sb == NT - 1
                at = slice(sb * P, T)
                for e in range(2):
                    nc.tensor.matmul(BANK[5 + e][:, at], HB[h % 2]["v"][:, sb, e * P:(e + 1) * P], SW[:, sb, 0:T - sb * P],
                                     start=first, stop=last)
                mm = nc.tensor.matmul(BANK[7][:, at], ONES[:, :], SW[:, sb, 0:T - sb * P], start=first, stop=last)
                if last:
                    mm.then_inc(nd_done, 1)

            def mean(h):
                pe.wait_ge(hn_ready, 2 * h + 2)
                for e in range(2):
                    mm = nc.tensor.matmul(BANK[2][:, :], ONES[:, :], HN[:, e, :], start=(e == 0), stop=(e == 1))
                mm.then_inc(mean_done, 1)

            def variance(h):
                pe.wait_ge(hcsq, h + 1)
                for e in range(2):
                    mm = nc.tensor.matmul(BANK[2][:, :], ONES[:, :], SQ[:, e, :], start=(e == 0), stop=(e == 1))
                mm.then_inc(var_done, 1)

            for n in range(HT):
                tile(n)
                if n in (5, 6):
                    turn_value(n - 1)
            pe.wait_ge(g_row, 15)
            pe.wait_ge(g_act, 1)
            for c in range(NT):
                tok = slice(c * P, (c + 1) * P)
                nc.tensor.transpose(BANK[6][:, 32 * c:32 * c + 4], GR[0:4, tok], IDENT[0:4, 0:4])
                mm = nc.tensor.transpose(BANK[5][:, 32 * c:32 * c + 24], GR[64:88, tok], IDENT[64:88, 64:88])
            mm.then_inc(gT_done, 1)
            pe.wait_ge(g_row, 17)
            for h in range(MH):
                m = HT * (h + 1)
                spread(h)
                tile(m)
                scores(h, 0)
                tile(m + 1)
                for sb in range(1, NT):
                    sums(h, sb - 1)
                    scores(h, sb)
                    tile(m + 1 + sb)
                sums(h, NT - 1)
                tile(m + 5)
                if h + 1 < MH:
                    turn_value(m + 4)
                mean(h)
                tile(m + 6)
                if h + 1 < MH:
                    turn_value(m + 5)
                variance(h)
                for n in range(7, HT):
                    tile(m + n)
            def turn_nsa_value(x):
                pe.wait_ge(gemm_free, TILE0[W2] + 49 + x)
                if x:
                    pe.wait_ge(vsw_ready, 1)
                for c in range(NT):
                    mm = nc.tensor.transpose(BANK[4][:, c * P:(c + 1) * P], CV[:, x, c * P:(c + 1) * P], IDENT)
                mm.then_inc(vsw_done, 1)

            def turn_rope(x):
                if x >= 2:
                    pe.wait_ge(roped, x - 1)
                pe.wait_ge(vstd, MH)
                src = QRAW[:, x, :] if x < NP_ else (KS, KW)[x - NP_]
                nc.tensor.matmul(BANK[2 + x % 2][:, :], const("rope_turn"), src, start=True, stop=True).then_inc(turn_done, 1)

            turn_rope(0)
            turn_rope(1)
            tile(NZ0)
            turn_nsa_value(0)
            turn_rope(2)
            turn_rope(3)
            tile(NZ0 + 1)
            turn_nsa_value(1)
            turn_rope(4)
            turn_rope(5)
            tile(NZ0 + 2)
            pe.wait_ge(cmp_w_in, 48)
            pe.wait_ge(uc_ready, 2)
            for x in range(2):
                for g in range(2):
                    half = slice(64 * g, 64 * g + 64)
                    at = 32 * x
                    for l in range(CMPL):
                        mm = nc.tensor.matmul(BANK[7 if g else 5][:, at:at + NCMP], (CW1K, CW1V)[x][half, l, :], UC[x][half, l, :],
                                              start=(l == 0), stop=(l == CMPL - 1))
            mm.then_inc(hid_done, 1)
            tile(NZ0 + 3)
            pe.wait_ge(hid_ready, 2)
            for g in range(2):
                nc.tensor.matmul(BANK[7][64 * g:64 * g + 64, 128:128 + NCMP], CW2[:, 0:64], HG[:, 32 * g:32 * g + NCMP],
                                 start=True, stop=True)
                mm = nc.tensor.matmul(BANK[7][0:NCMP, 192 + 64 * g:256 + 64 * g], HG[:, 64 + 32 * g:64 + 32 * g + NCMP],
                                      CW2[:, 64:128], start=True, stop=True)
            mm.then_inc(kvc_done, 1)

            def cmp_scores(s):
                g, j = s % 2, s // 2
                half = slice(64 * g, 64 * g + 64)
                pe.wait_ge(kvc_ready, 2)
                if s >= 1:
                    pe.wait_ge(pct_ready, s)
                for i in range(NT):
                    mm = nc.tensor.matmul(BANK[7][:, NCMP * i:NCMP * (i + 1)], QRAW[half, j, i * P:(i + 1) * P],
                                          KCC[half, :], start=True, stop=True)
                mm.then_inc(cs_done, 1)

            def cmp_turn(s):
                pe.wait_ge(cp_ready, s + 1)
                for i in range(NT):
                    mm = nc.tensor.transpose(BANK[7][0:NCMP, i * P:(i + 1) * P], CL[:, i, :], IDENT)
                mm.then_inc(ct_done, 1)

            def nsa_scores(w):
                s, i = w // NT, w % NT
                g, j = s % 2, s // 2
                half = slice(64 * g, 64 * g + 64)
                pe.wait_ge(roped, 6)
                if w >= 1:
                    pe.wait_ge(n_p, 2 * w)
                for c, keys in enumerate((KS, KW)):
                    nc.tensor.matmul(BANK[2 + c][:, 0:(i + 1) * P], QR[half, j, i * P:(i + 1) * P], keys[half, 0:(i + 1) * P],
                                     start=True, stop=False)
                    mm = nc.tensor.matmul(BANK[2 + c][:, i * P:(i + 1) * P], IDENT, const("future_neg"), start=False, stop=True)
                mm.then_inc(n_s, 1)

            def nsa_turn(w):
                i = w % NT
                pe.wait_ge(n_a, w + 1)
                if w >= 1:
                    pe.wait_ge(n_tc, 2 * w)
                else:
                    pe.wait_ge(vsw_ready, 2)
                for c in range(2):
                    for kb in range(i + 1):
                        mm = nc.tensor.transpose(BANK[4 + c][:, kb * P:(kb + 1) * P], PB[w % 2][c][:, kb * P:(kb + 1) * P], IDENT)
                mm.then_inc(n_t, 1)

            def nsa_v(w):
                s, i = w // NT, w % NT
                g, j = s % 2, s // 2
                pe.wait_ge(n_tc, 2 * w + 2)
                pe.wait_ge(pct_ready, s + 1)
                if w % 8 == 0 and w:
                    pe.wait_ge(yn_out, j)
                out_t = BANK[6][64 * g:64 * g + 64, i * P:(i + 1) * P]
                nc.tensor.matmul(out_t, VCC[0:NCMP, 64 * g:64 * g + 64], PCT[s % 2][0:NCMP, i * P:(i + 1) * P],
                                 start=True, stop=False)
                for c, values in enumerate((VS, VW)):
                    for kb in range(i + 1):
                        mm = nc.tensor.matmul(out_t, values[:, kb, 64 * g:64 * g + 64], AT2[c][:, kb * P:(kb + 1) * P],
                                              start=False, stop=(c == 1 and kb == i))
                mm.then_inc(n_o, 1)

            cmp_scores(0)
            cmp_turn(0)
            for w in range(NT * 8 + 2):
                if w % 4 == 1 and w < 32:
                    tile(GA0 + w // 4)
                if w < 32:
                    nsa_scores(w)
                if w >= 2:
                    nsa_v(w - 2)
                if 1 <= w < 33:
                    nsa_turn(w - 1)
                if w < 28 and w % NT == 0:
                    cmp_scores(w // NT + 1)
                if w < 28 and w % NT == 2:
                    cmp_turn(w // NT + 1)
            for n in range(GA0 + KD, GA0 + 2 * KD):
                tile(n)
            pe.wait_ge(ya_ready, 2 * MH)
            pe.wait_ge(yn_out, NP_)
            with pe.Fori(0, KD // 2) as i:
                for j in range(4):
                    gemm_tile(pe, "ab", i, j, lambda k: (YN if j % 2 else YA)[:, k, :], 4 if j % 2 else 8)

            def merged(pe, k, j):
                if j == 0:
                    pe.wait_ge(mg_ready, k + 1)
                return MG[:, k, :]
            add_pe(pe, "w_out2", merged, 8)
            norm_sum(pe, 5)

        def second_act(act):
            ga = Count(act, g_act)
            act.wait_ge(gemm_free, TILE0[W2])
            act.dma_start(COS.bitcast(mybir.dt.int32), A["pos"]).then_inc(pos_in, 16)
            act.wait_ge(g_row, 2)
            act.dma_start(CW2, A["cmp_w2"]).then_inc(cmp_w_in, 16)
            ga.step(nc.scalar.activation(GR[64:88, :], GR[64:88, :], ACT.Sigmoid))
            ga.step(nc.scalar.activation(FA[32:36, :], GR[32:36, :], ACT.Abs))
            ga.step(nc.scalar.activation(FA[32:36, :], FA[32:36, :], ACT.Exp, scale=-1.0))
            act.wait_ge(g_row, 3)
            ga.step(nc.scalar.activation(HN[32:36, 0, :], FW[32:36, :], ACT.Ln))
            ra = Count(act, rope_act)
            act.wait_ge(rope_step, 8)
            ra.step(nc.scalar.activation(SIN, HN[:, 1, :], ACT.Sin))
            ra.step(nc.scalar.activation(COS, HN[:, 1, :], ACT.Abs))
            act.wait_ge(rope_step, 9)
            ra.step(nc.scalar.activation(COS, COS, ACT.Sin))

            def rows(n):
                h, j = n // HT, n % HT
                b = HB[h % 2]
                if n < NQ0:
                    if h >= 2 and j == 0:
                        act.wait_ge(ya_ready, 2 * (h - 1))
                    if j < 4:
                        act.wait_ge(conv_ready, convs(n) + 1)
                        ins = nc.scalar.activation(b["q" if j < 2 else "k"][:, j % 2, :], CV[:, n % 2, :], ACT.Silu)
                    elif j < 6:
                        act.wait_ge(vt2_done, 2 * h + j - 3)
                        ins = nc.scalar.activation(b["v"][:, :, (j - 4) * P:(j - 3) * P],
                                                   BANK[4][:, :].rearrange("p (c d) -> p c d", d=P), ACT.Copy)
                    else:
                        act.wait_ge(gemm_free, TILE0[W2] + n + 1)
                        ins = nc.scalar.activation(b["o" if j < 8 else "z"][:, j % 2, :], U[:, n % 2, 3:3 + T],
                                                   ACT.Sigmoid if j < 8 else ACT.Silu)
                else:
                    act.wait_ge(gemm_free, TILE0[W2] + n + 1)
                    if n >= GA0:
                        act.wait_ge(hid_done, 1)
                        k = n - GA0
                        ins = nc.scalar.activation((SGA if k < KD else SGB)[:, k % KD, :], U[:, n % 2, 3:3 + T], ACT.Sigmoid)
                    else:
                        ins = nc.scalar.activation(NZ[:, n - NZ0, :], U[:, n % 2, 3:3 + T], ACT.Silu)
                ins.then_inc(row_used, 1)

            def decay(h, sb):
                act.wait_ge(dw_ready, NT * h + sb + 1)
                d = DW[sb % 2][:, 0:T - sb * P]
                nc.scalar.activation(d, d, ACT.Exp).then_inc(dwe_ready, 1)

            for n in range(HT):
                rows(n)
            for h in range(MH):
                m = HT * (h + 1)
                act.wait_ge(bc_done, h + 1)
                if h >= 1:
                    act.wait_ge(hn_ready, 2 * h)
                nc.scalar.activation(EM, BANK[4][:, :], ACT.Exp, scale=-1.0).then_inc(em_ready, 1)

                def next_rows(*js):
                    if h + 1 < MH:
                        for j in js:
                            rows(m + j)
                next_rows(0)
                decay(h, 0)
                next_rows(1)
                for sb in range(1, NT):
                    decay(h, sb)
                    if sb < 3:
                        next_rows(1 + sb)
                next_rows(4)
                act.wait_ge(hc_ready, 2 * h + 2)
                nc.scalar.activation(SQ[:, 0:2, :], HN, ACT.Square).then_inc(hcsq, 1)
                next_rows(5)
                act.wait_ge(var_done, h + 1)
                nc.scalar.activation(STD[:, :], BANK[2][:, :], ACT.Sqrt, bias=EPSC[:, 0:1], scale=1.0 / 256).then_inc(vstd, 1)
                next_rows(6, 7, 8, 9)

            def nsa_value(x):
                act.wait_ge(vsw_done, x + 1)
                nc.scalar.activation((VS, VW)[x], BANK[4][:, :].rearrange("p (c d) -> p c d", d=P), ACT.Copy).then_inc(vsw_ready, 1)

            act.wait_ge(ya_ready, 2 * MH)
            act.dma_start(CW1K, A["cmp_w1"][0]).then_inc(cmp_w_in, 16)
            nsa_value(0)
            rows(NZ0)
            nsa_value(1)
            rows(NZ0 + 1)
            act.wait_ge(roped, 6)
            act.dma_start(CW1V, A["cmp_w1"][1]).then_inc(cmp_w_in, 16)
            rows(NZ0 + 2)
            act.wait_ge(hid_done, 1)
            for g in range(2):
                nc.scalar.activation(HG.rearrange("p (a g n) -> p a g n", g=2, n=32)[:, :, g, 0:NCMP],
                                     BANK[7 if g else 5][:, 0:64].rearrange("p (a n) -> p a n", n=32)[:, :, 0:NCMP],
                                     ACT.Gelu_apprx_tanh).then_inc(hid_ready, 1)
            rows(NZ0 + 3)

            def cmp_exp(s):
                act.wait_ge(cl_ready, s + 1)
                nc.scalar.activation(CL, CL, ACT.Exp).then_inc(ce_ready, 1)

            def cmp_turned(s):
                act.wait_ge(ct_done, s + 1)
                if s >= 2:
                    act.wait_ge(n_o, NT * (s - 1))
                nc.scalar.activation(PCT[s % 2][0:NCMP, :], BANK[7][0:NCMP, :], ACT.Copy).then_inc(pct_ready, 1)

            def exps(w):
                n = (w % NT + 1) * P
                act.wait_ge(n_l, w + 1)
                if w >= 2:
                    act.wait_ge(n_t, w - 1)
                for c in range(2):
                    nc.scalar.activation(PB[w % 2][c][:, 0:n], BANK[2 + c][:, 0:n], ACT.Exp, bias=NM2[w % 2][:, c:c + 1],
                                         scale=0.125, accum_out=SM2[w % 2][:, c:c + 1]).then_inc(n_p, 1)

            def turned(w):
                n = (w % NT + 1) * P
                act.wait_ge(n_t, w + 1)
                if w >= 1:
                    act.wait_ge(n_o, w)
                for c in range(2):
                    nc.scalar.activation(AT2[c][:, 0:n], BANK[4 + c][:, 0:n], ACT.Copy).then_inc(n_tc, 1)

            cmp_exp(0)
            cmp_turned(0)
            for w in range(NT * 8 + 2):
                if 1 <= w < 33:
                    turned(w - 1)
                if w < 32:
                    exps(w)
                if w % 4 == 1 and w < 32:
                    rows(GA0 + w // 4)
                if w < 28 and w % NT == 0:
                    cmp_exp(w // NT + 1)
                if w < 28 and w % NT == 2:
                    cmp_turned(w // NT + 1)
            act.wait_ge(yn_out, NP_)
            for n in range(GA0 + KD, GA0 + 2 * KD):
                rows(n)
            add_act(act, "w_out2", 5)

        def second_dve(dve, step, rs, hr, fr, cv):
            gr, rp = Count(dve, g_row), Count(dve, rope_step)
            dve.wait_ge(gates_done, 1)
            gr.step(nc.vector.tensor_tensor(GR[0:88, :], BANK[6][0:88, :], RS[0:88, :], ALU.mult))
            gr.step(nc.vector.tensor_scalar(GR[0:88, :], GR[0:88, :], par("gate_bias", parts=88), None, ALU.add))
            f, fa, fw, fc = (b[32:36, :] for b in (GR, FA, FW, FC))
            dve.wait_ge(g_act, 3)
            gr.step(nc.vector.tensor_scalar(fw, fa, 1.0, None, ALU.add))
            gr.step(nc.vector.tensor_scalar(fc, fw, -1.0, None, ALU.add))
            gr.step(nc.vector.tensor_tensor(fa, fa, fc, ALU.subtract))
            gr.step(nc.vector.tensor_scalar(f, f, 0.0, None, ALU.min))
            dve.wait_ge(g_act, 4)
            gr.step(nc.vector.tensor_tensor(fa, fa, HN[32:36, 0, :], ALU.add))
            gr.step(nc.vector.tensor_tensor(f, f, fa, ALU.subtract))
            gr.step(nc.vector.memset(fw, 1.0))
            gr.step(nc.vector.tensor_tensor_scan(fc, fw, f, 0.0, ALU.mult, ALU.add))
            li, f0, mx, mt = GR[0:4, :], FC[0:4, :], FW[0:4, :], FA[0:4, :]
            gr.step(nc.vector.tensor_copy(f0, fc))
            gr.step(nc.vector.tensor_tensor(li, li, f0, ALU.subtract))
            gr.step(nc.vector.tensor_tensor_scan(mx, li, li, 0.0, ALU.max, ALU.max))
            gr.step(nc.vector.tensor_tensor(mt, mx, f0, ALU.add))
            gr.step(nc.vector.tensor_scalar(mx, mx, -1.0, None, ALU.mult))
            ang, turns = HN[:, 1, :], SIN
            dve.wait_ge(pos_in, 16)
            dve.wait_ge(row_used, R0)
            rp.step(nc.vector.tensor_copy(ang, COS.bitcast(mybir.dt.int32)))
            rp.step(nc.vector.tensor_scalar(ang, ang, const("rope_freq"), None, ALU.mult))
            rp.step(nc.vector.tensor_scalar(turns, ang, 1.0 / (2 * math.pi), 1.5 * 2 ** 23, ALU.mult, ALU.add))
            rp.step(nc.vector.tensor_scalar(turns, turns, -1.5 * 2 ** 23, None, ALU.add))
            p1, p2 = 6.28125, float(np.float32(2 * math.pi - 6.28125).view(np.uint32).__and__(np.uint32(0xFFFFF000)).view(np.float32))
            for part in (p1, p2, 2 * math.pi - p1 - p2):
                rp.step(nc.vector.scalar_tensor_tensor(ang, turns, -part, ang, ALU.mult, ALU.add))
            rp.step(nc.vector.tensor_scalar(ang, ang, 3.1415925, -3.1415925, ALU.min, ALU.max))
            dve.wait_ge(rope_act, 2)
            rp.step(nc.vector.tensor_scalar(COS, COS, -1.0, math.pi / 2, ALU.mult, ALU.add))

            def evac(n, dst):
                dve.wait_ge(gemm_done, TILE0[W2] + n + 1)
                fr.step(nc.vector.tensor_tensor(dst, BANK[(TILE0[W2] + n) % 2][:, :], RS[:, :], ALU.mult))

            def rows(n):
                h, j = n // HT, n % HT
                if n < NQ0 or n >= NZ0:
                    if n >= 2:
                        dve.wait_ge(row_used, used(n - 1))
                    evac(n, U[:, n % 2, 3:3 + T])
                    if n < NQ0 and j < 4:
                        t = 2 * h + j % 2 + (8 if j >= 2 else 0)
                        conv(dve, step, cv, n % 2, lambda k: par("qk_conv", 5 * t + k), 4)
                    return
                k = n - NQ0
                if k == 8:
                    dve.wait_ge(row_used, used(NQ0))
                evac(n, [QRAW[:, 0, :], QRAW[:, 1, :], QRAW[:, 2, :], QRAW[:, 3, :], KVC[:, 0, :], KVC[:, 1, :],
                         KS, KW, CV[:, 0, :], CV[:, 1, :]][k])

            dw, sw, hn, hc, ya = (Count(dve, s) for s in (dw_ready, sw_ready, hn_ready, hc_ready, ya_ready))

            def exponents(h, sb):
                if sb == 0:
                    dve.wait_ge(bc_done, h + 1)
                n = T - sb * P
                dw.step(nc.vector.tensor_scalar(DW[sb % 2][:, 0:n], BANK[2][:, sb * P:T], GK[:, sb, h:h + 1], 0.0,
                                                ALU.add, ALU.min))

            def weights(h, sb):
                n = T - sb * P
                dve.wait_ge(dwe_ready, NT * h + sb + 1)
                dve.wait_ge(s2_done, NT * h + sb + 1)
                step.step(nc.vector.scalar_tensor_tensor(SW[:, sb, 0:n], BANK[3][:, 0:n], 1.0 / 16, DW[sb % 2][:, 0:n],
                                                         ALU.mult, ALU.mult))
                sw.step(nc.vector.tensor_tensor(SW[:, sb, 0:P], SW[:, sb, 0:P], const("causal_st"), ALU.mult))

            def divide(h):
                dve.wait_ge(nd_done, h + 1)
                dve.wait_ge(em_ready, h + 1)
                step.step(nc.vector.tensor_scalar(RDEN, BANK[7][:, :], -1.0, None, ALU.mult))
                step.step(nc.vector.tensor_tensor(RDEN, RDEN, BANK[7][:, :], ALU.max))
                step.step(nc.vector.tensor_tensor(RDEN, RDEN, EM, ALU.max))
                step.step(nc.vector.reciprocal(RDEN, RDEN))
                for e in range(2):
                    hn.step(nc.vector.tensor_tensor(HN[:, e, :], BANK[5 + e][:, :], RDEN, ALU.mult))

            def center(h):
                dve.wait_ge(mean_done, h + 1)
                for e in range(2):
                    hc.step(nc.vector.scalar_tensor_tensor(HN[:, e, :], BANK[2][:, :], -1.0 / 256, HN[:, e, :], ALU.mult, ALU.add))

            def gated(h):
                dve.wait_ge(vstd, h + 1)
                dve.wait_ge(row_used, used(HT * (h + 1)))
                step.step(nc.vector.reciprocal(RDEN, STD[:, :]))
                for e in range(2):
                    step.step(nc.vector.scalar_tensor_tensor(HN[:, e, :], HN[:, e, :], par("mh_norm", 2 * h + e), RDEN, ALU.mult, ALU.mult))
                    step.step(nc.vector.tensor_tensor(HN[:, e, :], HN[:, e, :], HB[h % 2]["o"][:, e, :], ALU.mult))
                    ya.step(nc.vector.tensor_tensor(YA[:, 2 * h + e, :], HN[:, e, :], HB[h % 2]["z"][:, e, :], ALU.mult))

            for n in range(HT):
                rows(n)
            dve.wait_ge(gT_done, 1)
            b6 = BANK[6][:, 0:P].rearrange("p (c w) -> p c w", w=32)
            gr.step(nc.vector.tensor_copy(GK, b6[:, :, 0:4]))
            b5 = BANK[5][:, 0:P].rearrange("p (c w) -> p c w", w=32)
            gr.step(nc.vector.tensor_copy(GN, b5[:, :, 0:24]))
            for h in range(MH):
                m = HT * (h + 1)
                exponents(h, 0)
                rows(m)
                weights(h, 0)
                exponents(h, 1)
                rows(m + 1)
                for sb in range(1, NT):
                    weights(h, sb)
                    if sb + 1 < NT:
                        exponents(h, sb + 1)
                    rows(m + 1 + sb)
                divide(h)
                rows(m + 5)
                center(h)
                rows(m + 6)
                gated(h)
                for n in range(7, HT):
                    rows(m + n)

            ro, uc, kvc = (Count(dve, s) for s in (roped, uc_ready, kvc_ready))

            def rotate(x):
                dve.wait_ge(turn_done, x + 1)
                dve.wait_ge(rope_act, 3)
                src, dst = (QRAW[:, x, :], QR[:, x, :]) if x < NP_ else ((KS, KW)[x - NP_],) * 2
                step.step(nc.vector.tensor_tensor(RDEN, BANK[2 + x % 2][:, :], SIN, ALU.mult))
                step.step(nc.vector.tensor_tensor(dst, src, COS, ALU.mult))
                ro.step(nc.vector.tensor_tensor(dst, dst, RDEN, ALU.add))

            rotate(0)
            rotate(1)
            rows(NZ0)
            rotate(2)
            rotate(3)
            rows(NZ0 + 1)
            for x in range(2):
                blocks = bass.AP(tensor=KVC.tensor, offset=KVC[:, x, :].offset, ap=[KVC.ap[0], [1, CMPL], [16, NCMP]])
                uc.step(nc.vector.tensor_tensor(UC[x], blocks, par("cmp_pos", CMPL * x, CMPL).unsqueeze(2)
                                                .to_broadcast([P, CMPL, NCMP]), ALU.add))
            rotate(4)
            rotate(5)
            rows(NZ0 + 2)
            rows(NZ0 + 3)
            dve.wait_ge(kvc_done, 1)
            kvc.step(nc.vector.tensor_copy(KCC, BANK[7][:, 128:128 + NCMP]))
            kvc.step(nc.vector.tensor_copy(VCC[0:NCMP, :], BANK[7][0:NCMP, 192:320]))

            cl, cp, nl, na, yo, mg = (Count(dve, s) for s in (cl_ready, cp_ready, n_l, n_a, yn_out, mg_ready))
            cells = [P, NT, NCMP]

            def head_of(s):
                return s // 2 + 4 * (s % 2)

            def cmp_logits(s):
                dve.wait_ge(cs_done, s + 1)
                if s >= 1:
                    dve.wait_ge(ct_done, s)
                sc = BANK[7][:, 0:NT * NCMP].rearrange("p (i n) -> p i n", n=NCMP)
                neg = const("cmp_neg").rearrange("p (i n) -> p i n", n=NCMP)
                step.step(nc.vector.scalar_tensor_tensor(CL, sc, 0.125, neg, ALU.mult, ALU.add))
                step.step(nc.vector.tensor_reduce(CMX, CL, AX.X, ALU.max))
                cl.step(nc.vector.tensor_tensor(CL, CL, CMX.unsqueeze(2).to_broadcast(cells), ALU.subtract))

            def cmp_probs(s):
                dve.wait_ge(ce_ready, s + 1)
                h = head_of(s)
                step.step(nc.vector.tensor_reduce(CSM, CL, AX.X, ALU.add))
                step.step(nc.vector.reciprocal(CSM, CSM))
                step.step(nc.vector.tensor_tensor(CSM, CSM, GN[:, :, 3 * h], ALU.mult))
                step.step(nc.vector.tensor_tensor(CL, CL, const("cmp_seen").rearrange("p (i n) -> p i n", n=NCMP), ALU.mult))
                cp.step(nc.vector.tensor_tensor(CL, CL, CSM.unsqueeze(2).to_broadcast(cells), ALU.mult))

            def maxima(w):
                n = (w % NT + 1) * P
                dve.wait_ge(n_s, w + 1)
                for c in range(2):
                    step.step(nc.vector.tensor_reduce(NM2[w % 2][:, c:c + 1], BANK[2 + c][:, 0:n], AX.X, ALU.max, negate=True))
                nl.step(nc.vector.tensor_scalar(NM2[w % 2], NM2[w % 2], 0.125, None, ALU.mult))

            def probs(w):
                s, i = w // NT, w % NT
                h, n = head_of(s), (i + 1) * P
                dve.wait_ge(n_p, 2 * w + 2)
                sm = SM2[w % 2]
                step.step(nc.vector.reciprocal(sm, sm))
                step.step(nc.vector.tensor_tensor(sm, sm, GN[:, i, 3 * h + 1:3 * h + 3], ALU.mult))
                for c in range(2):
                    p = PB[w % 2][c][:, 0:n]
                    (na if c else step).step(nc.vector.tensor_scalar(p, p, sm[:, c:c + 1], None, ALU.mult))

            cmp_logits(0)
            cmp_probs(0)
            for w in range(NT * 8 + 2):
                if 1 <= w < 33:
                    probs(w - 1)
                if w % 4 == 1 and w < 32:
                    rows(GA0 + w // 4)
                if w < 32:
                    maxima(w)
                if w < 28 and w % NT == 0:
                    cmp_logits(w // NT + 1)
                if w < 28 and w % NT == 1:
                    cmp_probs(w // NT + 1)
                if w >= 2 and (w - 2) % 8 == 7:
                    j = (w - 2) // 8
                    dve.wait_ge(n_o, w - 1)
                    yo.step(nc.vector.tensor_tensor(YN[:, j, :], BANK[6][:, :], NZ[:, j, :], ALU.mult))

            for n in range(GA0 + KD, GA0 + 2 * KD):
                rows(n)
            dve.wait_ge(row_used, used(70))
            with dve.Fori(0, KD // 2) as i:
                for c, per in ((fr, 4), (mg, 2)):
                    c.enter(i, per)
                for j in range(4):
                    k = i * 2 + j // 2
                    dve.wait_ge(gemm_done, i * 4 + (TILE0["ab"] + j + 1))
                    gate = (SGB if j % 2 else SGA)[:, bass.ds(k, 1), :]
                    fr.step(nc.vector.tensor_tensor(CV[:, j % 2:j % 2 + 1, :], BANK[(TILE0["ab"] + j) % 2][:, :].unsqueeze(1), gate, ALU.mult))
                    if j % 2:
                        mg.step(nc.vector.tensor_tensor(MG[:, bass.ds(k, 1), :], CV[:, 0:1, :], CV[:, 1:2, :], ALU.add))
                for c in (fr, mg):
                    c.leave(KD // 2)
            add_dve(dve, "w_out2", 5, "final", hr, fr, rs)
            for k in range(KD):
                nc.vector.scalar_tensor_tensor(X[:, k, :], X[:, k, :], par("final", k), RS[:, :], ALU.mult, ALU.mult).then_inc(out_ready, 1)

        COUNT0 = {"conv0": (24, 40), "conv1": (46, 62)}
        H_READY = {turn: 2 * KD * (turn + 1) for turn in range(6)}

        def finish(sp):
            for k in range(KD):
                sp.wait_ge(out_ready, k + 1)
                sp.dma_start(out[:, k, :], X[:, k, :]).then_inc(stored, 16)
            sp.wait_ge(stored, 16 * KD)

        def rest_pe(pe):
            def ynorm(pe, k, j):
                if j == 0:
                    pe.wait_ge(yn_ready, k + 1)
                return YB[:, k, :]
            add_pe(pe, "out_w", ynorm, 8)
            ffn_pe(pe, 0)
            attention_pe(pe)
            ffn_pe(pe, 1)
            second_pe(pe)


        def rest_act(act):
            add_act(act, "out_w", 1)
            ffn_act(act, 0)
            attention_act(act)
            ffn_act(act, 1)
            second_act(act)

        def rest_dve(dve, step, rs, hr, fr, cv):
            add_dve(dve, "out_w", 1, "ffn_ln0", hr, fr, rs)
            ffn_dve(dve, 0, "kv_ln", step, rs, hr, fr, cv)
            attention_dve(dve, step, rs, hr, fr, cv)
            ffn_dve(dve, 1, "norm2", step, rs, hr, fr, cv)
            second_dve(dve, step, rs, hr, fr, cv)

        @block.sync
        def _(sp):
            sp.dma_start(X[:, :, :], A["xT"]).then_inc(loaded, 16)
            sp.dma_start(PAR[:, :], A["param"]).then_inc(loaded, 16)
            sp.dma_start(CST[:, :], A["const"]).then_inc(loaded, 16)
            sp.dma_start(SMALL[:, :, :], A["small"]).then_inc(loaded, 16)

            def load(name, cells, block_at, slot, free):
                if free is not None:
                    sp.wait_ge(*free)
                sp.dma_start(RAW[:, slot, 0:cells * P], A[name][bass.ds(block_at, 1), :, :]
                             .rearrange("a p n -> (a p) n")).then_inc(w_ready[slot], 16)

            last = []
            for name, n, cells, per, parts in STREAM:
                turns = n // TURN - 1
                for k in range(TURN):
                    free = loaded_used(*last[-SLOTS]) if len(last) >= SLOTS else None
                    load(name, cells, k, k % SLOTS, free)
                    last.append((name, per, k))
                with sp.Fori(0, turns) as i:
                    for j in range(TURN):
                        load(name, cells, i * TURN + (TURN + j), j % SLOTS, loaded_used(name, per, TURN + j - SLOTS, i))
                last += [(name, per, k) for k in range(TURN, TURN * (turns + 1))]
                for k in range(TURN * (turns + 1), n):
                    load(name, cells, k, k % SLOTS, loaded_used(*last[-SLOTS]))
                    last.append((name, per, k))
            finish(sp)

        @block.gpsimd
        def _(pool):
            def split(name, cells, k, i, free):
                slot, n = k % SLOTS, cells * P
                pool.wait_ge(w_ready[slot], (BASE[name] + k) // SLOTS * 16 + 16 + i * (16 * TURN // SLOTS))
                if free is not None:
                    pool.wait_ge(*free)
                nc.gpsimd.tensor_tensor(WH[:, slot, 0:8], RAW[:, slot, 0:8], ONES[:, 0:8], ALU.mult).then_inc(high_ready, 1)
                nc.gpsimd.tensor_scalar(WH[:, slot, 8:n], RAW[:, slot, 8:n], 1.0, 1.0, ALU.mult, ALU.mult).then_inc(high_ready, 1)
                pool.wait_ge(high_ready, 2 * (PART0[name] + k + 1) + i * (2 * TURN))
                nc.gpsimd.tensor_tensor(WL[:, slot, 0:n], RAW[:, slot, 0:n], WH[:, slot, 0:n].bitcast(F32),
                                        ALU.subtract).then_inc(split_done, 1)

            pool.wait_ge(ones_set, 1)
            last = []
            for name, n, cells, per, parts in STREAM:
                if not parts:
                    continue
                turns = n // TURN - 1
                for k in range(TURN):
                    split(name, cells, k, 0, products_done(*last[-SLOTS]) if len(last) >= SLOTS else None)
                    last.append((name, per, k))
                with pool.Fori(0, turns) as i:
                    for j in range(TURN):
                        split(name, cells, TURN + j, i, products_done(name, per, TURN + j - SLOTS, i))
                last += [(name, per, k) for k in range(TURN, TURN * (turns + 1))]
                for k in range(TURN * (turns + 1), n):
                    split(name, cells, k, 0, products_done(*last[-SLOTS]))
                    last.append((name, per, k))

        @block.tensor
        def _(pe):
            pe.wait_ge(ones_set, 3)
            pe.wait_ge(loaded, 64)
            pe.wait_ge(h_ready, 2 * KD)
            small_product(pe, BANK[6][0:32, :], slice(0, 32)).then_inc(dt_done, 1)
            norm_sum(pe, 0)

            def bias_row(h):
                if h >= 1:
                    pe.wait_ge(brow_ready, 2 * h)
                nc.tensor.matmul(BANK[2][:, :], REL[0:33, h:h + 1].to_broadcast([33, P]), BUCK[0:33, 0:T],
                                 start=True, stop=True)
                nc.tensor.matmul(BANK[3][:, 0:P], REL[0:33, h:h + 1].to_broadcast([33, P]), BUCK[0:33, T:640],
                                 start=True, stop=True).then_inc(brow_done, 1)

            def in_tile(g, j):
                gemm_tile(pe, "in_w", 0, GROUP_TILES * g + j, lambda k: (HH[:, k, :], HL[:, k, :]))

            pe.wait_ge(aux_in, 32)
            for j in range(GROUP_TILES):
                in_tile(0, j)
                if j < AH:
                    bias_row(j)
            pe.wait_ge(dt_row, 10 + NT)
            for c in range(NT):
                nc.tensor.transpose(BANK[6][:, c * 64:c * 64 + 32], DTR[0:32, c * P:(c + 1) * P], IDENT[0:32, 0:32])
                mm = nc.tensor.transpose(BANK[6][:, c * 64 + 32:c * 64 + 64], CSR[0:32, c * P:(c + 1) * P], IDENT[0:32, 0:32])
            mm.then_inc(dtT_done, 1)

            def unit_sums(u):
                pe.wait_ge(gsq_ready, u + 1)
                for k in range(GT):
                    mm = nc.tensor.matmul(BANK[4][:, 2 * P:3 * P], ONES[:, :], YSQ[:, k, :], start=(k == 0), stop=(k == GT - 1))
                mm.then_inc(usum_done, 1)

            for g in range(SSM_G):
                xb = XSB[g % 2]
                for c in range(NT):
                    u = NT * g + c
                    tok = slice(c * P, (c + 1) * P)
                    if c == 0:
                        pe.wait_ge(row_used, GROUP_TILES * (g + 1))
                        pe.wait_ge(dt_row, 12 + NT)
                    if u >= 1:
                        pe.wait_ge(d_ready, u)
                        pe.wait_ge(e_ready, 3 * u)
                    if u >= 2:
                        pe.wait_ge(gs_read, u - 1)
                    if u == 0:
                        pe.wait_ge(brow_ready, 2 * AH)
                    for h in range(SSM_HG):
                        nc.tensor.matmul(BANK[2 + h // 4][:, (h % 4) * P:(h % 4 + 1) * P],
                                         IDENT[0:32, SSM_HG * g + h:SSM_HG * g + h + 1].to_broadcast([32, P]),
                                         CSR[0:32, tok], start=True, stop=True)
                    nc.tensor.matmul(BANK[4][:, 0:P], xb[:, GT, tok], xb[:, GT + 1, tok], start=True, stop=True)
                    nc.tensor.transpose(BANK[4][:, P:2 * P], xb[:, GT, tok], IDENT)
                    for j in range(GT):
                        mm = nc.tensor.transpose(BANK[5][:, j * P:(j + 1) * P], xb[:, j, tok], IDENT)
                    mm.then_inc(p1_done, 1)
                    if g + 1 < SSM_G:
                        for j in range(sum(FILL[:c]), sum(FILL[:c + 1])):
                            in_tile(g + 1, j)
                    if u >= 1:
                        pe.wait_ge(d_ready, u + 1)
                        unit_sums(u - 1)
                    pe.wait_ge(mce_ready, u + 1)
                    if u >= 1:
                        pe.wait_ge(y_read, u)
                    if c >= 1:
                        pe.wait_ge(s_ready, 3 * g + c)
                    for h in range(SSM_HG):
                        y = BANK[6][64 * (h % 2):64 * (h % 2) + 64, (h // 2) * P:(h // 2 + 1) * P]
                        mm = nc.tensor.matmul(y, XDT[:, h, :], DEC[:, h, :], start=True, stop=(c == 0))
                        if c >= 1:
                            mm = nc.tensor.matmul(y, STATE[:, h * 64:(h + 1) * 64], ECS[:, h, :],
                                                  start=False, stop=True)
                    mm.then_inc(y_done, 1)
                    if c < NT - 1:
                        pe.wait_ge(xf_ready, 3 * g + c + 1)
                        if c >= 1:
                            pe.wait_ge(s_ready, 3 * g + c)
                        nc.tensor.matmul(BANK[7][:, :], BTOK, XF.rearrange("p a b -> p (a b)"),
                                         start=True, stop=True).then_inc(st_done, 1)
            pe.wait_ge(gs_read, UNITS - 1)
            unit_sums(UNITS - 1)
            rest_pe(pe)

        @block.scalar
        def _(act):
            a_step = Count(act, act_step)
            act.wait_ge(loaded, 64)
            act.wait_ge(ones_set, 3)
            act.dma_start(BUCK[0:33, :], A["bucket"]).then_inc(aux_in, 16)
            act.dma_start(REL[0:33, :], A["rel"]).then_inc(aux_in, 16)
            for k in range(KD):
                if k >= 2:
                    act.wait_ge(acc_ready, k)
                nc.scalar.activation(SQ[:, k % 2, :], X[:, k, :], ACT.Square).then_inc(sq_ready, 1)
            norm_scale_act(act, 0)
            dt = Count(act, dt_act)
            dt.step(nc.scalar.activation(ALOG[0:32, :], par("a_log", parts=32), ACT.Exp))
            act.wait_ge(dt_row, 2)
            dt.step(nc.scalar.activation(DTB[0:32, :], DTA[0:32, :], ACT.Abs))
            dt.step(nc.scalar.activation(DTB[0:32, :], DTB[0:32, :], ACT.Exp, scale=-1.0))
            act.wait_ge(dt_row, 3)
            dt.step(nc.scalar.activation(STD[0:32, :], DTC[0:32, :], ACT.Ln))

            def rows(g, j):
                n = GROUP_TILES * g + j
                if j < GT:
                    act.wait_ge(gemm_free, n + 1)
                else:
                    act.wait_ge(conv_ready, (GT + 2) * g + j - GT + 1)
                if g >= 2 and j == 0:
                    act.wait_ge(yb_ready, NT * (g - 1))
                src, dst = (U[:, n % 2, 3:3 + T], ZS[g % 2][:, j, :]) if j < GT else \
                           (CV[:, n % 2, :], XSB[g % 2][:, j - GT, :])
                nc.scalar.activation(dst, src, ACT.Silu).then_inc(row_used, 1)

            for j in range(GROUP_TILES):
                rows(0, j)
                if j < AH:
                    act.wait_ge(brow_done, j + 1)
                    nc.scalar.activation(BROW[:, j, 0:T], BANK[2][:, :], ACT.Copy).then_inc(brow_ready, 1)
                    nc.scalar.activation(BROW[:, j, T:640], BANK[3][:, 0:P], ACT.Copy).then_inc(brow_ready, 1)
            act.wait_ge(brow_ready, 2 * AH)
            act.dma_start(DSCR.rearrange("h p m -> p h m"), BROW).then_inc(brow_out, 16)

            def group_rms(g):
                act.wait_ge(gs_read, NT * (g + 1))
                nc.scalar.activation(STD[:, :], GSS, ACT.Sqrt, bias=EPSC[:, 0:1], scale=1.0 / (GT * P)).then_inc(gstd_ready, 1)

            for g in range(SSM_G):
                for c in range(NT):
                    u = NT * g + c
                    act.wait_ge(p1_done, u + 1)
                    nc.scalar.activation(BTOK, BANK[4][:, P:2 * P], ACT.Copy).then_inc(e_ready, 1)
                    for q in range(2):
                        nc.scalar.activation(ECS[:, 4 * q:4 * q + 4, :],
                                             BANK[2 + q][:, :].rearrange("p (h t) -> p h t", t=P),
                                             ACT.Exp).then_inc(e_ready, 1)
                    act.wait_ge(d_ready, u + 1)
                    nc.scalar.activation(DEC, DEC, ACT.Exp).then_inc(d_exp, 1)
                    nc.scalar.activation(FX, FX, ACT.Exp).then_inc(d_exp, 1)
                    if g + 1 < SSM_G:
                        for j in range(sum(FILL[:c]), sum(FILL[:c + 1])):
                            rows(g + 1, j)
                    act.wait_ge(yb_ready, u + 1)
                    nc.scalar.activation(YSQ, YB[:, GT * g:GT * (g + 1), c * P:(c + 1) * P], ACT.Square).then_inc(gsq_ready, 1)
                    if c == 0 and g >= 1:
                        group_rms(g - 1)
            group_rms(SSM_G - 1)
            rest_act(act)

        @block.vector
        def _(dve):
            step, rs, hr, fr = (Count(dve, s) for s in (dve_step, rs_ready, h_ready, gemm_free))
            nc.vector.memset(ONES[:, :], 1.0).then_inc(ones_set, 1)
            nc.vector.memset(EPSC[:, :], EPS).then_inc(ones_set, 1)
            nc.vector.memset(U[:, :, 0:3], 0.0).then_inc(ones_set, 1)
            dve.wait_ge(ones_set, 3)
            dve.wait_ge(loaded, 64)
            norm_head(dve, hr, "ssm_ln")
            norm_scale_dve(dve, 0, rs)
            r = Count(dve, dt_row)
            dve.wait_ge(dt_done, 1)
            r.step(nc.vector.tensor_tensor(DTA[0:32, :], BANK[6][0:32, :], RS[0:32, :], ALU.mult))
            r.step(nc.vector.tensor_scalar(DTA[0:32, :], DTA[0:32, :], par("dt_bias", parts=32), None, ALU.add))
            dve.wait_ge(dt_act, 3)
            r.step(nc.vector.tensor_scalar(DTC[0:32, :], DTB[0:32, :], 1.0, None, ALU.add))
            r.step(nc.vector.tensor_scalar(CSR[0:32, :], DTC[0:32, :], -1.0, None, ALU.add))
            r.step(nc.vector.tensor_tensor(DTB[0:32, :], DTB[0:32, :], CSR[0:32, :], ALU.subtract))
            r.step(nc.vector.tensor_scalar(DTA[0:32, :], DTA[0:32, :], 0.0, None, ALU.max))
            dve.wait_ge(dt_act, 4)
            r.step(nc.vector.tensor_tensor(DTB[0:32, :], DTB[0:32, :], STD[0:32, :], ALU.add))
            r.step(nc.vector.tensor_tensor(DTR[0:32, :], DTA[0:32, :], DTB[0:32, :], ALU.add))
            r.step(nc.vector.tensor_scalar(DTA[0:32, :], DTR[0:32, :], ALOG[0:32, 0:1], -1.0, ALU.mult, ALU.mult))
            r.step(nc.vector.memset(DTC[0:32, :], 1.0))
            for c in range(NT):
                tok = slice(c * P, (c + 1) * P)
                r.step(nc.vector.tensor_tensor_scan(CSR[0:32, tok], DTC[0:32, tok], DTA[0:32, tok], 0.0,
                                                    ALU.mult, ALU.add))

            cv = Count(dve, conv_ready)

            def rows(g, j):
                n = GROUP_TILES * g + j
                dve.wait_ge(gemm_done, n + 1)
                if n >= 2:
                    dve.wait_ge(row_used, n - 1)
                u = U[:, n % 2, :]
                fr.step(nc.vector.tensor_tensor(u[:, 3:3 + T], BANK[n % 2][:, :], RS[:, :], ALU.mult))
                if j >= GT:
                    conv(dve, step, cv, n % 2, lambda k: par("ssm_conv", 5 * ((GT + 2) * g + j - GT) + k), 4)

            for j in range(GROUP_TILES):
                rows(0, j)
            dve.wait_ge(dtT_done, 1)
            b6 = BANK[6][:, 0:NT * 64].rearrange("p (c w) -> p c w", w=64)
            tt = Count(dve, dt_row)
            tt.n = r.n
            tt.step(nc.vector.tensor_copy(DTT, b6[:, :, 0:32]))
            tt.step(nc.vector.tensor_copy(CSTK, b6[:, :, 32:64]))
            mce, xf, yr, yb, sr, dr, yn = (Count(dve, s) for s in (mce_ready, xf_ready, y_read, yb_ready, s_ready,
                                                                  d_ready, yn_ready))

            gsr = Count(dve, gs_read)

            def square_sums(u):
                dve.wait_ge(usum_done, u + 1)
                gsr.step(nc.vector.tensor_copy(GSS[:, u % NT * P:(u % NT + 1) * P], BANK[4][:, 2 * P:3 * P]))

            def group_norm(g):
                dve.wait_ge(gstd_ready, g + 1)
                rs.step(nc.vector.reciprocal(RSG[:, :], STD[:, :]))
                for k in range(GT * g, GT * (g + 1)):
                    yn.step(nc.vector.scalar_tensor_tensor(YB[:, k, :], YB[:, k, :], par("ssm_norm", k), RSG[:, :],
                                                           ALU.mult, ALU.mult))

            for g in range(SSM_G):
                xb = XSB[g % 2]
                heads = slice(SSM_HG * g, SSM_HG * (g + 1))
                for c in range(NT):
                    u = NT * g + c
                    tok = slice(c * P, (c + 1) * P)
                    xdt, x_f, dec, ecs, fx, etot = XDT, XF, DEC, ECS, FX, ETOT
                    dve.wait_ge(p1_done, u + 1)
                    step.step(nc.vector.tensor_tensor(xdt, BANK[5][:, :].rearrange("p (h d) -> p h d", d=64),
                                                      DTT[:, c, heads].unsqueeze(2).to_broadcast([P, SSM_HG, 64]), ALU.mult))
                    dve.wait_ge(e_ready, 3 * u + 1)
                    step.step(nc.vector.tensor_tensor(CBM, BANK[4][:, 0:P], const("causal_st"), ALU.mult))
                    dve.wait_ge(e_ready, 3 * u + 3)
                    for q in range(2):
                        step.step(nc.vector.tensor_copy(etot[:, 4 * q:4 * q + 4], BANK[2 + q][:, P - 1:T:P]))
                    step.step(nc.vector.tensor_tensor(fx, etot, CSTK[:, c, heads], ALU.subtract))
                    for h in range(SSM_HG):
                        ins = nc.vector.tensor_scalar(dec[:, h, :], BANK[2 + h // 4][:, (h % 4) * P:(h % 4 + 1) * P],
                                                      CSTK[:, c, SSM_HG * g + h:SSM_HG * g + h + 1], 0.0,
                                                      ALU.subtract, ALU.min)
                    dr.step(ins)
                    dve.wait_ge(d_exp, 2 * u + 2)
                    step.step(nc.vector.tensor_tensor(dec, dec, CBM.unsqueeze(1).to_broadcast([P, SSM_HG, P]), ALU.mult))
                    step.step(nc.vector.tensor_copy(etot, ecs[:, :, P - 1]))
                    mce.step(nc.vector.tensor_tensor(ecs, ecs, xb[:, GT + 1, tok].unsqueeze(1).to_broadcast([P, SSM_HG, P]),
                                                     ALU.mult))
                    if c < NT - 1:
                        xf.step(nc.vector.tensor_tensor(x_f, xdt, fx.unsqueeze(2).to_broadcast([P, SSM_HG, 64]), ALU.mult))
                    if g + 1 < SSM_G:
                        for j in range(sum(FILL[:c]), sum(FILL[:c + 1])):
                            rows(g + 1, j)
                    if u >= 1:
                        square_sums(u - 1)
                    step.step(nc.vector.tensor_tensor(TMPY, xb[:, 0:GT, tok],
                                                      par("ssm_d", GT * g, GT).unsqueeze(2).to_broadcast([P, GT, P]), ALU.mult))
                    dve.wait_ge(y_done, u + 1)
                    yr.step(nc.vector.tensor_tensor(TMPY, TMPY, BANK[6][:, :].rearrange("p (j t) -> p j t", t=P), ALU.add))
                    if u == 0:
                        dve.wait_ge(brow_out, 16)
                    yb.step(nc.vector.tensor_tensor(YB[:, GT * g:GT * (g + 1), tok], TMPY, ZS[g % 2][:, :, tok], ALU.mult))
                    if c < NT - 1:
                        dve.wait_ge(st_done, 3 * g + c + 1)
                        st3 = STATE.rearrange("p (h d) -> p h d", d=64)
                        if c == 0:
                            sr.step(nc.vector.tensor_copy(STATE, BANK[7][:, :]))
                        else:
                            step.step(nc.vector.tensor_tensor(st3, st3, etot.unsqueeze(2).to_broadcast([P, SSM_HG, 64]), ALU.mult))
                            sr.step(nc.vector.tensor_tensor(STATE, STATE, BANK[7][:, :], ALU.add))
                    if c == 0 and g >= 1:
                        group_norm(g - 1)
            square_sums(UNITS - 1)
            group_norm(SSM_G - 1)
            rest_dve(dve, step, rs, hr, fr, cv)


def _tiles(v):
    return np.asarray(v).reshape(-1, P).T


def _blocks(w, cells=8):
    k, n = w.shape
    b = w.reshape(k // (cells * P), cells, P, n // P, P).transpose(3, 0, 2, 1, 4)
    return np.ascontiguousarray(b).reshape(-1, P, cells * P)


def _constants():
    c = np.zeros((P, CONST[None]), np.float32)

    def put(name, v):
        a, n = CONST[name]
        c[:, a:a + n] = v.reshape(P, n)

    i = np.arange(P)
    put("ident", np.eye(P))
    put("half_ones", (i[:, None] // 64 == i[None, :] // 64) * 1.0)
    put("causal_st", (i[:, None] <= i[None, :]) * 1.0)
    put("future_neg", (i[None, :] > i[:, None]) * NEG)
    turn = np.zeros((P, P))
    freq = np.zeros(P)
    inv = np.power(np.float32(500000.0), -np.arange(8, dtype=np.float32) * np.float32(2.0 / 16)).astype(np.float32)
    for half in (0, 64):
        for d in range(8):
            turn[half + d + 8, half + d] = -1.0
            turn[half + d, half + d + 8] = 1.0
            freq[half + d] = freq[half + d + 8] = inv[d]
    put("rope_turn", turn)
    put("rope_freq", freq)
    t = np.arange(T).reshape(NT, P)
    seen = (np.arange(NCMP)[None, None, :] * 16 + 31 <= t.T[:, :, None]) * 1.0
    put("cmp_seen", seen)
    put("cmp_neg", (1.0 - seen) * NEG)
    return c


def _bucket_rows():
    n = np.maximum(T - 1 - np.arange(640), 0)
    nf = np.maximum(n, 1).astype(np.float32)
    large = 16 + (np.log(nf / np.float32(16)).astype(np.float32) / np.float32(math.log(8.0)) * np.float32(16)).astype(np.int32)
    bucket = np.where(n < 16, n, np.minimum(large, 31))
    rows = np.zeros((33, 640), np.float32)
    rows[bucket, np.arange(640)] = 1.0
    rows[32] = np.where(T - 1 - np.arange(640) < 0, NEG, 0.0)
    return rows


def _arrays(d):
    d = {k: np.asarray(v) for k, v in d.items()}
    f32 = np.float32
    par = np.zeros((P, PARAM[None]), f32)

    def put(name, v):
        a, n = PARAM[name]
        par[:v.shape[0], a:a + n] = v.reshape(v.shape[0], n)

    def conv(w, b, order):
        v = np.concatenate([w, b[None]], 0)[:, order]
        return v.reshape(v.shape[0], -1, P).transpose(2, 1, 0)

    for name, v in (("ssm_ln", d["ssm_ln_g"][0]), ("kv_ln", d["kv_ln_g"]), ("attn_ln", d["attn_ln_g"][0]),
                    ("ffn_ln0", d["ffn_ln_g"][0]), ("ffn_ln1", d["ffn_ln_g"][1]), ("norm2", d["norm_g_2"][0]),
                    ("final", d["final_norm_g_2"]), ("ssm_d", np.repeat(d["ssm_d"][0], 64)),
                    ("ssm_norm", d["ssm_norm_g"][0]), ("k_norm", np.tile(d["k_norm_g"], 2)),
                    ("q_norm", np.tile(d["q_norm_g"][0], 2)), ("subln", d["subln_g"][0]),
                    ("mh_norm", d["mh_norm_g_2"][0])):
        put(name, _tiles(v))
    z0, x0, b0, c0 = 0, 2048, 4096, 4608
    groups = [np.concatenate([z0 + 512 * g + np.arange(512), x0 + 512 * g + np.arange(512),
                              b0 + 128 * g + np.arange(128), c0 + 128 * g + np.arange(128)]) for g in range(4)]
    put("ssm_conv", conv(d["ssm_conv_w"][0], d["ssm_conv_b"][0], np.concatenate([g[512:] - 2048 for g in groups])))
    ffo = (np.arange(22)[:, None, None] * P + np.arange(2)[None, :, None] * 2816 + np.arange(P)).reshape(-1)
    for i in range(2):
        put(f"ffn_conv{i}", conv(d["ffn_conv_w"][i], d["ffn_conv_b"][i], ffo))
    put("qk_conv", np.concatenate([conv(d["conv_q_w_2"][0], d["conv_q_b_2"][0], np.arange(1024)),
                                   conv(d["conv_k_w_2"][0], d["conv_k_b_2"][0], np.arange(1024))], 1))
    gate = np.zeros((P, 1), f32)
    gate[0:4, 0] = d["b_igate_2"][0]
    gate[32:36, 0] = d["b_fgate_2"][0]
    gate[64:88, 0] = d["b_nsa_gate_2"][0]
    put("gate_bias", gate)
    put("dt_bias", d["ssm_dt_bias"][0][:, None])
    put("a_log", d["ssm_a_log"][0][:, None])
    put("cmp_pos", np.tile(np.concatenate([d["cmp_pos_k_2"][0].T, d["cmp_pos_v_2"][0].T], 1), (2, 1)))
    put("lam", np.tile(d["lam_vecs"][0].reshape(1, 256), (P, 1)))

    w2 = d["w_in_2"][0]
    small = np.zeros((1024, 120), f32)
    small[:, 0:32] = d["ssm_in_w"][0][:, 5120:5152]
    small[:, 32:36] = w2[:, 5120:5124]
    small[:, 64:68] = w2[:, 5124:5128]
    nq, nz, ng = 5128, 5128 + 512 + 768 + 24, 5128 + 512 + 768
    small[:, 96:120] = w2[:, ng:ng + 24]
    kc, vc, ks, vs, kw, vw = (5640 + 128 * i + np.arange(128) for i in range(6))
    pair = np.concatenate([np.concatenate([64 * j + np.arange(64), 64 * (j + 4) + np.arange(64)]) for j in range(4)])
    m = [np.arange(1024) + 1024 * i for i in range(5)]
    ga = nz + 512 + np.arange(1024)
    head = [np.concatenate([x[256 * h:256 * h + 256] for x in m]) for h in range(4)]
    order = np.concatenate(head + [nq + pair, kc, vc, ks, kw, vs, vw, nz + pair, ga, ga + 1024])
    kvw = d["kv_w"]
    kvq = np.concatenate([np.concatenate([kvw[:, 128 * h:128 * h + 128], kvw[:, 1024 + 128 * h:1152 + 128 * h],
                                          d["q_w"][0][:, 128 * h:128 * h + 128]], 1) for h in range(8)], 1)
    wa, wb = _blocks(d["w_branch_a_2"][0]), _blocks(d["w_branch_b_2"][0][pair], 4)
    ab = np.zeros((16, P, 8 * P), f32)
    ab[0::2], ab[1::2, :, 0:4 * P] = wa, wb
    return {
        "const": _constants(), "param": par, "bucket": _bucket_rows(),
        "rel": np.concatenate([d["rel_bias"], np.ones((1, 8), f32)], 0),
        "pos": np.broadcast_to(d["positions_2"].reshape(1, T), (P, T)),
        "xT": d["x"][0].T.reshape(KD, P, T).transpose(1, 0, 2),
        "small": small.reshape(KD, P, 120).transpose(1, 0, 2),
        "in_w": _blocks(d["ssm_in_w"][0][:, np.concatenate(groups)]), "out_w": _blocks(d["ssm_out_w"][0]),
        "up0": _blocks(d["ffn_up_w"][0][:, ffo]), "down0": _blocks(d["ffn_down_w"][0], 11),
        "kvq": _blocks(kvq), "attn_out": _blocks(d["attn_out_w"][0]),
        "up1": _blocks(d["ffn_up_w"][1][:, ffo]), "down1": _blocks(d["ffn_down_w"][1], 11),
        "w_in2": _blocks(w2[:, order]), "ab": ab, "w_out2": _blocks(d["w_out_2"][0]),
        "cmp_w1": np.stack([np.tile(d[f"cmp_w1_{x}_2"][0].reshape(CMPL, 64, P).transpose(1, 0, 2), (2, 1, 1))
                            for x in "kv"], 0),
        "cmp_w2": np.concatenate([d["cmp_w2_k_2"][0], d["cmp_w2_v_2"][0]], 1),
    }


def kernel(**inputs):
    import concourse.bacc as bacc
    from concourse.bass_utils import run_bass_kernel_spmd

    nc = bacc.Bacc("TRN2", target_bir_lowering=False, num_devices=1)
    arrays = {f"{k}_dram": np.ascontiguousarray(v) for k, v in _arrays(inputs).items()}
    aps = {k[:-5]: nc.dram_tensor(k, v.shape, mybir.dt.from_np(v.dtype), kind="ExternalInput").ap()
           for k, v in arrays.items()}
    out = nc.dram_tensor("out_dram", (P, KD, T), F32, kind="ExternalOutput").ap()
    three_parts(nc, aps, out)
    r = run_bass_kernel_spmd(nc, [arrays], core_ids=[0])
    return r.results[0]["out_dram"].transpose(1, 0, 2).reshape(1, DM, T).transpose(0, 2, 1)
```

```python
import concourse.bass as bass
from concourse import mybir
from contextlib import ExitStack
import numpy as np
import math

F32 = mybir.dt.float32
F32R = mybir.dt.float32r
ACT = mybir.ActivationFunctionType
ALU = mybir.AluOpType
AX = mybir.AxisListType

T = 512
P = 128
NT = T // P
DM = 1024
KD = DM // P
SSM_G, SSM_HG = 4, 8
SSM_H = SSM_G * SSM_HG
GT = 4
GROUP_TILES = 2 * GT + 2
FF_TILES = 22
AH = 8
MH = 4
NP_ = 4
NCMP = (T - 32) // 16 + 1
CMPL = 32
EPS = 1e-6
NEG = -1e30
LAM_INIT = 0.8 - 0.6 * math.exp(-0.3)
TURN = 4
SLOTS = 2
CELLS = 11


def layout(spec):
    at, out = 0, {}
    for name, n in spec:
        out[name] = (at, n)
        at += n
    out[None] = at
    return out


CONST = layout([("ident", P), ("half_ones", P), ("causal_st", P), ("future_neg", P), ("rope_turn", P),
                ("rope_freq", 1), ("cmp_seen", NT * NCMP), ("cmp_neg", NT * NCMP)])
PARAM = layout([("ssm_ln", KD), ("kv_ln", KD), ("attn_ln", KD), ("ffn_ln0", KD), ("ffn_ln1", KD),
                ("norm2", KD), ("final", KD), ("ssm_d", 16), ("ssm_norm", 16), ("k_norm", 1),
                ("q_norm", 1), ("subln", 1), ("mh_norm", 8), ("ssm_conv", 24 * 5),
                ("ffn_conv0", 44 * 4), ("ffn_conv1", 44 * 4), ("qk_conv", 16 * 5),
                ("gate_bias", 1), ("dt_bias", 1), ("a_log", 1), ("cmp_pos", 2 * CMPL), ("lam", 256)])


class Count:

    def __init__(self, eng, sem):
        self.eng, self.sem, self.n, self.k = eng, sem, 0, 0

    def step(self, ins):
        ins.then_inc(self.sem, 1)
        self.n = self.n + 1
        self.k += 1
        self.eng.wait_ge(self.sem, self.n)

    def enter(self, i, per):
        self.base, self.per, self.k = self.n, per, 0
        self.n = i * per + self.base

    def leave(self, turns):
        assert self.k == self.per, (self.k, self.per)
        self.n = self.base + turns * self.per


def three_parts(nc, A, out):
    ctx = ExitStack()
    with ctx:
        def sb(name, shape, dt=F32):
            return ctx.enter_context(nc.sbuf_tensor(name, shape, dt))

        def sem(name):
            return ctx.enter_context(nc.semaphore(name))

        X = sb("residual", [P, KD, T])
        HH = sb("scaled_in_high", [P, KD, T], F32R)
        HL = sb("scaled_in_low", [P, KD, T], F32R)
        RAW = sb("weight_ring", [P, SLOTS, CELLS * P])
        WH = sb("weights_high", [P, SLOTS, CELLS * P], F32R)
        WL = sb("weights_low", [P, SLOTS, CELLS * P], F32R)
        SQ = sb("squares", [P, 2, T])
        ACC = sb("square_sums", [P, T])
        RS = sb("inv_rms", [P, T])
        STD = sb("rms", [P, T])
        CST = sb("constants", [P, CONST[None]])
        PAR = sb("params", [P, PARAM[None]])
        ONES = sb("ones", [P, P])
        FLAT = sb("small_buffers", [P, 400])
        ONEHOT = sb("identity_for_one_pass", [P, P], F32R)
        FUTURE = sb("future_for_one_pass", [P, P], F32R)
        EPSC = sb("eps_column", [P, 1])
        UNUSED = sb("unused_exp", [P, 1])
        U = sb("padded_rows", [P, 2, T + 4])
        CV = sb("conv_rows", [P, 2, T])
        EMB = sb("floor", [P, T])
        RDB = sb("reciprocals", [P, T])
        AREA = 23860
        with ExitStack() as plain:
            ARENA = plain.enter_context(nc.sbuf_tensor("arena", [P, AREA], F32))
        with ExitStack() as ffn_parts:
            FFH = ffn_parts.enter_context(nc.sbuf_tensor("gated_high", [P, FF_TILES, T], F32R))
            FFL = ffn_parts.enter_context(nc.sbuf_tensor("gated_low", [P, FF_TILES, T], F32R))
        with ExitStack() as query_parts:
            HQH = query_parts.enter_context(nc.sbuf_tensor("query_in_high", [P, KD, T], F32R))
            HQL = query_parts.enter_context(nc.sbuf_tensor("query_in_low", [P, KD, T], F32R))
        BANK = [ctx.enter_context(nc.psum_tensor(f"bank{i}", [P, T], F32)) for i in range(8)]

        def const(name, parts=P):
            a, n = CONST[name]
            return CST[0:parts, a:a + n]

        def par(name, i=0, n=1, parts=P):
            a, _ = PARAM[name]
            return PAR[0:parts, a + i:a + i + n]

        class Carve:

            def __init__(self):
                self.at = 0

            def __call__(self, *shape):
                n = int(np.prod(shape))
                v = ARENA[:, self.at:self.at + n]
                self.at += n
                assert self.at <= AREA, self.at
                if len(shape) == 2:
                    v = v.rearrange("p (a b) -> p a b", b=shape[1])
                if len(shape) == 3:
                    v = v.rearrange("p (a b c) -> p a b c", b=shape[1], c=shape[2])
                return v

        IDENT = const("ident")

        loaded = sem("constants_in")
        params_in = sem("params_in")
        sq_used = sem("squares_used")
        x_in = [sem(f"input_tiles{2 * i}_{2 * i + 1}") for i in range(KD // 2)]
        masks_set = sem("one_pass_constants_set")
        w_ready = [sem(f"weights_in_slot{i}") for i in range(SLOTS)]
        high_ready = sem("weights_high_ready")
        split_done = sem("weights_split")
        acc_ready = sem("square_sums_ready")
        gemm_done = sem("gemm_tile_done")
        half_done = sem("first_block_used")
        gemm_free = sem("gemm_bank_read")
        ones_set = sem("ones_set")
        h_ready = sem("scaled_in_ready")
        ff_ready = sem("gated_ready")
        sq_ready = sem("squares_ready")
        ssq_done = sem("square_sum_done")
        std_ready = sem("rms_ready")
        rs_ready = sem("inv_rms_ready")
        row_used = sem("tile_rows_used")
        conv_ready = sem("tile_rows_ready")
        exp_set = sem("exp_tables_asked_for")
        dve_step = sem("dve_step")
        dt_row = sem("dt_rows_step")
        dt_act = sem("dt_act_step")
        dtT_done = sem("dt_turned")
        p1_done = sem("ssd_inputs_done")
        e_ready = sem("ssd_exps_of_sums")
        d_ready = sem("ssd_exponents_ready")
        d_exp = sem("ssd_decay_ready")
        mce_ready = sem("ssd_operands_ready")
        xf_ready = sem("ssd_state_input_ready")
        y_done = sem("ssd_y_done")
        st_done = sem("ssd_state_done")
        y_read = sem("ssd_y_read")
        s_ready = sem("ssd_state_ready")
        yb_ready = sem("ssd_y_ready")
        gsq_ready = sem("group_squares_ready")
        usum_done = sem("unit_square_sum_done")
        gs_read = sem("unit_square_sum_read")
        aux_in = sem("bucket_rows_in")
        brow_done = sem("bias_row_done")
        brow_ready = sem("bias_row_ready")
        brow_out = sem("bias_rows_in_dram")
        DSCR = nc.dram_tensor("bias_scratch", (AH, P, 640), F32, kind="Internal").ap()
        gstd_ready = sem("group_rms_ready")
        yn_ready = sem("normed_y_ready")

        block = ctx.enter_context(nc.Block())

        STREAM = [("dt_w", 1, 8, 1, True), ("in_w", 40, 8, 1, True), ("out_a", 8, 8, 1, False), ("out_b", 8, 8, 1, False), ("up0", 44, 8, 1, True), ("down0", 16, 11, 2, True),
                  ("kvq", 24, 8, 1, True), ("attn_out", 8, 8, 1, True), ("up1", 44, 8, 1, True), ("down1", 16, 11, 2, True),
                  ("gates_w", 1, 8, 1, True), ("w_in2", 70, 8, 1, True), ("ab", 16, 8, 1, False), ("w_out2", 8, 8, 1, True)]
        BASE, TILE0, HALF0, PART0 = {}, {}, {}, {}
        b = t = h = q = 0
        for name, n, cells, per, parts in STREAM:
            BASE[name], TILE0[name], HALF0[name], PART0[name] = b, t, h, q
            b, t, h, q = b + n, t + n // per, h + (n // 2 if per == 2 else 0), q + (n if parts else 0)
        PARTED = {x[0]: x[4] for x in STREAM}

        def raw_slot(name, k):
            return (BASE[name] + k) % SLOTS

        def part_slot(name, k):
            return (PART0[name] + k) % SLOTS

        def products_done(name, per, k, i=0):
            if per == 1:
                return gemm_done, TILE0[name] + k + 1 + i * TURN
            if k % 2 == 0:
                return half_done, HALF0[name] + k // 2 + 1 + i * (TURN // 2)
            return gemm_done, TILE0[name] + k // 2 + 1 + i * (TURN // 2)

        def loaded_used(name, per, k, i=0):
            if PARTED[name]:
                return split_done, PART0[name] + k + 1 + i * TURN
            return products_done(name, per, k, i)

        def gemm_tile(pe, name, i, j, rhs, cells=8, per=1, only=None):
            turn = TURN // per
            n = TILE0[name] + j + i * turn
            bank = BANK[(TILE0[name] + j) % 2][:, :]
            if TILE0[name] + j >= 2 and (only is None or 0 in only):
                pe.wait_ge(gemm_free, n - 1)
            for part in range(per):
                k0 = per * j + part
                slot = (part_slot if PARTED[name] else raw_slot)(name, k0)
                if PARTED[name]:
                    pe.wait_ge(split_done, PART0[name] + k0 + 1 + i * TURN)
                else:
                    pe.wait_ge(w_ready[slot], (BASE[name] + k0) // SLOTS * 16 + 16 + i * (16 * TURN // SLOTS))
                for c in only or range(cells):
                    k = part * cells + c
                    first, last = k == 0, k == per * cells - 1
                    cell = slice(c * P, (c + 1) * P)
                    if PARTED[name]:
                        high, low = rhs(k)
                        nc.tensor.matmul(bank, WH[:, slot, cell], high, start=first, stop=False)
                        nc.tensor.matmul(bank, WH[:, slot, cell], low, start=False, stop=False)
                        mm = nc.tensor.matmul(bank, WL[:, slot, cell], high, start=False, stop=last)
                    else:
                        mm = nc.tensor.matmul(bank, RAW[:, slot, cell], rhs(k), start=first, stop=last)
                if part < per - 1:
                    mm.then_inc(half_done, 1)
            if only is None or cells - 1 in only:
                mm.then_inc(gemm_done, 1)

        def scaled_in(pe, turn):
            def rhs(k):
                pe.wait_ge(h_ready, 2 * (KD * turn + k + 1))
                return HH[:, k, :], HL[:, k, :]
            return rhs

        def norm_sum(pe, turn):
            pe.wait_ge(acc_ready, (KD + 1) * (turn + 1))
            nc.tensor.matmul(BANK[7][:, :], ONES[:, :], ACC[:, :], start=True, stop=True).then_inc(ssq_done, 1)

        def split_scaled(hr, high, low, x, gain):
            hr.step(nc.vector.tensor_scalar(high, x, gain, None, ALU.mult))
            hr.step(nc.vector.scalar_tensor_tensor(low, x, gain, high.bitcast(F32), ALU.mult, ALU.subtract))

        def add_squares(dve, ac, turn, k, sq):
            dve.wait_ge(sq_ready, k + (KD * turn + 1))
            ac.step(nc.vector.tensor_tensor(ACC[:, :].unsqueeze(1), ACC[:, :].unsqueeze(1), sq, ALU.add))

        def norm_scale_act(act, turn):
            act.wait_ge(ssq_done, turn + 1)
            nc.scalar.activation(STD[:, :], BANK[7][:, :], ACT.Sqrt, bias=EPSC[:, 0:1],
                                 scale=1.0 / DM).then_inc(std_ready, 1)

        def norm_scale_dve(dve, turn, rs):
            dve.wait_ge(std_ready, turn + 1)
            rs.step(nc.vector.reciprocal(RS[:, :], STD[:, :]))

        def exp_tables(ahead):
            ahead.step(nc.scalar.activation(UNUSED[:, :], EPSC[:, :], ACT.Exp))

        def conv(dve, step, done, b, taps_and_bias, taps, out=None):
            u, y = U[:, b, :], CV[:, b, :] if out is None else out
            step.step(nc.vector.tensor_scalar(y, u[:, 3:3 + T], taps_and_bias(taps - 1), taps_and_bias(taps),
                                              ALU.mult, ALU.add))
            for k in range(taps - 1):
                at = 3 - (taps - 1) + k
                (done if k == taps - 2 else step).step(nc.vector.scalar_tensor_tensor(
                    y, u[:, at:at + T], taps_and_bias(k), y, ALU.mult, ALU.add))

        mb = Carve()
        YB = mb(4 * GT, T)
        ZS = [mb(GT, T) for _ in range(2)]
        XSB = [mb(GT + 2, T) for _ in range(2)]
        XDT = mb(SSM_HG, 64)
        XF = mb(SSM_HG, 64)
        DEC = mb(SSM_HG, P)
        ECS = mb(SSM_HG, P)
        CBM = mb(P)
        BTOK = mb(P)
        FX = mb(SSM_HG)
        ETOT = mb(SSM_HG)
        STATE = EMB[:, :]
        RSG = RDB[:, :]
        TMPY = ACC[:, :].rearrange("p (j t) -> p j t", t=P)
        YSQ = SQ[:, 0, :].rearrange("p (j t) -> p j t", t=P)
        GSS = SQ[:, 1, :]
        DTR = mb(T)
        CSR = mb(T)
        DTA, DTB, DTC = (YB[:, i, :] for i in range(3))
        ALOG = mb(1)
        DTT = mb(NT, 32)
        CSTK = mb(NT, 32)
        UNITS = SSM_G * NT
        FILL = [3, 2, 3, 2]

        bb = Carve()
        bb.at = 3 * T
        BROW = bb(AH, 640)
        BUCK = bb(640)
        REL = bb(AH)


        def add_pe(pe, name, rhs, cells, ready=None):
            per = 2 if name in ("down0", "down1") else 1
            turn = TURN // per
            with pe.Fori(0, KD // turn) as i:
                for j in range(turn):
                    gemm_tile(pe, name, i, j, lambda k: rhs(pe, k, j), cells, per)

        def add_act(act, name, turn):
            with act.Fori(0, KD // 2) as i:
                for j in range(2):
                    act.wait_ge(gemm_free, i * 2 + (TILE0[name] + j + 1))
                    act.wait_ge(acc_ready, i * 2 + ((KD + 1) * turn + j))
                    nc.scalar.activation(SQ[:, j:j + 1, :], X[:, bass.ds(i * 2 + j, 1), :], ACT.Square).then_inc(sq_ready, 1)
            norm_scale_act(act, turn)

        def add_dve(dve, name, turn, gains, hr, fr, rs, meanwhile=None):
            ac = Count(dve, acc_ready)
            ac.n = (KD + 1) * turn
            ac.step(nc.vector.memset(ACC[:, :], 0.0))
            with dve.Fori(0, KD // 2) as i:
                fr.enter(i, 2)
                hr.enter(i, 4 if gains else 0)
                ac.enter(i, 2)
                for j in range(2):
                    k = i * 2 + j
                    dve.wait_ge(gemm_done, i * 2 + (TILE0[name] + j + 1))
                    x = X[:, bass.ds(k, 1), :]
                    fr.step(nc.vector.tensor_tensor(x, x, BANK[(TILE0[name] + j) % 2][:, :].unsqueeze(1), ALU.add))
                    if gains:
                        split_scaled(hr, HH[:, bass.ds(k, 1), :], HL[:, bass.ds(k, 1), :], x,
                                     PAR[:, bass.ds(k + PARAM[gains][0], 1)])
                    add_squares(dve, ac, turn, k, SQ[:, j:j + 1, :])
                fr.leave(KD // 2)
                hr.leave(KD // 2)
                ac.leave(KD // 2)
            if meanwhile:
                meanwhile()
            norm_scale_dve(dve, turn, rs)

        ff = Carve()
        ff.at = FF_TILES * T * 2
        GATE = ff(T)

        def ffn_pe(pe, layer):
            turn = 2 * layer + 1
            for j in range(TURN):
                gemm_tile(pe, f"up{layer}", 0, j, scaled_in(pe, turn) if j == 0 else lambda k: (HH[:, k, :], HL[:, k, :]))
                if j == 0:
                    norm_sum(pe, turn)
            with pe.Fori(1, 2 * FF_TILES // TURN) as i:
                for j in range(TURN):
                    gemm_tile(pe, f"up{layer}", i, j, lambda k: (HH[:, k, :], HL[:, k, :]))

            def gated(pe, k, j):
                if j == 0 and (k == 0 or k >= FF_TILES - 3):
                    pe.wait_ge(ff_ready, 2 * (FF_TILES * layer + max(k + 1, FF_TILES - 3)))
                return FFH[:, k, :], FFL[:, k, :]
            add_pe(pe, f"down{layer}", gated, 11)

        def ffn_act(act, layer):
            c0, _ = COUNT0[f"conv{layer}"]
            with act.Fori(0, FF_TILES) as m:
                act.wait_ge(conv_ready, m + (c0 + 1))
                nc.scalar.activation(GATE, CV[:, 0, :], ACT.Silu).then_inc(row_used, 1)
            add_act(act, f"down{layer}", 2 * layer + 2)

        def ffn_dve(dve, layer, gains, step, rs, hr, fr, cv, meanwhile=None):
            name = f"up{layer}"
            _, r0 = COUNT0[f"conv{layer}"]
            ffr = Count(dve, ff_ready)
            ffr.n = 2 * FF_TILES * layer
            a, _ = PARAM[f"ffn_conv{layer}"]
            with dve.Fori(0, FF_TILES // 2) as i:
                for c, per in ((fr, 4), (step, 12), (cv, 2), (ffr, 4)):
                    c.enter(i, per)
                for j in range(4):
                    b = j % 2
                    dve.wait_ge(gemm_done, i * 4 + (TILE0[name] + j + 1))
                    if b == 0:
                        dve.wait_ge(row_used, i * 2 + (r0 + j // 2))
                    fr.step(nc.vector.tensor_tensor(U[:, b, 3:3 + T], BANK[(TILE0[name] + j) % 2][:, :], RS[:, :], ALU.mult))
                    conv(dve, step, cv if b == 0 else step, b,
                         lambda k: PAR[:, bass.ds(i * 16 + (a + 4 * j + k), 1)], 3)
                    if b == 1:
                        dve.wait_ge(row_used, i * 2 + (r0 + j // 2 + 1))
                        product = CV[:, 1:2, :]
                        high, low = (f[:, bass.ds(i * 2 + j // 2, 1), :] for f in (FFH, FFL))
                        step.step(nc.vector.tensor_tensor(product, product, GATE.unsqueeze(1), ALU.mult))
                        ffr.step(nc.vector.tensor_copy(high, product))
                        ffr.step(nc.vector.tensor_tensor(low, product, high.bitcast(F32), ALU.subtract))
                for c in (fr, step, cv, ffr):
                    c.leave(FF_TILES // 2)
            add_dve(dve, f"down{layer}", 2 * layer + 2, gains, hr, fr, rs, meanwhile)

        at = Carve()
        at.at = 2 * KD * T
        BIAS = at(AH, T)
        OH = at(AH, T)
        KN = [at(T) for _ in range(2)]
        QN = [at(T) for _ in range(2)]
        VT = [at(NT, P) for _ in range(2)]
        PR = [[at(T) for _ in range(2)] for _ in range(2)]
        ATT = [at(T) for _ in range(2)]
        OB = at(T)
        SQO = ACC[:, :]
        NM = [at(2) for _ in range(2)]
        SUMS = [at(2) for _ in range(2)]
        KSTD, KRMS, QSTD, QRMS = (at(NT, 2) for _ in range(4))
        KCOLS = at(NT, P)
        OSTD, ORMS = at(NT), at(NT)
        LAM = at(72)

        bias_in = sem("bias_table_in")
        hq_ready = sem("query_in_ready")
        lam_step = sem("lambda_step")
        lam_exp = sem("lambda_exps")
        lam_act = sem("lambda_act_step")
        hsq = sem("head_squares_ready")
        hss = sem("head_square_sum_done")
        hstd = sem("head_rms_ready")
        rk_ready = sem("k_inv_rms_ready")
        rq_ready = sem("q_inv_rms_ready")
        ro_ready = sem("out_inv_rms_ready")
        kb_done = sem("k_inv_rms_spread")
        outb_done = sem("out_inv_rms_spread")
        kq_ready = sem("head_k_ready")
        vt_done = sem("v_turned")
        v_ready = sem("v_ready")
        s_done = sem("scores_done")
        l_ready = sem("logits_ready")
        p_ready = sem("exps_ready")
        a_ready = sem("attn_ready")
        t_done = sem("attn_turned")
        t_ready = sem("attn_turned_ready")
        o_done = sem("attn_out_done")
        ob_ready = sem("head_out_ready")
        oss_done = sem("head_out_square_sum")
        ostd_ready = sem("head_out_rms")
        oh_ready = sem("head_out_normed")

        def attention_pe(pe):
            def tile(h, j, only=None):
                def rhs(k):
                    if h == 0 and j == 2:
                        pe.wait_ge(hq_ready, 2 * (k + 1))
                    return (HQH[:, k, :], HQL[:, k, :]) if j == 2 else (HH[:, k, :], HL[:, k, :])
                gemm_tile(pe, "kvq", 0, 3 * h + j, rhs, only=only)

            def quarter(h, i):
                for j in range(3):
                    cells = [c - 8 * j for c in range(6 * i, 6 * i + 6) if 0 <= c - 8 * j < 8]
                    if cells and h < AH:
                        tile(h, j, cells)

            def head_sums(h, which):
                if which == 0 and h >= 1:
                    pe.wait_ge(kq_ready, h)
                if which == 1 and h >= 2:
                    pe.wait_ge(ostd_ready, h - 1)
                pe.wait_ge(hsq, 2 * h + which + 1)
                for c in range(NT):
                    at = 8 * which + 2 * c
                    mm = nc.tensor.matmul(BANK[6 + which][:, at:at + 2], SQ[:, which, c * P:(c + 1) * P],
                                          const("half_ones")[:, 0:P:64], start=True, stop=True)
                mm.then_inc(hss, 1)

            def spread_k(h):
                pe.wait_ge(rk_ready, 2 * h + 2)
                pe.wait_ge(v_ready, h + 1)
                for c in range(NT):
                    mm = nc.tensor.matmul(BANK[6][:, c * P:(c + 1) * P], KCOLS[:, c, :],
                                          IDENT, start=True, stop=True)
                mm.then_inc(kb_done, 1)

            def spread_out(h):
                pe.wait_ge(ro_ready, h + 1)
                pe.wait_ge(hstd, 2 * min(h + 3, AH))
                for c in range(NT):
                    mm = nc.tensor.matmul(BANK[7][:, c * P:(c + 1) * P], ORMS[:, c:c + 1].to_broadcast([P, P]),
                                          IDENT, start=True, stop=True)
                mm.then_inc(outb_done, 1)

            def turn_v(h):
                pe.wait_ge(hstd, 2 * h + 1)
                pe.wait_ge(gemm_free, TILE0["kvq"] + 3 * h + 2)
                for c in range(NT):
                    mm = nc.tensor.transpose(BANK[6][:, c * P:(c + 1) * P], U[:, 1, 3 + c * P:3 + (c + 1) * P], IDENT)
                mm.then_inc(vt_done, 1)

            def scores(h, i):
                w = NT * h + i
                if w >= 1:
                    pe.wait_ge(l_ready, w)
                pe.wait_ge(kq_ready, h + 1)
                n = (i + 1) * P
                for c in range(2):
                    mm = nc.tensor.matmul(BANK[2 + c][:, 0:n], QN[h % 2][64 * c:64 * c + 64, i * P:(i + 1) * P],
                                          KN[h % 2][64 * c:64 * c + 64, 0:n], start=True, stop=True)
                mm.then_inc(s_done, 1)

            def turn_attn(h, i):
                w = NT * h + i
                pe.wait_ge(a_ready, w + 1)
                if w >= 1:
                    pe.wait_ge(t_ready, w)
                for kb in range(i + 1):
                    mm = nc.tensor.transpose(BANK[4][:, kb * P:(kb + 1) * P], PR[w % 2][0][:, kb * P:(kb + 1) * P], IDENT)
                mm.then_inc(t_done, 1)

            def attn_v(h, i):
                w = NT * h + i
                pe.wait_ge(t_ready, w + 1)
                pe.wait_ge(v_ready, h + 1)
                if i == 0 and h >= 1:
                    pe.wait_ge(ob_ready, 2 * h)
                for kb in range(i + 1):
                    mm = nc.tensor.matmul(BANK[5][:, i * P:(i + 1) * P], VT[h % 2][:, kb, :],
                                          ATT[w % 2][:, kb * P:(kb + 1) * P], start=(kb == 0), stop=(kb == i))
                mm.then_inc(o_done, 1)

            def out_sums(h):
                pe.wait_ge(ob_ready, 2 * h + 2)
                pe.wait_ge(hstd, 2 * min(h + 2, AH))
                if h >= 1:
                    pe.wait_ge(oh_ready, h)
                for c in range(NT):
                    mm = nc.tensor.matmul(BANK[7][:, c:c + 1], SQO[:, c * P:(c + 1) * P], ONES[:, 0:1], start=True, stop=True)
                mm.then_inc(oss_done, 1)

            gemm_tile(pe, "kvq", 0, 0, scaled_in(pe, 2))
            norm_sum(pe, 2)
            tile(0, 1)
            tile(0, 2)
            head_sums(0, 0)
            turn_v(0)
            head_sums(0, 1)
            spread_k(0)
            quarter(1, 0)
            for h in range(AH + 1):
                for i in range(NT):
                    w = NT * h + i
                    quarter(*((h + 1, i + 1) if i < 3 else (h + 2, 0)))
                    if h < AH:
                        scores(h, i)
                    if 1 <= w < NT * AH + 1:
                        turn_attn((w - 1) // NT, (w - 1) % NT)
                    if 2 <= w < NT * AH + 2:
                        attn_v((w - 2) // NT, (w - 2) % NT)
                    if h + 1 < AH:
                        if i == 1:
                            head_sums(h + 1, 0)
                        if i == 2:
                            turn_v(h + 1)
                        if i == 3:
                            spread_k(h + 1)
                            head_sums(h + 1, 1)
                    if i == 2 and h >= 1:
                        out_sums(h - 1)
                    if i == 0 and h >= 2:
                        spread_out(h - 2)
            spread_out(AH - 1)

            def normed(pe, k, j):
                if j == 0:
                    pe.wait_ge(hq_ready, 2 * (KD + k + 1))
                return HQH[:, k, :], HQL[:, k, :]
            add_pe(pe, "attn_out", normed, 8)

        def attention_act(act, ahead):
            la = Count(act, lam_act)
            act.wait_ge(lam_step, 4)
            la.step(nc.scalar.activation(LAM[:, 66:68], LAM[:, 64:66], ACT.Exp))
            act.wait_ge(gemm_free, TILE0["kvq"])
            skewed = bass.AP(tensor=DSCR.tensor, offset=P - 1, ap=[[639, P], [P * 640, AH], [1, T]])
            act.dma_start(BIAS, skewed).then_inc(bias_in, 16)

            def squares(h, which):
                act.wait_ge(gemm_free, TILE0["kvq"] + 3 * h + 1 + 2 * which)
                if h >= 1:
                    act.wait_ge(hss, 2 * h + which - 1)
                nc.scalar.activation(SQ[:, which, :], U[:, 0, 3:3 + T] if which == 0 else QN[h % 2],
                                     ACT.Square).then_inc(hsq, 1)

            def rms(h, which):
                act.wait_ge(hss, 2 * h + which + 1)
                if h >= 1:
                    act.wait_ge(*((rq_ready, 2 * h) if which else (rk_ready, 2 * h)))
                sums = BANK[6 + which][:, 8 * which:8 * which + 8].rearrange("p (c n) -> p c n", n=2)
                nc.scalar.activation(QSTD if which else KSTD, sums, ACT.Sqrt, bias=EPSC[:, 0:1], scale=1.0 / 64).then_inc(hstd, 1)

            def v_out(h):
                act.wait_ge(vt_done, h + 1)
                if h >= 2:
                    act.wait_ge(o_done, NT * (h - 1))
                nc.scalar.activation(VT[h % 2], BANK[6][:, :].rearrange("p (c d) -> p c d", d=P), ACT.Copy).then_inc(v_ready, 1)

            def exps(h, i):
                w = NT * h + i
                act.wait_ge(l_ready, w + 1)
                n = (i + 1) * P
                for c in range(2):
                    p = PR[w % 2][c][:, 0:n]
                    nc.scalar.activation(p, p, ACT.Exp, bias=NM[w % 2][:, c:c + 1],
                                         accum_out=SUMS[w % 2][:, c:c + 1]).then_inc(p_ready, 1)

            def turned(h, i):
                w = NT * h + i
                act.wait_ge(t_done, w + 1)
                if w >= 2:
                    act.wait_ge(o_done, w - 1)
                nc.scalar.activation(ATT[w % 2][:, 0:(i + 1) * P], BANK[4][:, 0:(i + 1) * P], ACT.Copy).then_inc(t_ready, 1)

            def head_out(h):
                act.wait_ge(o_done, NT * (h + 1))
                if h >= 1:
                    act.wait_ge(oh_ready, h)
                nc.scalar.activation(OB, BANK[5][:, :], ACT.Copy).then_inc(ob_ready, 1)
                nc.scalar.activation(SQO, BANK[5][:, :], ACT.Square).then_inc(ob_ready, 1)

            def head_rms(h):
                act.wait_ge(oss_done, h + 1)
                if h >= 1:
                    act.wait_ge(ro_ready, h)
                nc.scalar.activation(OSTD, BANK[7][:, 0:NT], ACT.Sqrt, bias=EPSC[:, 0:1], scale=1.0 / P).then_inc(ostd_ready, 1)

            squares(0, 0)
            squares(0, 1)
            rms(0, 0)
            v_out(0)
            rms(0, 1)
            for h in range(AH + 1):
                for i in range(NT):
                    w = NT * h + i
                    if h + 1 < AH and i in (0, 2):
                        squares(h + 1, i // 2)
                    if 1 <= w < NT * AH + 1:
                        turned((w - 1) // NT, (w - 1) % NT)
                    if i == 1 and h >= 1:
                        head_out(h - 1)
                    if h < AH:
                        exps(h, i)
                    if h + 1 < AH:
                        if i == 1:
                            rms(h + 1, 0)
                            exp_tables(ahead)
                        if i == 2:
                            v_out(h + 1)
                        if i == 3:
                            rms(h + 1, 1)
                            exp_tables(ahead)
                    if i == 2 and h >= 1:
                        head_rms(h - 1)
                        exp_tables(ahead)
            add_act(act, "attn_out", 3)

        QUERY_EARLY = 3

        def split_query():
            hq = Count(nc.vector, hq_ready)
            nc.vector.wait_ge(gemm_done, TILE0["down0"] + KD)
            for k in range(QUERY_EARLY):
                split_scaled(hq, HQH[:, k, :], HQL[:, k, :], X[:, k, :], par("attn_ln", k))

        def attention_dve(dve, step, rs, hr, fr, cv):
            ls, kq, lr, ar, ohr, hq = (Count(dve, s) for s in (lam_step, kq_ready, l_ready, a_ready, oh_ready, hq_ready))
            rk, rq, ro = (Count(dve, s) for s in (rk_ready, rq_ready, ro_ready))
            for m in range(2):
                ls.step(nc.vector.tensor_tensor(LAM[:, 0:64], par("lam", 128 * m, 64), par("lam", 128 * m + 64, 64), ALU.mult))
                ls.step(nc.vector.tensor_reduce(LAM[:, 64 + m:65 + m], LAM[:, 0:64], AX.X, ALU.add))
            dve.wait_ge(lam_act, 1)
            ls.step(nc.vector.tensor_tensor(LAM[:, 68:69], LAM[:, 67:68], LAM[:, 66:67], ALU.subtract))
            ls.step(nc.vector.tensor_scalar(LAM[:, 68:69], LAM[:, 68:69], -LAM_INIT, None, ALU.add))
            ls.step(nc.vector.tensor_scalar(LAM[:, 69:70], par("subln"), 1.0 - LAM_INIT, None, ALU.mult))
            ls.step(nc.vector.tensor_scalar(LAM[:, 70:71], par("q_norm"), par("k_norm"), None, ALU.mult))

            def evac(h, j):
                dve.wait_ge(gemm_done, TILE0["kvq"] + 3 * h + j + 1)
                if j == 1 and h >= 1:
                    dve.wait_ge(vt_done, h)
                if j == 2 and h >= 2:
                    dve.wait_ge(s_done, NT * (h - 1))
                dst = (U[:, 0, 3:3 + T], U[:, 1, 3:3 + T], QN[h % 2])[j]
                fr.step(nc.vector.tensor_tensor(dst, BANK[(TILE0["kvq"] + 3 * h + j) % 2][:, :], RS[:, :], ALU.mult))

            def k_inverse(h):
                dve.wait_ge(hstd, 2 * h + 1)
                rk.step(nc.vector.reciprocal(KRMS, KSTD))
                rk.step(nc.vector.tensor_copy(KCOLS.rearrange("p c (n d) -> p (c n) d", d=64),
                                              KRMS.rearrange("p c n -> p (c n)").unsqueeze(2).to_broadcast([P, 2 * NT, 64])))

            def k_norm(h):
                dve.wait_ge(kb_done, h + 1)
                if h >= 2:
                    dve.wait_ge(s_done, NT * (h - 1))
                kq.step(nc.vector.scalar_tensor_tensor(KN[h % 2], U[:, 0, 3:3 + T], LAM[:, 70:71], BANK[6][:, :],
                                                       ALU.mult, ALU.mult))

            def q_inverse(h):
                dve.wait_ge(hstd, 2 * h + 2)
                rq.step(nc.vector.reciprocal(QRMS, QSTD))
                rq.step(nc.vector.tensor_scalar(QRMS, QRMS, 0.125, None, ALU.mult))

            def out_inverse(h):
                dve.wait_ge(ostd_ready, h + 1)
                ro.step(nc.vector.reciprocal(ORMS, OSTD))

            def logits(h, i):
                w = NT * h + i
                n = (i + 1) * P
                if w == 0:
                    dve.wait_ge(bias_in, 16)
                dve.wait_ge(s_done, w + 1)
                if w >= 2:
                    dve.wait_ge(t_done, w - 1)
                for c in range(2):
                    p = PR[w % 2][c][:, 0:n]
                    step.step(nc.vector.scalar_tensor_tensor(p, BANK[2 + c][:, 0:n], QRMS[:, i, c:c + 1], BIAS[:, h, T - n:T],
                                                             ALU.mult, ALU.add))
                    red = nc.vector.tensor_reduce(NM[w % 2][:, c:c + 1], p, AX.X, ALU.max, negate=True)
                    (lr if c else step).step(red)

            def combine(h, i):
                w = NT * h + i
                n = (i + 1) * P
                dve.wait_ge(p_ready, 2 * w + 2)
                s, (p0, p1) = SUMS[w % 2], PR[w % 2]
                step.step(nc.vector.reciprocal(s, s))
                step.step(nc.vector.tensor_tensor(s[:, 1:2], s[:, 1:2], LAM[:, 68:69], ALU.mult))
                step.step(nc.vector.tensor_scalar(p1[:, 0:n], p1[:, 0:n], s[:, 1:2], None, ALU.mult))
                ar.step(nc.vector.scalar_tensor_tensor(p0[:, 0:n], p0[:, 0:n], s[:, 0:1], p1[:, 0:n], ALU.mult, ALU.add))

            def out_norm(h):
                dve.wait_ge(outb_done, h + 1)
                ohr.step(nc.vector.scalar_tensor_tensor(OH[:, h, :], OB, LAM[:, 69:70], BANK[7][:, :], ALU.mult, ALU.mult))

            def split_out(k):
                dve.wait_ge(gemm_done, TILE0["kvq"] + 3 * AH)
                hq.step(nc.vector.tensor_copy(HQH[:, k, :], OH[:, k, :]))
                hq.step(nc.vector.tensor_tensor(HQL[:, k, :], OH[:, k, :], HQH[:, k, :].bitcast(F32), ALU.subtract))

            evac(0, 0)
            evac(0, 1)
            hq.n = 2 * QUERY_EARLY
            for k in range(QUERY_EARLY, KD):
                split_scaled(hq, HQH[:, k, :], HQL[:, k, :], X[:, k, :], par("attn_ln", k))
            evac(0, 2)
            k_inverse(0)
            k_norm(0)
            for h in range(AH + 1):
                for i in range(NT):
                    w = NT * h + i
                    if 1 <= w < NT * AH + 1:
                        combine((w - 1) // NT, (w - 1) % NT)
                    if i == 0 and h < AH:
                        q_inverse(h)
                    if h + 1 < AH and i < 3:
                        evac(h + 1, i)
                    if h < AH:
                        logits(h, i)
                    if h + 1 < AH and i == 2:
                        k_inverse(h + 1)
                    if h + 1 < AH and i == 3:
                        k_norm(h + 1)
                    if i == 3 and h >= 1:
                        out_inverse(h - 1)
                    if i == 0 and h >= 2:
                        out_norm(h - 2)
                    if h == AH - 1 and i < 3:
                        for k in range(2 * i, 2 * i + 2):
                            split_out(k)
            out_norm(AH - 1)
            for k in range(AH - 2, AH):
                split_out(k)
            add_dve(dve, "attn_out", 3, "ffn_ln1", hr, fr, rs)

        sec = Carve()
        YA = sec(2 * MH, T)
        YN = sec(NP_, T)
        GR, FA, FW, FC = (YN[:, i, :] for i in range(NP_))
        nz_at = sec.at
        NZ = sec(NP_, T)
        head_at = sec.at
        HB = []
        for _ in range(2):
            HB.append(dict(q=sec(2, T), k=sec(2, T), v=sec(NT, 2 * P), o=sec(2, T), z=sec(2, T)))
        SW = sec(NT, T)
        cos_at = AREA - 2 * T
        assert sec.at <= cos_at
        sec.at = nz_at
        DW = [sec(T) for _ in range(2)]
        HN = sec(2, T)
        sec.at = head_at
        QRAW = sec(NP_, T)
        KVC = sec(2, T)
        KS, KW = sec(T), sec(T)
        VS, VW = sec(NT, P), sec(NT, P)
        QR = sec(NP_, T)
        cw_at = sec.at
        CW1K = sec(CMPL, P)
        assert sec.at <= cos_at
        CW1V = sec(CMPL, P)
        sec.at = cos_at
        COS, SIN = sec(T), sec(T)
        sec.at = cw_at
        SGA = sec(KD, T)
        pb_at = sec.at
        PB = [[sec(T) for _ in range(2)] for _ in range(2)]
        AT2 = [sec(T) for _ in range(2)]
        NM2 = [sec(2) for _ in range(2)]
        SM2 = [sec(2) for _ in range(2)]
        CL = sec(NT, NCMP)
        CMX, CSM = sec(NT), sec(NT)
        SGB = [sec(T), sec(T), KVC[:, 0, :], KVC[:, 1, :], SQ[:, 0, :], SQ[:, 1, :], ACC[:, :], STD[:, :]]
        sec.at = 8 * T
        UC = [sec(CMPL, NCMP) for _ in range(2)]
        PCT = [EMB[:, :], RDB[:, :]]
        EM, RDEN, HG = EMB[:, :], RDB[:, :], STD[:, 0:P]
        flat = FLAT[:, :]
        GK = flat[:, 0:16].rearrange("p (c h) -> p c h", h=4)
        GN = flat[:, 16:112].rearrange("p (c h) -> p c h", h=24)
        KCC = flat[:, 112:112 + NCMP]
        VCC = flat[:, 144:272]
        CW2 = flat[:, 272:400]

        g_row = sem("gate_rows_step")
        g_act = sem("gate_act_step")
        gT_done = sem("gates_turned")
        pos_in = sem("positions_in")
        rope_step = sem("rope_step")
        rope_act = sem("rope_act_step")
        bc_done = sem("maxima_spread")
        em_ready = sem("floor_ready")
        dw_ready = sem("mlstm_exponents")
        dwe_ready = sem("mlstm_decay")
        s2_done = sem("mlstm_scores")
        sw_ready = sem("mlstm_weights")
        nd_done = sem("mlstm_sums")
        hn_ready = sem("mlstm_heads")
        mean_done = sem("head_mean_sum")
        hc_ready = sem("head_centered")
        hcsq = sem("head_centered_squares")
        var_done = sem("head_variance_sum")
        vstd = sem("head_deviation")
        ya_ready = sem("mlstm_out_ready")
        vt2_done = sem("values_turned")
        cmp_w_in = [sem(f"compress_weights_in_{x}") for x in "kv"]
        cmp_w2_in = sem("compress_out_weights_in")
        hidT_done = sem("compress_hidden_turned")
        turn_done = sem("rope_turn_done")
        roped = sem("rope_ready")
        vsw_done = sem("nsa_values_turned")
        vsw_ready = sem("nsa_values_ready")
        uc_ready = sem("compress_blocks_ready")
        hid_done = sem("compress_hidden_done")
        hid_ready = sem("compress_hidden_ready")
        kvc_done = sem("compressed_done")
        kvc_ready = sem("compressed_ready")
        cs_done = sem("compressed_scores")
        cl_ready = sem("compressed_logits")
        ce_ready = sem("compressed_exps")
        cp_ready = sem("compressed_probs")
        ct_done = sem("compressed_turned")
        pct_ready = sem("compressed_turned_ready")
        n_s = sem("nsa_scores")
        n_l = sem("nsa_maxima")
        n_p = sem("nsa_exps")
        n_a = sem("nsa_probs")
        n_t = sem("nsa_turned")
        n_tc = sem("nsa_turned_ready")
        n_o = sem("nsa_out")
        yn_out = sem("nsa_gated")
        mg_ready = sem("merged_ready")
        sg_ready = sem("branch_gates_ready")
        out_ready = sem("output_ready")
        stored = sem("output_stored")

        HT = 10
        NQ0, NZ0, GA0 = 40, 50, 54
        R0, C0 = 84, 68
        W2 = "w_in2"

        def used(n):
            return R0 + min(n, NQ0) + max(min(n, GA0) - NZ0, 0)

        def convs(n):
            return C0 + 4 * (n // HT) + min(n % HT, 4)

        def second_pe(pe):
            gemm_tile(pe, "gates_w", 0, 0, scaled_in(pe, 4))
            norm_sum(pe, 4)

            def tile(n, only=None):
                gemm_tile(pe, W2, 0, n, lambda k: (HH[:, k, :], HL[:, k, :]), only=only)

            def turn_value(n):
                pe.wait_ge(gemm_free, TILE0[W2] + n + 1)
                pe.wait_ge(row_used, used(n))
                for c in range(NT):
                    mm = nc.tensor.transpose(BANK[4][:, c * P:(c + 1) * P], U[:, n % 2, 3 + c * P:3 + (c + 1) * P], IDENT)
                mm.then_inc(vt2_done, 1)

            def spread(h):
                if h >= 1:
                    pe.wait_ge(vstd, h)
                pe.wait_ge(row_used, used(HT * h + 6))
                nc.tensor.matmul(BANK[2][:, :], IDENT[0:4, h:h + 1].to_broadcast([4, P]), FW[0:4, :], start=True, stop=True)
                nc.tensor.matmul(BANK[4][:, :], IDENT[0:4, h:h + 1].to_broadcast([4, P]), FA[0:4, :],
                                 start=True, stop=True).then_inc(bc_done, 1)

            def scores(h, sb):
                if h or sb:
                    pe.wait_ge(sw_ready, NT * h + sb)
                pe.wait_ge(row_used, used(HT * h + 4))
                b = HB[h % 2]
                for e in range(2):
                    mm = nc.tensor.matmul(BANK[3][:, 0:T - sb * P], b["k"][:, e, sb * P:(sb + 1) * P], b["q"][:, e, sb * P:T],
                                          start=(e == 0), stop=(e == 1))
                mm.then_inc(s2_done, 1)

            def sums(h, sb):
                pe.wait_ge(sw_ready, NT * h + sb + 1)
                if sb == 0 and h >= 1:
                    pe.wait_ge(hn_ready, 2 * h)
                pe.wait_ge(row_used, used(HT * h + 6))
                first, last = sb == 0, sb == NT - 1
                at = slice(sb * P, T)
                for e in range(2):
                    nc.tensor.matmul(BANK[5 + e][:, at], HB[h % 2]["v"][:, sb, e * P:(e + 1) * P], SW[:, sb, 0:T - sb * P],
                                     start=first, stop=last)
                mm = nc.tensor.matmul(BANK[7][:, at], ONES[:, :], SW[:, sb, 0:T - sb * P], start=first, stop=last)
                if last:
                    mm.then_inc(nd_done, 1)

            def mean(h):
                pe.wait_ge(hn_ready, 2 * h + 2)
                for e in range(2):
                    mm = nc.tensor.matmul(BANK[2][:, :], ONES[:, :], HN[:, e, :], start=(e == 0), stop=(e == 1))
                mm.then_inc(mean_done, 1)

            def variance(h):
                pe.wait_ge(hcsq, h + 1)
                for e in range(2):
                    mm = nc.tensor.matmul(BANK[2][:, :], ONES[:, :], SQ[:, e, :], start=(e == 0), stop=(e == 1))
                mm.then_inc(var_done, 1)

            for n in range(HT):
                tile(n)
                if n in (5, 6):
                    turn_value(n - 1)
            pe.wait_ge(g_row, 14)
            pe.wait_ge(g_act, 1)
            for c in range(NT):
                tok = slice(c * P, (c + 1) * P)
                nc.tensor.transpose(BANK[6][:, 32 * c:32 * c + 4], GR[0:4, tok], IDENT[0:4, 0:4])
                mm = nc.tensor.transpose(BANK[5][:, 32 * c:32 * c + 24], GR[64:88, tok], IDENT[64:88, 64:88])
            mm.then_inc(gT_done, 1)
            pe.wait_ge(g_row, 16)
            pe.wait_ge(masks_set, 2)
            for h in range(MH):
                m = HT * (h + 1)
                spread(h)
                tile(m)
                scores(h, 0)
                tile(m + 1)
                for sb in range(1, NT):
                    sums(h, sb - 1)
                    scores(h, sb)
                    tile(m + 1 + sb)
                sums(h, NT - 1)
                tile(m + 5)
                if h + 1 < MH:
                    turn_value(m + 4)
                mean(h)
                tile(m + 6)
                if h + 1 < MH:
                    turn_value(m + 5)
                variance(h)
                for n in range(7, HT):
                    tile(m + n)
            def turn_nsa_value(x):
                pe.wait_ge(gemm_free, TILE0[W2] + 49 + x)
                if x:
                    pe.wait_ge(vsw_ready, 1)
                for c in range(NT):
                    mm = nc.tensor.transpose(BANK[4][:, c * P:(c + 1) * P], CV[:, x, c * P:(c + 1) * P], IDENT)
                mm.then_inc(vsw_done, 1)

            def turn_rope(x):
                if x >= 2:
                    pe.wait_ge(roped, x - 1)
                pe.wait_ge(vstd, MH)
                src = QRAW[:, x, :] if x < NP_ else (KS, KW)[x - NP_]
                nc.tensor.matmul(BANK[2 + x % 2][:, :], const("rope_turn"), src, start=True, stop=True).then_inc(turn_done, 1)

            turn_rope(0)
            turn_rope(1)
            tile(NZ0)
            turn_nsa_value(0)
            turn_rope(2)
            turn_rope(3)
            tile(NZ0 + 1)
            turn_nsa_value(1)
            turn_rope(4)
            turn_rope(5)
            tile(NZ0 + 2)
            pe.wait_ge(uc_ready, 2)
            for x in range(2):
                pe.wait_ge(cmp_w_in[x], 16)
                for g in range(2):
                    half = slice(64 * g, 64 * g + 64)
                    for l in range(CMPL):
                        mm = nc.tensor.matmul(BANK[7 if g else 5][0:NCMP, x * P:(x + 1) * P], UC[x][half, l, :],
                                              (CW1K, CW1V)[x][half, l, :], start=(l == 0), stop=(l == CMPL - 1))
            mm.then_inc(hid_done, 1)
            tile(NZ0 + 3)
            pe.wait_ge(hid_ready, 2)
            for g in range(2):
                for x in range(2):
                    mm = nc.tensor.transpose(BANK[5][:, 64 * x + 32 * g:64 * x + 32 * g + NCMP],
                                             EM[0:NCMP, (2 * g + x) * P:(2 * g + x + 1) * P], IDENT[0:NCMP, 0:NCMP])
            mm.then_inc(hidT_done, 1)
            pe.wait_ge(cmp_w2_in, 16)
            pe.wait_ge(hid_ready, 3)
            for g in range(2):
                nc.tensor.matmul(BANK[7][64 * g:64 * g + 64, 128:128 + NCMP], CW2[:, 0:64], HG[:, 32 * g:32 * g + NCMP],
                                 start=True, stop=True)
                mm = nc.tensor.matmul(BANK[7][0:NCMP, 192 + 64 * g:256 + 64 * g], HG[:, 64 + 32 * g:64 + 32 * g + NCMP],
                                      CW2[:, 64:128], start=True, stop=True)
            mm.then_inc(kvc_done, 1)

            def cmp_scores(s):
                g, j = s % 2, s // 2
                half = slice(64 * g, 64 * g + 64)
                pe.wait_ge(kvc_ready, 2)
                if s >= 1:
                    pe.wait_ge(pct_ready, s)
                for i in range(NT):
                    mm = nc.tensor.matmul(BANK[7][:, NCMP * i:NCMP * (i + 1)], QRAW[half, j, i * P:(i + 1) * P],
                                          KCC[half, :], start=True, stop=True)
                mm.then_inc(cs_done, 1)

            def cmp_turn(s):
                pe.wait_ge(cp_ready, s + 1)
                for i in range(NT):
                    mm = nc.tensor.transpose(BANK[7][0:NCMP, i * P:(i + 1) * P], CL[:, i, :], IDENT)
                mm.then_inc(ct_done, 1)

            def nsa_scores(w):
                s, i = w // NT, w % NT
                g, j = s % 2, s // 2
                half = slice(64 * g, 64 * g + 64)
                pe.wait_ge(roped, 6)
                if w >= 1:
                    pe.wait_ge(n_p, 2 * w)
                for c, keys in enumerate((KS, KW)):
                    nc.tensor.matmul(BANK[2 + c][:, 0:(i + 1) * P], QR[half, j, i * P:(i + 1) * P], keys[half, 0:(i + 1) * P],
                                     start=True, stop=False)
                    mm = nc.tensor.matmul(BANK[2 + c][:, i * P:(i + 1) * P], ONEHOT[:, :], FUTURE[:, :], start=False, stop=True)
                mm.then_inc(n_s, 1)

            def nsa_turn(w):
                i = w % NT
                pe.wait_ge(n_a, w + 1)
                if w >= 1:
                    pe.wait_ge(n_tc, 2 * w)
                else:
                    pe.wait_ge(vsw_ready, 2)
                for c in range(2):
                    for kb in range(i + 1):
                        mm = nc.tensor.transpose(BANK[4 + c][:, kb * P:(kb + 1) * P], PB[w % 2][c][:, kb * P:(kb + 1) * P], IDENT)
                mm.then_inc(n_t, 1)

            def nsa_v(w):
                s, i = w // NT, w % NT
                g, j = s % 2, s // 2
                pe.wait_ge(n_tc, 2 * w + 2)
                pe.wait_ge(pct_ready, s + 1)
                if w % 8 == 0 and w:
                    pe.wait_ge(yn_out, j)
                out_t = BANK[6][64 * g:64 * g + 64, i * P:(i + 1) * P]
                nc.tensor.matmul(out_t, VCC[0:NCMP, 64 * g:64 * g + 64], PCT[s % 2][0:NCMP, i * P:(i + 1) * P],
                                 start=True, stop=False)
                for c, values in enumerate((VS, VW)):
                    for kb in range(i + 1):
                        mm = nc.tensor.matmul(out_t, values[:, kb, 64 * g:64 * g + 64], AT2[c][:, kb * P:(kb + 1) * P],
                                              start=False, stop=(c == 1 and kb == i))
                mm.then_inc(n_o, 1)

            cmp_scores(0)
            cmp_turn(0)
            for w in range(NT * 8 + 2):
                if w < 32:
                    tile(GA0 + w // 2, range(4 * (w % 2), 4 * (w % 2) + 4))
                if w < 32:
                    nsa_scores(w)
                if w >= 2:
                    nsa_v(w - 2)
                if 1 <= w < 33:
                    nsa_turn(w - 1)
                if w < 28 and w % NT == 0:
                    cmp_scores(w // NT + 1)
                if w < 28 and w % NT == 2:
                    cmp_turn(w // NT + 1)
            pe.wait_ge(ya_ready, 2 * MH)
            pe.wait_ge(yn_out, NP_)
            with pe.Fori(0, KD // 2) as i:
                for j in range(4):
                    gemm_tile(pe, "ab", i, j, lambda k: (YN if j % 2 else YA)[:, k, :], 4 if j % 2 else 8)

            def merged(pe, k, j):
                if j == 0:
                    pe.wait_ge(mg_ready, 2 * (k + 1))
                return HH[:, k, :], HL[:, k, :]
            add_pe(pe, "w_out2", merged, 8)
            norm_sum(pe, 5)

        def second_act(act):
            ga = Count(act, g_act)
            act.wait_ge(gemm_free, TILE0["gates_w"])
            act.dma_start(COS.bitcast(mybir.dt.int32), A["pos"]).then_inc(pos_in, 16)
            act.dma_start(CW2, A["cmp_w2"]).then_inc(cmp_w2_in, 16)
            act.wait_ge(g_row, 1)
            ga.step(nc.scalar.activation(GR[64:88, :], GR[64:88, :], ACT.Sigmoid))
            ga.step(nc.scalar.activation(FA[32:36, :], GR[32:36, :], ACT.Abs))
            ga.step(nc.scalar.activation(FA[32:36, :], FA[32:36, :], ACT.Exp, scale=-1.0))
            act.wait_ge(g_row, 2)
            ga.step(nc.scalar.activation(HN[32:36, 0, :], FW[32:36, :], ACT.Ln))
            def rows(n):
                h, j = n // HT, n % HT
                b = HB[h % 2]
                if n < NQ0:
                    if h >= 2 and j == 0:
                        act.wait_ge(ya_ready, 2 * (h - 1))
                    if j < 4:
                        act.wait_ge(conv_ready, convs(n) + 1)
                        ins = nc.scalar.activation(b["q" if j < 2 else "k"][:, j % 2, :], CV[:, n % 2, :], ACT.Silu)
                    elif j < 6:
                        act.wait_ge(vt2_done, 2 * h + j - 3)
                        ins = nc.scalar.activation(b["v"][:, :, (j - 4) * P:(j - 3) * P],
                                                   BANK[4][:, :].rearrange("p (c d) -> p c d", d=P), ACT.Copy)
                    else:
                        act.wait_ge(gemm_free, TILE0[W2] + n + 1)
                        ins = nc.scalar.activation(b["o" if j < 8 else "z"][:, j % 2, :], U[:, n % 2, 3:3 + T],
                                                   ACT.Sigmoid if j < 8 else ACT.Silu)
                else:
                    act.wait_ge(gemm_free, TILE0[W2] + n + 1)
                    ins = nc.scalar.activation(NZ[:, n - NZ0, :], U[:, n % 2, 3:3 + T], ACT.Silu)
                ins.then_inc(row_used, 1)

            def decay(h, sb):
                act.wait_ge(dw_ready, NT * h + sb + 1)
                d = DW[sb % 2][:, 0:T - sb * P]
                nc.scalar.activation(d, d, ACT.Exp).then_inc(dwe_ready, 1)

            rows(0)
            ra = Count(act, rope_act)
            act.wait_ge(rope_step, 8)
            ra.step(nc.scalar.activation(SIN, HN[:, 1, :], ACT.Sin))
            ra.step(nc.scalar.activation(COS, HN[:, 1, :], ACT.Abs))
            rows(1)
            act.wait_ge(rope_step, 9)
            ra.step(nc.scalar.activation(COS, COS, ACT.Sin))
            for n in range(2, HT):
                rows(n)
            for h in range(MH):
                m = HT * (h + 1)
                act.wait_ge(bc_done, h + 1)
                if h >= 1:
                    act.wait_ge(hn_ready, 2 * h)
                nc.scalar.activation(EM, BANK[4][:, :], ACT.Exp, scale=-1.0).then_inc(em_ready, 1)

                def next_rows(*js):
                    if h + 1 < MH:
                        for j in js:
                            rows(m + j)
                next_rows(0)
                decay(h, 0)
                next_rows(1)
                for sb in range(1, NT):
                    decay(h, sb)
                    if sb < 3:
                        next_rows(1 + sb)
                next_rows(4)
                act.wait_ge(hc_ready, 2 * h + 2)
                nc.scalar.activation(SQ[:, 0:2, :], HN, ACT.Square).then_inc(hcsq, 1)
                next_rows(5)
                act.wait_ge(var_done, h + 1)
                nc.scalar.activation(STD[:, :], BANK[2][:, :], ACT.Sqrt, bias=EPSC[:, 0:1], scale=1.0 / 256).then_inc(vstd, 1)
                next_rows(6, 7, 8, 9)

            def nsa_value(x):
                act.wait_ge(vsw_done, x + 1)
                nc.scalar.activation((VS, VW)[x], BANK[4][:, :].rearrange("p (c d) -> p c d", d=P), ACT.Copy).then_inc(vsw_ready, 1)

            act.wait_ge(ya_ready, 2 * MH)
            act.dma_start(CW1K, A["cmp_w1"][0]).then_inc(cmp_w_in[0], 16)
            nsa_value(0)
            rows(NZ0)
            nsa_value(1)
            rows(NZ0 + 1)
            act.wait_ge(roped, 6)
            act.dma_start(CW1V, A["cmp_w1"][1]).then_inc(cmp_w_in[1], 16)
            rows(NZ0 + 2)
            act.wait_ge(hid_done, 1)
            for g in range(2):
                nc.scalar.activation(EM[0:NCMP, 2 * g * P:(2 * g + 2) * P], BANK[7 if g else 5][0:NCMP, 0:2 * P],
                                     ACT.Gelu_apprx_tanh).then_inc(hid_ready, 1)
            rows(NZ0 + 3)
            act.wait_ge(hidT_done, 1)
            nc.scalar.activation(HG.rearrange("p (a n) -> p a n", n=32)[:, :, 0:NCMP],
                                 BANK[5][:, 0:P].rearrange("p (a n) -> p a n", n=32)[:, :, 0:NCMP],
                                 ACT.Copy).then_inc(hid_ready, 1)

            def cmp_exp(s):
                act.wait_ge(cl_ready, s + 1)
                nc.scalar.activation(CL, CL, ACT.Exp).then_inc(ce_ready, 1)

            def cmp_turned(s):
                act.wait_ge(ct_done, s + 1)
                if s >= 2:
                    act.wait_ge(n_o, NT * (s - 1))
                nc.scalar.activation(PCT[s % 2][0:NCMP, :], BANK[7][0:NCMP, :], ACT.Copy).then_inc(pct_ready, 1)

            def exps(w):
                n = (w % NT + 1) * P
                act.wait_ge(n_l, w + 1)
                if w >= 2:
                    act.wait_ge(n_t, w - 1)
                for c in range(2):
                    nc.scalar.activation(PB[w % 2][c][:, 0:n], BANK[2 + c][:, 0:n], ACT.Exp, bias=NM2[w % 2][:, c:c + 1],
                                         scale=0.125, accum_out=SM2[w % 2][:, c:c + 1]).then_inc(n_p, 1)

            def turned(w):
                n = (w % NT + 1) * P
                act.wait_ge(n_t, w + 1)
                if w >= 1:
                    act.wait_ge(n_o, w)
                for c in range(2):
                    nc.scalar.activation(AT2[c][:, 0:n], BANK[4 + c][:, 0:n], ACT.Copy).then_inc(n_tc, 1)

            cmp_exp(0)
            cmp_turned(0)
            for w in range(NT * 8 + 2):
                if w < 32:
                    exps(w)
                if 1 <= w < 33:
                    turned(w - 1)
                if w < 28 and w % NT == 0:
                    cmp_exp(w // NT + 1)
                if w < 28 and w % NT == 2:
                    cmp_turned(w // NT + 1)
            for k in range(KD):
                for branch, gate in enumerate((SGA[:, k, :], SGB[k])):
                    if k == 0:
                        act.wait_ge(gemm_free, TILE0[W2] + GA0 + 2 * KD)
                    nc.scalar.activation(gate, gate, ACT.Sigmoid).then_inc(sg_ready, 1)
            add_act(act, "w_out2", 5)

        def second_dve(dve, step, rs, hr, fr, cv):
            gr, rp = Count(dve, g_row), Count(dve, rope_step)
            nc.vector.tensor_copy(ONEHOT[:, :], IDENT).then_inc(masks_set, 1)
            nc.vector.tensor_copy(FUTURE[:, :], const("future_neg")).then_inc(masks_set, 1)
            dve.wait_ge(gemm_done, TILE0["gates_w"] + 1)
            fr.step(nc.vector.tensor_tensor(GR[0:88, :], BANK[TILE0["gates_w"] % 2][0:88, :], RS[0:88, :], ALU.mult))
            gr.step(nc.vector.tensor_scalar(GR[0:88, :], GR[0:88, :], par("gate_bias", parts=88), None, ALU.add))
            def evac(n, dst):
                dve.wait_ge(gemm_done, TILE0[W2] + n + 1)
                fr.step(nc.vector.tensor_tensor(dst, BANK[(TILE0[W2] + n) % 2][:, :], RS[:, :], ALU.mult))

            def rows(n):
                h, j = n // HT, n % HT
                if n >= GA0:
                    k = n - GA0
                    evac(n, SGA[:, k, :] if k < KD else SGB[k - KD])
                    return
                if n < NQ0 or n >= NZ0:
                    if n >= 2:
                        dve.wait_ge(row_used, used(n - 1))
                    evac(n, U[:, n % 2, 3:3 + T])
                    if n < NQ0 and j < 4:
                        t = 2 * h + j % 2 + (8 if j >= 2 else 0)
                        conv(dve, step, cv, n % 2, lambda k: par("qk_conv", 5 * t + k), 4)
                    return
                k = n - NQ0
                if k == 8:
                    dve.wait_ge(row_used, used(NQ0))
                evac(n, [QRAW[:, 0, :], QRAW[:, 1, :], QRAW[:, 2, :], QRAW[:, 3, :], KVC[:, 0, :], KVC[:, 1, :],
                         KS, KW, CV[:, 0, :], CV[:, 1, :]][k])

            dw, sw, hn, hc, ya = (Count(dve, s) for s in (dw_ready, sw_ready, hn_ready, hc_ready, ya_ready))

            def exponents(h, sb):
                if sb == 0:
                    dve.wait_ge(bc_done, h + 1)
                n = T - sb * P
                dw.step(nc.vector.tensor_scalar(DW[sb % 2][:, 0:n], BANK[2][:, sb * P:T], GK[:, sb, h:h + 1], 0.0,
                                                ALU.add, ALU.min))

            def weights(h, sb):
                n = T - sb * P
                dve.wait_ge(dwe_ready, NT * h + sb + 1)
                dve.wait_ge(s2_done, NT * h + sb + 1)
                step.step(nc.vector.scalar_tensor_tensor(SW[:, sb, 0:n], BANK[3][:, 0:n], 1.0 / 16, DW[sb % 2][:, 0:n],
                                                         ALU.mult, ALU.mult))
                sw.step(nc.vector.tensor_tensor(SW[:, sb, 0:P], SW[:, sb, 0:P], const("causal_st"), ALU.mult))

            def divide(h):
                dve.wait_ge(nd_done, h + 1)
                dve.wait_ge(em_ready, h + 1)
                step.step(nc.vector.tensor_scalar(RDEN, BANK[7][:, :], -1.0, None, ALU.mult))
                step.step(nc.vector.tensor_tensor(RDEN, RDEN, BANK[7][:, :], ALU.max))
                step.step(nc.vector.tensor_tensor(RDEN, RDEN, EM, ALU.max))
                step.step(nc.vector.reciprocal(RDEN, RDEN))
                for e in range(2):
                    hn.step(nc.vector.tensor_tensor(HN[:, e, :], BANK[5 + e][:, :], RDEN, ALU.mult))

            def center(h):
                dve.wait_ge(mean_done, h + 1)
                for e in range(2):
                    hc.step(nc.vector.scalar_tensor_tensor(HN[:, e, :], BANK[2][:, :], -1.0 / 256, HN[:, e, :], ALU.mult, ALU.add))

            def gated(h):
                dve.wait_ge(vstd, h + 1)
                dve.wait_ge(row_used, used(HT * (h + 1)))
                step.step(nc.vector.reciprocal(RDEN, STD[:, :]))
                for e in range(2):
                    step.step(nc.vector.scalar_tensor_tensor(HN[:, e, :], HN[:, e, :], par("mh_norm", 2 * h + e), RDEN, ALU.mult, ALU.mult))
                    step.step(nc.vector.tensor_tensor(HN[:, e, :], HN[:, e, :], HB[h % 2]["o"][:, e, :], ALU.mult))
                    ya.step(nc.vector.tensor_tensor(YA[:, 2 * h + e, :], HN[:, e, :], HB[h % 2]["z"][:, e, :], ALU.mult))

            rows(0)
            f, fa, fw, fc = (b[32:36, :] for b in (GR, FA, FW, FC))
            dve.wait_ge(g_act, 3)
            gr.step(nc.vector.tensor_scalar(fw, fa, 1.0, None, ALU.add))
            gr.step(nc.vector.tensor_scalar(fc, fw, -1.0, None, ALU.add))
            gr.step(nc.vector.tensor_tensor(fa, fa, fc, ALU.subtract))
            gr.step(nc.vector.tensor_scalar(f, f, 0.0, None, ALU.min))
            dve.wait_ge(g_act, 4)
            gr.step(nc.vector.tensor_tensor(fa, fa, HN[32:36, 0, :], ALU.add))
            gr.step(nc.vector.tensor_tensor(f, f, fa, ALU.subtract))
            gr.step(nc.vector.memset(fw, 1.0))
            gr.step(nc.vector.tensor_tensor_scan(fc, fw, f, 0.0, ALU.mult, ALU.add))
            li, f0, mx, mt = GR[0:4, :], FC[0:4, :], FW[0:4, :], FA[0:4, :]
            gr.step(nc.vector.tensor_copy(f0, fc))
            gr.step(nc.vector.tensor_tensor(li, li, f0, ALU.subtract))
            gr.step(nc.vector.tensor_tensor_scan(mx, li, li, 0.0, ALU.max, ALU.max))
            gr.step(nc.vector.tensor_tensor(mt, mx, f0, ALU.add))
            gr.step(nc.vector.tensor_scalar(mx, mx, -1.0, None, ALU.mult))
            rows(1)
            ang, turns = HN[:, 1, :], SIN
            dve.wait_ge(pos_in, 16)
            dve.wait_ge(row_used, R0)
            rp.step(nc.vector.tensor_copy(ang, COS.bitcast(mybir.dt.int32)))
            rp.step(nc.vector.tensor_scalar(ang, ang, const("rope_freq"), None, ALU.mult))
            rp.step(nc.vector.tensor_scalar(turns, ang, 1.0 / (2 * math.pi), 1.5 * 2 ** 23, ALU.mult, ALU.add))
            rp.step(nc.vector.tensor_scalar(turns, turns, -1.5 * 2 ** 23, None, ALU.add))
            p1, p2 = 6.28125, float(np.float32(2 * math.pi - 6.28125).view(np.uint32).__and__(np.uint32(0xFFFFF000)).view(np.float32))
            for part in (p1, p2, 2 * math.pi - p1 - p2):
                rp.step(nc.vector.scalar_tensor_tensor(ang, turns, -part, ang, ALU.mult, ALU.add))
            rp.step(nc.vector.tensor_scalar(ang, ang, 3.1415925, -3.1415925, ALU.min, ALU.max))
            rows(2)
            dve.wait_ge(rope_act, 2)
            rp.step(nc.vector.tensor_scalar(COS, COS, -1.0, math.pi / 2, ALU.mult, ALU.add))
            for n in range(3, HT):
                rows(n)
            dve.wait_ge(gT_done, 1)
            b6 = BANK[6][:, 0:P].rearrange("p (c w) -> p c w", w=32)
            gr.step(nc.vector.tensor_copy(GK, b6[:, :, 0:4]))
            b5 = BANK[5][:, 0:P].rearrange("p (c w) -> p c w", w=32)
            gr.step(nc.vector.tensor_copy(GN, b5[:, :, 0:24]))
            for h in range(MH):
                m = HT * (h + 1)
                exponents(h, 0)
                rows(m)
                weights(h, 0)
                exponents(h, 1)
                rows(m + 1)
                for sb in range(1, NT):
                    weights(h, sb)
                    if sb + 1 < NT:
                        exponents(h, sb + 1)
                    rows(m + 1 + sb)
                divide(h)
                rows(m + 5)
                center(h)
                rows(m + 6)
                gated(h)
                for n in range(7, HT):
                    rows(m + n)

            ro, uc, kvc = (Count(dve, s) for s in (roped, uc_ready, kvc_ready))

            def rotate(x):
                dve.wait_ge(turn_done, x + 1)
                dve.wait_ge(rope_act, 3)
                src, dst = (QRAW[:, x, :], QR[:, x, :]) if x < NP_ else ((KS, KW)[x - NP_],) * 2
                step.step(nc.vector.tensor_tensor(RDEN, BANK[2 + x % 2][:, :], SIN, ALU.mult))
                step.step(nc.vector.tensor_tensor(dst, src, COS, ALU.mult))
                ro.step(nc.vector.tensor_tensor(dst, dst, RDEN, ALU.add))

            rotate(0)
            rotate(1)
            rows(NZ0)
            rotate(2)
            rotate(3)
            rows(NZ0 + 1)
            for x in range(2):
                blocks = bass.AP(tensor=KVC.tensor, offset=KVC[:, x, :].offset, ap=[KVC.ap[0], [1, CMPL], [16, NCMP]])
                uc.step(nc.vector.tensor_tensor(UC[x], blocks, par("cmp_pos", CMPL * x, CMPL).unsqueeze(2)
                                                .to_broadcast([P, CMPL, NCMP]), ALU.add))
            rotate(4)
            rotate(5)
            rows(NZ0 + 2)
            rows(NZ0 + 3)
            dve.wait_ge(kvc_done, 1)
            kvc.step(nc.vector.tensor_copy(KCC, BANK[7][:, 128:128 + NCMP]))
            kvc.step(nc.vector.tensor_copy(VCC[0:NCMP, :], BANK[7][0:NCMP, 192:320]))

            cl, cp, nl, na, yo, mg = (Count(dve, s) for s in (cl_ready, cp_ready, n_l, n_a, yn_out, mg_ready))
            cells = [P, NT, NCMP]

            def head_of(s):
                return s // 2 + 4 * (s % 2)

            def cmp_logits(s):
                dve.wait_ge(cs_done, s + 1)
                if s >= 1:
                    dve.wait_ge(ct_done, s)
                sc = BANK[7][:, 0:NT * NCMP].rearrange("p (i n) -> p i n", n=NCMP)
                neg = const("cmp_neg").rearrange("p (i n) -> p i n", n=NCMP)
                step.step(nc.vector.scalar_tensor_tensor(CL, sc, 0.125, neg, ALU.mult, ALU.add))
                step.step(nc.vector.tensor_reduce(CMX, CL, AX.X, ALU.max))
                cl.step(nc.vector.tensor_tensor(CL, CL, CMX.unsqueeze(2).to_broadcast(cells), ALU.subtract))

            def cmp_probs(s):
                dve.wait_ge(ce_ready, s + 1)
                h = head_of(s)
                step.step(nc.vector.tensor_reduce(CSM, CL, AX.X, ALU.add))
                step.step(nc.vector.reciprocal(CSM, CSM))
                step.step(nc.vector.tensor_tensor(CSM, CSM, GN[:, :, 3 * h], ALU.mult))
                step.step(nc.vector.tensor_tensor(CL, CL, const("cmp_seen").rearrange("p (i n) -> p i n", n=NCMP), ALU.mult))
                cp.step(nc.vector.tensor_tensor(CL, CL, CSM.unsqueeze(2).to_broadcast(cells), ALU.mult))

            def maxima(w):
                n = (w % NT + 1) * P
                dve.wait_ge(n_s, w + 1)
                for c in range(2):
                    step.step(nc.vector.tensor_reduce(NM2[w % 2][:, c:c + 1], BANK[2 + c][:, 0:n], AX.X, ALU.max, negate=True))
                nl.step(nc.vector.tensor_scalar(NM2[w % 2], NM2[w % 2], 0.125, None, ALU.mult))

            def probs(w):
                s, i = w // NT, w % NT
                h, n = head_of(s), (i + 1) * P
                dve.wait_ge(n_p, 2 * w + 2)
                sm = SM2[w % 2]
                step.step(nc.vector.reciprocal(sm, sm))
                step.step(nc.vector.tensor_tensor(sm, sm, GN[:, i, 3 * h + 1:3 * h + 3], ALU.mult))
                for c in range(2):
                    p = PB[w % 2][c][:, 0:n]
                    (na if c else step).step(nc.vector.tensor_scalar(p, p, sm[:, c:c + 1], None, ALU.mult))

            cmp_logits(0)
            cmp_probs(0)
            for w in range(NT * 8 + 2):
                if 1 <= w < 33:
                    probs(w - 1)
                if w % 2 == 1 and w < 32:
                    rows(GA0 + w // 2)
                if w < 32:
                    maxima(w)
                if w < 28 and w % NT == 0:
                    cmp_logits(w // NT + 1)
                if w < 28 and w % NT == 1:
                    cmp_probs(w // NT + 1)
                if w >= 2 and (w - 2) % 8 == 7:
                    j = (w - 2) // 8
                    dve.wait_ge(n_o, w - 1)
                    yo.step(nc.vector.tensor_tensor(YN[:, j, :], BANK[6][:, :], NZ[:, j, :], ALU.mult))

            for k in range(KD):
                for branch, gate in enumerate((SGA[:, k, :], SGB[k])):
                    n = TILE0["ab"] + 2 * k + branch
                    dve.wait_ge(gemm_done, n + 1)
                    dve.wait_ge(sg_ready, 2 * k + branch + 1)
                    fr.step(nc.vector.tensor_tensor(CV[:, branch, :], BANK[n % 2][:, :], gate, ALU.mult))
                step.step(nc.vector.tensor_tensor(CV[:, 0, :], CV[:, 0, :], CV[:, 1, :], ALU.add))
                mg.step(nc.vector.tensor_copy(HH[:, k, :], CV[:, 0, :]))
                mg.step(nc.vector.tensor_tensor(HL[:, k, :], CV[:, 0, :], HH[:, k, :].bitcast(F32), ALU.subtract))
            add_dve(dve, "w_out2", 5, None, hr, fr, rs)
            for k in range(KD):
                nc.vector.scalar_tensor_tensor(X[:, k, :], X[:, k, :], par("final", k), RS[:, :], ALU.mult, ALU.mult).then_inc(out_ready, 1)

        COUNT0 = {"conv0": (24, 40), "conv1": (46, 62)}

        def finish(sp):
            for k in range(KD):
                sp.wait_ge(out_ready, k + 1)
                sp.dma_start(out[:, k, :], X[:, k, :]).then_inc(stored, 16)
            sp.wait_ge(stored, 16 * KD)

        def rest_pe(pe):
            def ynorm(pe, k, j):
                if j == 0:
                    pe.wait_ge(yn_ready, 2 * GT + k + 1)
                return YB[:, 2 * GT + k, :]
            add_pe(pe, "out_b", ynorm, 8)
            ffn_pe(pe, 0)
            attention_pe(pe)
            ffn_pe(pe, 1)
            second_pe(pe)


        def rest_act(act, ahead):
            add_act(act, "out_b", 1)
            ffn_act(act, 0)
            attention_act(act, ahead)
            ffn_act(act, 1)
            second_act(act)

        def rest_dve(dve, step, rs, hr, fr, cv):
            add_dve(dve, "out_b", 1, "ffn_ln0", hr, fr, rs)
            ffn_dve(dve, 0, "kv_ln", step, rs, hr, fr, cv, split_query)
            attention_dve(dve, step, rs, hr, fr, cv)
            ffn_dve(dve, 1, "norm2", step, rs, hr, fr, cv)
            second_dve(dve, step, rs, hr, fr, cv)

        @block.sync
        def _(sp):
            def load(name, cells, block_at, slot, free):
                if free is not None:
                    sp.wait_ge(*free)
                sp.dma_start(RAW[:, slot, 0:cells * P], A[name][bass.ds(block_at, 1), :, :]
                             .rearrange("a p n -> (a p) n")).then_inc(w_ready[slot], 16)

            def load_input(i):
                sp.dma_start(X[:, 2 * i:2 * i + 2, :], A["xT"][:, 2 * i:2 * i + 2, :]).then_inc(x_in[i], 16)

            load_input(0)
            last = []
            for name, n, cells, per, parts in STREAM:
                turns = n // TURN - 1
                for k in range(min(TURN, n)):
                    free = loaded_used(*last[-SLOTS]) if len(last) >= SLOTS else None
                    load(name, cells, k, raw_slot(name, k), free)
                    last.append((name, per, k))
                    if len(last) == 1:
                        for i in range(1, KD // 2):
                            load_input(i)
                if n < TURN:
                    continue
                with sp.Fori(0, turns) as i:
                    for j in range(TURN):
                        load(name, cells, i * TURN + (TURN + j), raw_slot(name, j), loaded_used(name, per, TURN + j - SLOTS, i))
                last += [(name, per, k) for k in range(TURN, TURN * (turns + 1))]
                for k in range(TURN * (turns + 1), n):
                    load(name, cells, k, raw_slot(name, k), loaded_used(*last[-SLOTS]))
                    last.append((name, per, k))
            finish(sp)

        @block.gpsimd
        def _(pool):
            def split(name, cells, k, i, free):
                raw, slot, n = raw_slot(name, k), part_slot(name, k), cells * P
                pool.wait_ge(w_ready[raw], (BASE[name] + k) // SLOTS * 16 + 16 + i * (16 * TURN // SLOTS))
                if free is not None:
                    pool.wait_ge(*free)
                nc.gpsimd.tensor_tensor(WH[:, slot, 0:8], RAW[:, raw, 0:8], ONES[:, 0:8], ALU.mult).then_inc(high_ready, 1)
                nc.gpsimd.tensor_scalar(WH[:, slot, 8:n], RAW[:, raw, 8:n], 1.0, 1.0, ALU.mult, ALU.mult).then_inc(high_ready, 1)
                pool.wait_ge(high_ready, 2 * (PART0[name] + k + 1) + i * (2 * TURN))
                nc.gpsimd.tensor_tensor(WL[:, slot, 0:n], RAW[:, raw, 0:n], WH[:, slot, 0:n].bitcast(F32),
                                        ALU.subtract).then_inc(split_done, 1)

            pool.wait_ge(ones_set, 1)
            last = []
            for name, n, cells, per, parts in STREAM:
                if not parts:
                    continue
                turns = n // TURN - 1
                for k in range(min(TURN, n)):
                    split(name, cells, k, 0, products_done(*last[-SLOTS]) if len(last) >= SLOTS else None)
                    last.append((name, per, k))
                if n < TURN:
                    continue
                with pool.Fori(0, turns) as i:
                    for j in range(TURN):
                        split(name, cells, TURN + j, i, products_done(name, per, TURN + j - SLOTS, i))
                last += [(name, per, k) for k in range(TURN, TURN * (turns + 1))]
                for k in range(TURN * (turns + 1), n):
                    split(name, cells, k, 0, products_done(*last[-SLOTS]))
                    last.append((name, per, k))

        @block.tensor
        def _(pe):
            pe.wait_ge(ones_set, 3)
            for k in range(KD):
                pe.wait_ge(sq_ready, k + 1)
                mm = nc.tensor.matmul(BANK[7][:, :], ONES[:, :], SQ[:, k % 2, :], start=(k == 0), stop=(k == KD - 1))
                mm.then_inc(sq_used if k < KD - 1 else ssq_done, 1)
            gemm_tile(pe, "dt_w", 0, 0, scaled_in(pe, 0))
            pe.wait_ge(loaded, 16)

            def bias_row(h):
                if h >= 1:
                    pe.wait_ge(brow_ready, 2 * h)
                nc.tensor.matmul(BANK[2][:, :], REL[0:33, h:h + 1].to_broadcast([33, P]), BUCK[0:33, 0:T],
                                 start=True, stop=True)
                nc.tensor.matmul(BANK[3][:, 0:P], REL[0:33, h:h + 1].to_broadcast([33, P]), BUCK[0:33, T:640],
                                 start=True, stop=True).then_inc(brow_done, 1)

            def in_tile(g, j):
                gemm_tile(pe, "in_w", 0, GROUP_TILES * g + j, lambda k: (HH[:, k, :], HL[:, k, :]))

            pe.wait_ge(aux_in, 32)
            for j in range(GROUP_TILES):
                in_tile(0, j)
                if j >= GROUP_TILES - AH:
                    bias_row(j - (GROUP_TILES - AH))
            pe.wait_ge(dt_row, 9 + NT)
            for c in range(NT):
                nc.tensor.transpose(BANK[6][:, c * 64:c * 64 + 32], DTR[0:32, c * P:(c + 1) * P], IDENT[0:32, 0:32])
                mm = nc.tensor.transpose(BANK[6][:, c * 64 + 32:c * 64 + 64], CSR[0:32, c * P:(c + 1) * P], IDENT[0:32, 0:32])
            mm.then_inc(dtT_done, 1)

            def unit_sums(u):
                pe.wait_ge(gsq_ready, u + 1)
                for k in range(GT):
                    mm = nc.tensor.matmul(BANK[4][:, 2 * P:3 * P], ONES[:, :], YSQ[:, k, :], start=(k == 0), stop=(k == GT - 1))
                mm.then_inc(usum_done, 1)

            for g in range(SSM_G):
                xb = XSB[g % 2]
                for c in range(NT):
                    u = NT * g + c
                    tok = slice(c * P, (c + 1) * P)
                    if c == 0:
                        pe.wait_ge(dt_row, 11 + NT)
                    if u >= 1:
                        pe.wait_ge(d_ready, u)
                        pe.wait_ge(e_ready, 3 * u)
                    if u >= 2:
                        pe.wait_ge(gs_read, u - 1)
                    if u == 0:
                        pe.wait_ge(brow_ready, 2 * AH)
                    for h in range(SSM_HG):
                        nc.tensor.matmul(BANK[2 + h // 4][:, (h % 4) * P:(h % 4 + 1) * P],
                                         IDENT[0:32, SSM_HG * g + h:SSM_HG * g + h + 1].to_broadcast([32, P]),
                                         CSR[0:32, tok], start=True, stop=True)
                    for j in range(GT):
                        if c == 0:
                            pe.wait_ge(row_used, GROUP_TILES * g + GT + j + 1)
                        nc.tensor.transpose(BANK[5][:, j * P:(j + 1) * P], xb[:, j, tok], IDENT)
                    if c == 0:
                        pe.wait_ge(row_used, GROUP_TILES * (g + 1))
                    nc.tensor.transpose(BANK[4][:, P:2 * P], xb[:, GT, tok], IDENT)
                    nc.tensor.matmul(BANK[4][:, 0:P], xb[:, GT, tok], xb[:, GT + 1, tok],
                                     start=True, stop=True).then_inc(p1_done, 1)
                    if g + 1 < SSM_G:
                        for j in range(sum(FILL[:c]), sum(FILL[:c + 1])):
                            in_tile(g + 1, j)
                    else:
                        pe.wait_ge(yn_ready, 2 * GT)
                        for j in range(2 * c, 2 * c + 2):
                            gemm_tile(pe, "out_a", 0, j, lambda k: YB[:, k, :])
                    if u >= 1:
                        pe.wait_ge(d_ready, u + 1)
                        unit_sums(u - 1)
                    pe.wait_ge(mce_ready, u + 1)
                    if u >= 1:
                        pe.wait_ge(y_read, u)
                    if c >= 1:
                        pe.wait_ge(s_ready, 3 * g + c)
                    for h in range(SSM_HG):
                        y = BANK[6][64 * (h % 2):64 * (h % 2) + 64, (h // 2) * P:(h // 2 + 1) * P]
                        mm = nc.tensor.matmul(y, XDT[:, h, :], DEC[:, h, :], start=True, stop=(c == 0))
                        if c >= 1:
                            mm = nc.tensor.matmul(y, STATE[:, h * 64:(h + 1) * 64], ECS[:, h, :],
                                                  start=False, stop=True)
                    mm.then_inc(y_done, 1)
                    if c < NT - 1:
                        pe.wait_ge(xf_ready, 3 * g + c + 1)
                        if c >= 1:
                            pe.wait_ge(s_ready, 3 * g + c)
                        nc.tensor.matmul(BANK[7][:, :], BTOK, XF.rearrange("p a b -> p (a b)"),
                                         start=True, stop=True).then_inc(st_done, 1)
            pe.wait_ge(gs_read, UNITS - 1)
            unit_sums(UNITS - 1)
            rest_pe(pe)

        @block.scalar
        def _(act):
            ahead = Count(act, exp_set)
            act.dma_start(PAR[:, :], A["param"]).then_inc(params_in, 16)
            act.dma_start(BUCK[0:33, :], A["bucket"]).then_inc(aux_in, 16)
            act.dma_start(REL[0:33, :], A["rel"]).then_inc(aux_in, 16)
            for k in range(KD):
                if k % 2 == 0:
                    act.wait_ge(x_in[k // 2], 16)
                if k >= 2:
                    act.wait_ge(sq_used, k - 1)
                nc.scalar.activation(SQ[:, k % 2, :], X[:, k, :], ACT.Square).then_inc(sq_ready, 1)
            act.dma_start(CST[:, :], A["const"]).then_inc(loaded, 16)
            act.wait_ge(ones_set, 3)
            act.wait_ge(params_in, 16)
            act.wait_ge(loaded, 16)
            norm_scale_act(act, 0)
            dt = Count(act, dt_act)
            dt.step(nc.scalar.activation(ALOG[0:32, :], par("a_log", parts=32), ACT.Exp))
            act.wait_ge(dt_row, 1)
            dt.step(nc.scalar.activation(DTB[0:32, :], DTA[0:32, :], ACT.Abs))
            dt.step(nc.scalar.activation(DTB[0:32, :], DTB[0:32, :], ACT.Exp, scale=-1.0))
            act.wait_ge(dt_row, 2)
            dt.step(nc.scalar.activation(STD[0:32, :], DTC[0:32, :], ACT.Ln))

            def rows(g, j):
                n = GROUP_TILES * g + j
                if j < GT:
                    act.wait_ge(gemm_free, TILE0["in_w"] + n + 1)
                else:
                    act.wait_ge(conv_ready, (GT + 2) * g + j - GT + 1)
                if g >= 2 and j == 0:
                    act.wait_ge(yb_ready, NT * (g - 1))
                src, dst = (U[:, n % 2, 3:3 + T], ZS[g % 2][:, j, :]) if j < GT else \
                           (CV[:, n % 2, :], XSB[g % 2][:, j - GT, :])
                nc.scalar.activation(dst, src, ACT.Silu).then_inc(row_used, 1)

            for j in range(GROUP_TILES):
                rows(0, j)
                b = j - (GROUP_TILES - AH)
                if b >= 0:
                    act.wait_ge(brow_done, b + 1)
                    nc.scalar.activation(BROW[:, b, 0:T], BANK[2][:, :], ACT.Copy).then_inc(brow_ready, 1)
                    nc.scalar.activation(BROW[:, b, T:640], BANK[3][:, 0:P], ACT.Copy).then_inc(brow_ready, 1)
            act.wait_ge(brow_ready, 2 * AH)
            act.dma_start(DSCR.rearrange("h p m -> p h m"), BROW).then_inc(brow_out, 16)

            def square_sums(u):
                act.wait_ge(usum_done, u + 1)
                nc.scalar.activation(GSS[:, u % NT * P:(u % NT + 1) * P], BANK[4][:, 2 * P:3 * P], ACT.Copy).then_inc(gs_read, 1)

            def group_rms(g):
                act.wait_ge(gs_read, NT * (g + 1))
                nc.scalar.activation(STD[:, :], GSS, ACT.Sqrt, bias=EPSC[:, 0:1], scale=1.0 / (GT * P)).then_inc(gstd_ready, 1)

            for g in range(SSM_G):
                for c in range(NT):
                    u = NT * g + c
                    act.wait_ge(p1_done, u + 1)
                    nc.scalar.activation(BTOK, BANK[4][:, P:2 * P], ACT.Copy).then_inc(e_ready, 1)
                    for q in range(2):
                        nc.scalar.activation(ECS[:, 4 * q:4 * q + 4, :],
                                             BANK[2 + q][:, :].rearrange("p (h t) -> p h t", t=P),
                                             ACT.Exp).then_inc(e_ready, 1)
                    act.wait_ge(d_ready, u + 1)
                    nc.scalar.activation(DEC, DEC, ACT.Exp).then_inc(d_exp, 1)
                    nc.scalar.activation(FX, FX, ACT.Exp).then_inc(d_exp, 1)
                    if g + 1 < SSM_G:
                        for j in range(sum(FILL[:c]), sum(FILL[:c + 1])):
                            if j == sum(FILL[:c + 1]) - 1 and u >= 1:
                                square_sums(u - 1)
                            rows(g + 1, j)
                        exp_tables(ahead)
                    else:
                        square_sums(u - 1)
                    act.wait_ge(yb_ready, u + 1)
                    nc.scalar.activation(YSQ, YB[:, GT * g:GT * (g + 1), c * P:(c + 1) * P], ACT.Square).then_inc(gsq_ready, 1)
                    if c == 0 and g >= 1:
                        group_rms(g - 1)
                        exp_tables(ahead)
            square_sums(UNITS - 1)
            group_rms(SSM_G - 1)
            rest_act(act, ahead)

        @block.vector
        def _(dve):
            step, rs, hr, fr = (Count(dve, s) for s in (dve_step, rs_ready, h_ready, gemm_free))
            nc.vector.memset(ONES[:, :], 1.0).then_inc(ones_set, 1)
            nc.vector.memset(EPSC[:, :], EPS).then_inc(ones_set, 1)
            nc.vector.memset(U[:, :, 0:3], 0.0).then_inc(ones_set, 1)
            dve.wait_ge(ones_set, 3)
            dve.wait_ge(params_in, 16)
            for k in range(KD):
                if k % 2 == 0:
                    dve.wait_ge(x_in[k // 2], 16)
                split_scaled(hr, HH[:, k, :], HL[:, k, :], X[:, k, :], par("ssm_ln", k))
            nc.vector.memset(ACC[:, :], 0.0).then_inc(acc_ready, KD + 1)
            dve.wait_ge(loaded, 16)
            dve.wait_ge(acc_ready, KD + 1)
            norm_scale_dve(dve, 0, rs)
            r = Count(dve, dt_row)
            dve.wait_ge(gemm_done, 1)
            fr.step(nc.vector.tensor_tensor(DTA[0:32, :], BANK[0][0:32, :], RS[0:32, :], ALU.mult))
            r.step(nc.vector.tensor_scalar(DTA[0:32, :], DTA[0:32, :], par("dt_bias", parts=32), None, ALU.add))
            cv = Count(dve, conv_ready)

            def rows(g, j):
                n = GROUP_TILES * g + j
                dve.wait_ge(gemm_done, TILE0["in_w"] + n + 1)
                if n >= 2:
                    dve.wait_ge(row_used, n - 1)
                u = U[:, n % 2, :]
                fr.step(nc.vector.tensor_tensor(u[:, 3:3 + T], BANK[(TILE0["in_w"] + n) % 2][:, :], RS[:, :], ALU.mult))
                if j >= GT:
                    conv(dve, step, cv, n % 2, lambda k: par("ssm_conv", 5 * ((GT + 2) * g + j - GT) + k), 4)

            rows(0, 0)
            rows(0, 1)
            dve.wait_ge(dt_act, 3)
            r.step(nc.vector.tensor_scalar(DTC[0:32, :], DTB[0:32, :], 1.0, None, ALU.add))
            r.step(nc.vector.tensor_scalar(CSR[0:32, :], DTC[0:32, :], -1.0, None, ALU.add))
            r.step(nc.vector.tensor_tensor(DTB[0:32, :], DTB[0:32, :], CSR[0:32, :], ALU.subtract))
            r.step(nc.vector.tensor_scalar(DTA[0:32, :], DTA[0:32, :], 0.0, None, ALU.max))
            dve.wait_ge(dt_act, 4)
            r.step(nc.vector.tensor_tensor(DTB[0:32, :], DTB[0:32, :], STD[0:32, :], ALU.add))
            r.step(nc.vector.tensor_tensor(DTR[0:32, :], DTA[0:32, :], DTB[0:32, :], ALU.add))
            r.step(nc.vector.tensor_scalar(DTA[0:32, :], DTR[0:32, :], ALOG[0:32, 0:1], -1.0, ALU.mult, ALU.mult))
            r.step(nc.vector.memset(DTC[0:32, :], 1.0))
            for c in range(NT):
                tok = slice(c * P, (c + 1) * P)
                r.step(nc.vector.tensor_tensor_scan(CSR[0:32, tok], DTC[0:32, tok], DTA[0:32, tok], 0.0,
                                                    ALU.mult, ALU.add))
            for j in range(2, GROUP_TILES):
                rows(0, j)
            dve.wait_ge(dtT_done, 1)
            b6 = BANK[6][:, 0:NT * 64].rearrange("p (c w) -> p c w", w=64)
            tt = Count(dve, dt_row)
            tt.n = r.n
            tt.step(nc.vector.tensor_copy(DTT, b6[:, :, 0:32]))
            tt.step(nc.vector.tensor_copy(CSTK, b6[:, :, 32:64]))
            mce, xf, yr, yb, sr, dr, yn = (Count(dve, s) for s in (mce_ready, xf_ready, y_read, yb_ready, s_ready,
                                                                  d_ready, yn_ready))

            def group_norm(g):
                dve.wait_ge(gstd_ready, g + 1)
                rs.step(nc.vector.reciprocal(RSG[:, :], STD[:, :]))
                for k in range(GT * g, GT * (g + 1)):
                    yn.step(nc.vector.scalar_tensor_tensor(YB[:, k, :], YB[:, k, :], par("ssm_norm", k), RSG[:, :],
                                                           ALU.mult, ALU.mult))

            for g in range(SSM_G):
                xb = XSB[g % 2]
                heads = slice(SSM_HG * g, SSM_HG * (g + 1))
                for c in range(NT):
                    u = NT * g + c
                    tok = slice(c * P, (c + 1) * P)
                    xdt, x_f, dec, ecs, fx, etot = XDT, XF, DEC, ECS, FX, ETOT
                    dve.wait_ge(p1_done, u + 1)
                    step.step(nc.vector.tensor_tensor(xdt, BANK[5][:, :].rearrange("p (h d) -> p h d", d=64),
                                                      DTT[:, c, heads].unsqueeze(2).to_broadcast([P, SSM_HG, 64]), ALU.mult))
                    dve.wait_ge(e_ready, 3 * u + 1)
                    step.step(nc.vector.tensor_tensor(CBM, BANK[4][:, 0:P], const("causal_st"), ALU.mult))
                    dve.wait_ge(e_ready, 3 * u + 3)
                    for q in range(2):
                        step.step(nc.vector.tensor_copy(etot[:, 4 * q:4 * q + 4], BANK[2 + q][:, P - 1:T:P]))
                    step.step(nc.vector.tensor_tensor(fx, etot, CSTK[:, c, heads], ALU.subtract))
                    for h in range(SSM_HG):
                        ins = nc.vector.tensor_scalar(dec[:, h, :], BANK[2 + h // 4][:, (h % 4) * P:(h % 4 + 1) * P],
                                                      CSTK[:, c, SSM_HG * g + h:SSM_HG * g + h + 1], 0.0,
                                                      ALU.subtract, ALU.min)
                    dr.step(ins)
                    dve.wait_ge(d_exp, 2 * u + 2)
                    step.step(nc.vector.tensor_tensor(dec, dec, CBM.unsqueeze(1).to_broadcast([P, SSM_HG, P]), ALU.mult))
                    step.step(nc.vector.tensor_copy(etot, ecs[:, :, P - 1]))
                    mce.step(nc.vector.tensor_tensor(ecs, ecs, xb[:, GT + 1, tok].unsqueeze(1).to_broadcast([P, SSM_HG, P]),
                                                     ALU.mult))
                    if c < NT - 1:
                        xf.step(nc.vector.tensor_tensor(x_f, xdt, fx.unsqueeze(2).to_broadcast([P, SSM_HG, 64]), ALU.mult))
                    if g + 1 < SSM_G:
                        for j in range(sum(FILL[:c]), sum(FILL[:c + 1])):
                            rows(g + 1, j)
                    else:
                        for j in range(2 * c, 2 * c + 2):
                            dve.wait_ge(gemm_done, TILE0["out_a"] + j + 1)
                            fr.step(nc.vector.tensor_tensor(X[:, j, :], X[:, j, :], BANK[(TILE0["out_a"] + j) % 2][:, :], ALU.add))
                    step.step(nc.vector.tensor_tensor(TMPY, xb[:, 0:GT, tok],
                                                      par("ssm_d", GT * g, GT).unsqueeze(2).to_broadcast([P, GT, P]), ALU.mult))
                    dve.wait_ge(y_done, u + 1)
                    yr.step(nc.vector.tensor_tensor(TMPY, TMPY, BANK[6][:, :].rearrange("p (j t) -> p j t", t=P), ALU.add))
                    if u == 0:
                        dve.wait_ge(brow_out, 16)
                    yb.step(nc.vector.tensor_tensor(YB[:, GT * g:GT * (g + 1), tok], TMPY, ZS[g % 2][:, :, tok], ALU.mult))
                    if c < NT - 1:
                        dve.wait_ge(st_done, 3 * g + c + 1)
                        st3 = STATE.rearrange("p (h d) -> p h d", d=64)
                        if c == 0:
                            sr.step(nc.vector.tensor_copy(STATE, BANK[7][:, :]))
                        else:
                            step.step(nc.vector.tensor_tensor(st3, st3, etot.unsqueeze(2).to_broadcast([P, SSM_HG, 64]), ALU.mult))
                            sr.step(nc.vector.tensor_tensor(STATE, STATE, BANK[7][:, :], ALU.add))
                    if c == 0 and g >= 1:
                        group_norm(g - 1)
            group_norm(SSM_G - 1)
            rest_dve(dve, step, rs, hr, fr, cv)


def _tiles(v):
    return np.asarray(v).reshape(-1, P).T


def _blocks(w, cells=8):
    k, n = w.shape
    b = w.reshape(k // (cells * P), cells, P, n // P, P).transpose(3, 0, 2, 1, 4)
    return np.ascontiguousarray(b).reshape(-1, P, cells * P)


def _constants():
    c = np.zeros((P, CONST[None]), np.float32)

    def put(name, v):
        a, n = CONST[name]
        c[:, a:a + n] = v.reshape(P, n)

    i = np.arange(P)
    put("ident", np.eye(P))
    put("half_ones", (i[:, None] // 64 == i[None, :] // 64) * 1.0)
    put("causal_st", (i[:, None] <= i[None, :]) * 1.0)
    put("future_neg", (i[None, :] > i[:, None]) * NEG)
    turn = np.zeros((P, P))
    freq = np.zeros(P)
    inv = np.power(np.float32(500000.0), -np.arange(8, dtype=np.float32) * np.float32(2.0 / 16)).astype(np.float32)
    for half in (0, 64):
        for d in range(8):
            turn[half + d + 8, half + d] = -1.0
            turn[half + d, half + d + 8] = 1.0
            freq[half + d] = freq[half + d + 8] = inv[d]
    put("rope_turn", turn)
    put("rope_freq", freq)
    t = np.arange(T).reshape(NT, P)
    seen = (np.arange(NCMP)[None, None, :] * 16 + 31 <= t.T[:, :, None]) * 1.0
    put("cmp_seen", seen)
    put("cmp_neg", (1.0 - seen) * NEG)
    return c


def _bucket_rows():
    n = np.maximum(T - 1 - np.arange(640), 0)
    nf = np.maximum(n, 1).astype(np.float32)
    large = 16 + (np.log(nf / np.float32(16)).astype(np.float32) / np.float32(math.log(8.0)) * np.float32(16)).astype(np.int32)
    bucket = np.where(n < 16, n, np.minimum(large, 31))
    rows = np.zeros((33, 640), np.float32)
    rows[bucket, np.arange(640)] = 1.0
    rows[32] = np.where(T - 1 - np.arange(640) < 0, NEG, 0.0)
    return rows


def _arrays(d):
    d = {k: np.asarray(v) for k, v in d.items()}
    f32 = np.float32
    par = np.zeros((P, PARAM[None]), f32)

    def put(name, v):
        a, n = PARAM[name]
        par[:v.shape[0], a:a + n] = v.reshape(v.shape[0], n)

    def conv(w, b, order):
        v = np.concatenate([w, b[None]], 0)[:, order]
        return v.reshape(v.shape[0], -1, P).transpose(2, 1, 0)

    for name, v in (("ssm_ln", d["ssm_ln_g"][0]), ("kv_ln", d["kv_ln_g"]), ("attn_ln", d["attn_ln_g"][0]),
                    ("ffn_ln0", d["ffn_ln_g"][0]), ("ffn_ln1", d["ffn_ln_g"][1]), ("norm2", d["norm_g_2"][0]),
                    ("final", d["final_norm_g_2"]), ("ssm_d", np.repeat(d["ssm_d"][0], 64)),
                    ("ssm_norm", d["ssm_norm_g"][0]), ("k_norm", np.tile(d["k_norm_g"], 2)),
                    ("q_norm", np.tile(d["q_norm_g"][0], 2)), ("subln", d["subln_g"][0]),
                    ("mh_norm", d["mh_norm_g_2"][0])):
        put(name, _tiles(v))
    z0, x0, b0, c0 = 0, 2048, 4096, 4608
    groups = [np.concatenate([z0 + 512 * g + np.arange(512), x0 + 512 * g + np.arange(512),
                              b0 + 128 * g + np.arange(128), c0 + 128 * g + np.arange(128)]) for g in range(4)]
    put("ssm_conv", conv(d["ssm_conv_w"][0], d["ssm_conv_b"][0], np.concatenate([g[512:] - 2048 for g in groups])))
    ffo = (np.arange(22)[:, None, None] * P + np.arange(2)[None, :, None] * 2816 + np.arange(P)).reshape(-1)
    for i in range(2):
        put(f"ffn_conv{i}", conv(d["ffn_conv_w"][i], d["ffn_conv_b"][i], ffo))
    put("qk_conv", np.concatenate([conv(d["conv_q_w_2"][0], d["conv_q_b_2"][0], np.arange(1024)),
                                   conv(d["conv_k_w_2"][0], d["conv_k_b_2"][0], np.arange(1024))], 1))
    gate = np.zeros((P, 1), f32)
    gate[0:4, 0] = d["b_igate_2"][0]
    gate[32:36, 0] = d["b_fgate_2"][0]
    gate[64:88, 0] = d["b_nsa_gate_2"][0]
    put("gate_bias", gate)
    put("dt_bias", d["ssm_dt_bias"][0][:, None])
    put("a_log", d["ssm_a_log"][0][:, None])
    put("cmp_pos", np.tile(np.concatenate([d["cmp_pos_k_2"][0].T, d["cmp_pos_v_2"][0].T], 1), (2, 1)))
    put("lam", np.tile(d["lam_vecs"][0].reshape(1, 256), (P, 1)))

    w2 = d["w_in_2"][0]
    dt_w, gates_w = np.zeros((1024, P), f32), np.zeros((1024, P), f32)
    dt_w[:, 0:32] = d["ssm_in_w"][0][:, 5120:5152]
    gates_w[:, 0:4] = w2[:, 5120:5124]
    gates_w[:, 32:36] = w2[:, 5124:5128]
    nq, nz, ng = 5128, 5128 + 512 + 768 + 24, 5128 + 512 + 768
    gates_w[:, 64:88] = w2[:, ng:ng + 24]
    kc, vc, ks, vs, kw, vw = (5640 + 128 * i + np.arange(128) for i in range(6))
    pair = np.concatenate([np.concatenate([64 * j + np.arange(64), 64 * (j + 4) + np.arange(64)]) for j in range(4)])
    m = [np.arange(1024) + 1024 * i for i in range(5)]
    ga = nz + 512 + np.arange(1024)
    head = [np.concatenate([x[256 * h:256 * h + 256] for x in m]) for h in range(4)]
    order = np.concatenate(head + [nq + pair, kc, vc, ks, kw, vs, vw, nz + pair, ga, ga + 1024])
    kvw = d["kv_w"]
    kvq = np.concatenate([np.concatenate([kvw[:, 128 * h:128 * h + 128], kvw[:, 1024 + 128 * h:1152 + 128 * h],
                                          d["q_w"][0][:, 128 * h:128 * h + 128]], 1) for h in range(8)], 1)
    wa, wb = _blocks(d["w_branch_a_2"][0]), _blocks(d["w_branch_b_2"][0][pair], 4)
    ab = np.zeros((16, P, 8 * P), f32)
    ab[0::2], ab[1::2, :, 0:4 * P] = wa, wb
    return {
        "const": _constants(), "param": par, "bucket": _bucket_rows(),
        "rel": np.concatenate([d["rel_bias"], np.ones((1, 8), f32)], 0),
        "pos": np.broadcast_to(d["positions_2"].reshape(1, T), (P, T)),
        "xT": d["x"][0].T.reshape(KD, P, T).transpose(1, 0, 2),
        "dt_w": _blocks(dt_w), "gates_w": _blocks(gates_w),
        "in_w": _blocks(d["ssm_in_w"][0][:, np.concatenate(groups)]), "out_a": _blocks(d["ssm_out_w"][0][:1024]), "out_b": _blocks(d["ssm_out_w"][0][1024:]),
        "up0": _blocks(d["ffn_up_w"][0][:, ffo]), "down0": _blocks(d["ffn_down_w"][0], 11),
        "kvq": _blocks(kvq), "attn_out": _blocks(d["attn_out_w"][0]),
        "up1": _blocks(d["ffn_up_w"][1][:, ffo]), "down1": _blocks(d["ffn_down_w"][1], 11),
        "w_in2": _blocks(w2[:, order]), "ab": ab, "w_out2": _blocks(d["w_out_2"][0]),
        "cmp_w1": np.stack([np.tile(d[f"cmp_w1_{x}_2"][0].reshape(CMPL, 64, P).transpose(1, 0, 2), (2, 1, 1))
                            for x in "kv"], 0),
        "cmp_w2": np.concatenate([d["cmp_w2_k_2"][0], d["cmp_w2_v_2"][0]], 1),
    }


def kernel(**inputs):
    import concourse.bacc as bacc
    from concourse.bass_utils import run_bass_kernel_spmd

    nc = bacc.Bacc("TRN2", target_bir_lowering=False, num_devices=1)
    arrays = {f"{k}_dram": np.ascontiguousarray(v) for k, v in _arrays(inputs).items()}
    aps = {k[:-5]: nc.dram_tensor(k, v.shape, mybir.dt.from_np(v.dtype), kind="ExternalInput").ap()
           for k, v in arrays.items()}
    out = nc.dram_tensor("out_dram", (P, KD, T), F32, kind="ExternalOutput").ap()
    three_parts(nc, aps, out)
    r = run_bass_kernel_spmd(nc, [arrays], core_ids=[0])
    return r.results[0]["out_dram"].transpose(1, 0, 2).reshape(1, DM, T).transpose(0, 2, 1)
```
